# Optimizing a Trainium2 kernel written in Bass

```python
import math
import jax, jax.numpy as jnp
from jax import lax
import numpy as np

D_MODEL = 1024
BATCH = 1
SEQ = 256
DEPTH = 2

CTX_LEN = 256
GRID_W = 64
N_MIXERS = 2
N_HEADS = 8
HEAD_DIM = 64
V_DIM = 2 * HEAD_DIM
QK_WIDTH = N_HEADS * 2 * HEAD_DIM
V_WIDTH = N_HEADS * V_DIM
ROPE_THETA = 10000.0
ROPE_PAIRS = HEAD_DIM // 4
N_FOURIER_GROUPS = 4
FOURIER_GROUP = D_MODEL // N_FOURIER_GROUPS
D_FF = 2816
N_MOD = 9
Q_BLOCK = 128
EPS = 1e-6
N_ATTN_LAYERS = (DEPTH + N_MIXERS - 1) // N_MIXERS
N_FOURIER_LAYERS = DEPTH // N_MIXERS


def rms_norm(x, g):
    x32 = x.astype(jnp.float32)
    y = x32 * lax.rsqrt(jnp.mean(x32 * x32, axis=-1, keepdims=True) + EPS)
    return (y * g.astype(jnp.float32)).astype(x.dtype)

def modulate(h, shift, scale):
    return h * (1 + scale) + shift

def swiglu(h, w_gu, w_d):
    g, u = jnp.split(h @ w_gu, 2, axis=-1)
    return (jax.nn.silu(g) * u) @ w_d

def ada_params(cond, w_mod, b_mod):
    m = jax.nn.silu(cond) @ w_mod + b_mod
    m = m.reshape(m.shape[:-1] + (N_MOD, 1, D_MODEL))
    return [m[..., k, :, :] for k in range(N_MOD)]

def axial_rope_tables(n_tokens):
    rows = n_tokens // GRID_W
    row = jnp.repeat(jnp.arange(rows, dtype=jnp.float32), GRID_W)
    col = jnp.tile(jnp.arange(GRID_W, dtype=jnp.float32), rows)
    inv_freq = ROPE_THETA ** (-(jnp.arange(ROPE_PAIRS, dtype=jnp.float32) / ROPE_PAIRS))
    ang = jnp.concatenate([row[:, None] * inv_freq, col[:, None] * inv_freq], axis=-1)
    ang = ang.reshape(n_tokens, 2, ROPE_PAIRS)
    return jnp.cos(ang), jnp.sin(ang)

def apply_axial_rope(t, cos, sin):
    shp = t.shape
    t = t.reshape(shp[:-1] + (2, 2, ROPE_PAIRS))
    t1, t2 = t[..., 0, :], t[..., 1, :]
    cs = cos.astype(t.dtype)[:, None, None]
    sn = sin.astype(t.dtype)[:, None, None]
    out = jnp.stack([t1 * cs - t2 * sn, t2 * cs + t1 * sn], axis=-2)
    return out.reshape(shp)

def diff_attn_core(q, k, v, lam):
    s = jnp.einsum('bqhcd,bkhcd->bhcqk', q.astype(jnp.float32), k.astype(jnp.float32))
    p = jax.nn.softmax(s * (1.0 / math.sqrt(HEAD_DIM)), axis=-1)
    a = p[:, :, 0] - lam * p[:, :, 1]
    return jnp.einsum('bhqk,bkhe->bqhe', a.astype(v.dtype), v)

def split_qkv(h, w_qkv):
    b, n, _ = h.shape
    qkv = h @ w_qkv
    q = qkv[..., :QK_WIDTH].reshape(b, n, N_HEADS, 2, HEAD_DIM)
    k = qkv[..., QK_WIDTH:2 * QK_WIDTH].reshape(b, n, N_HEADS, 2, HEAD_DIM)
    v = qkv[..., 2 * QK_WIDTH:].reshape(b, n, N_HEADS, V_DIM)
    return q, k, v

def diff_head_out(o, sub_g, w_o, lambda_init):
    b, n = o.shape[:2]
    o = rms_norm(o, sub_g) * (1.0 - lambda_init)
    return o.reshape(b, n, V_WIDTH) @ w_o

def diff_attention(hx, hy, w_qkv, w_o, q_g, k_g, lq1, lk1, lq2, lk2, sub_g,
                   lambda_init, cos, sin, with_ctx_queries):
    b, n, _ = hx.shape
    lam = (jnp.exp(jnp.sum(lq1.astype(jnp.float32) * lk1.astype(jnp.float32)))
           - jnp.exp(jnp.sum(lq2.astype(jnp.float32) * lk2.astype(jnp.float32)))
           + lambda_init)
    q, k, v = split_qkv(hx, w_qkv)
    q = apply_axial_rope(rms_norm(q, q_g), cos, sin)
    k = apply_axial_rope(rms_norm(k, k_g), cos, sin)
    qy, ky, vy = split_qkv(hy, w_qkv)
    ky = rms_norm(ky, k_g)
    keys = jnp.concatenate([ky, k], axis=1)
    vals = jnp.concatenate([vy, v], axis=1)
    nb = n // Q_BLOCK
    qb = q.reshape(b, nb, Q_BLOCK, N_HEADS, 2, HEAD_DIM).swapaxes(0, 1)
    ob = lax.map(lambda qq: diff_attn_core(qq, keys, vals, lam), qb)
    o = ob.swapaxes(0, 1).reshape(b, n, N_HEADS, V_DIM)
    out_x = diff_head_out(o, sub_g, w_o, lambda_init)
    out_y = None
    if with_ctx_queries:
        qy = rms_norm(qy, q_g)
        oy = diff_attn_core(qy, ky, vy, lam)
        out_y = diff_head_out(oy, sub_g, w_o, lambda_init)
    return out_x, out_y

def fourier_mix(h, w_f):
    b, n, d = h.shape
    hg = h.astype(jnp.float32).reshape(b, n, N_FOURIER_GROUPS, FOURIER_GROUP)
    f = jnp.fft.fft2(hg, axes=(1, 3), norm="ortho").real
    return f.reshape(b, n, d).astype(h.dtype) @ w_f

def first_inputs(seed: int = 0) -> dict:
    key = jax.random.key(seed)
    ks = jax.random.split(key, 24)
    nrm = jax.random.normal
    f32 = jnp.float32
    NA, NF = N_ATTN_LAYERS, N_FOURIER_LAYERS
    return {
        "x": nrm(ks[0], (BATCH, SEQ, D_MODEL), f32),
        "c": nrm(ks[1], (BATCH, D_MODEL), f32),
        "ctx": nrm(ks[2], (BATCH, CTX_LEN, D_MODEL), f32),
        "c_ctx": nrm(ks[3], (D_MODEL,), f32),
        "norm_g": 1.0 + 0.05 * nrm(ks[4], (DEPTH, 3, D_MODEL), f32),
        "w_mod": 0.5 * nrm(ks[5], (DEPTH, D_MODEL, N_MOD * D_MODEL), f32) * D_MODEL ** -0.5,
        "b_mod": 0.01 * nrm(ks[6], (DEPTH, N_MOD * D_MODEL), f32),
        "ffn1_w_gu": nrm(ks[7], (DEPTH, D_MODEL, 2 * D_FF), f32) * D_MODEL ** -0.5,
        "ffn1_w_d": nrm(ks[8], (DEPTH, D_FF, D_MODEL), f32) * D_FF ** -0.5,
        "ffn2_w_gu": nrm(ks[9], (DEPTH, D_MODEL, 2 * D_FF), f32) * D_MODEL ** -0.5,
        "ffn2_w_d": nrm(ks[10], (DEPTH, D_FF, D_MODEL), f32) * D_FF ** -0.5,
        "attn_w_qkv": nrm(ks[11], (NA, D_MODEL, 2 * QK_WIDTH + V_WIDTH), f32) * D_MODEL ** -0.5,
        "attn_w_o": nrm(ks[12], (NA, V_WIDTH, D_MODEL), f32) * V_WIDTH ** -0.5,
        "attn_q_g": 1.0 + 0.05 * nrm(ks[13], (NA, HEAD_DIM), f32),
        "attn_k_g": 1.0 + 0.05 * nrm(ks[14], (NA, HEAD_DIM), f32),
        "attn_lam_q1": 0.1 * nrm(ks[15], (NA, HEAD_DIM), f32),
        "attn_lam_k1": 0.1 * nrm(ks[16], (NA, HEAD_DIM), f32),
        "attn_lam_q2": 0.1 * nrm(ks[17], (NA, HEAD_DIM), f32),
        "attn_lam_k2": 0.1 * nrm(ks[18], (NA, HEAD_DIM), f32),
        "attn_sub_g": 1.0 + 0.05 * nrm(ks[19], (NA, V_DIM), f32),
        "fourier_w": nrm(ks[20], (NF, D_MODEL, D_MODEL), f32) * D_MODEL ** -0.5,
    }

def first_block(x, c, ctx, c_ctx, norm_g, w_mod, b_mod, ffn1_w_gu, ffn1_w_d, ffn2_w_gu,
              ffn2_w_d, attn_w_qkv, attn_w_o, attn_q_g, attn_k_g, attn_lam_q1, attn_lam_k1,
              attn_lam_q2, attn_lam_k2, attn_sub_g, fourier_w):
    n_lat = x.shape[1]
    cos, sin = axial_rope_tables(n_lat)
    y = ctx
    for i in range(DEPTH):
        kind = i % N_MIXERS
        ctx_needed_after = any(j % N_MIXERS == 0 for j in range(i + 1, DEPTH))
        ctx_in_layer = ctx_needed_after or kind == 0
        mx = ada_params(c, w_mod[i], b_mod[i])
        x = x + 0.5 * mx[2] * swiglu(modulate(rms_norm(x, norm_g[i, 0]), mx[0], mx[1]),
                                     ffn1_w_gu[i], ffn1_w_d[i])
        if ctx_in_layer:
            my = ada_params(c_ctx, w_mod[i], b_mod[i])
            y = y + 0.5 * my[2] * swiglu(modulate(rms_norm(y, norm_g[i, 0]), my[0], my[1]),
                                         ffn1_w_gu[i], ffn1_w_d[i])
        hx = modulate(rms_norm(x, norm_g[i, 1]), mx[3], mx[4])
        if kind == 0:
            a = i // N_MIXERS
            hy = modulate(rms_norm(y, norm_g[i, 1]), my[3], my[4])
            lambda_init = 0.8 - 0.6 * math.exp(-0.3 * i)
            ox, oy = diff_attention(hx, hy, attn_w_qkv[a], attn_w_o[a], attn_q_g[a],
                                    attn_k_g[a], attn_lam_q1[a], attn_lam_k1[a],
                                    attn_lam_q2[a], attn_lam_k2[a], attn_sub_g[a],
                                    lambda_init, cos, sin, ctx_needed_after)
            x = x + mx[5] * ox
            if ctx_needed_after:
                y = y + my[5] * oy
        else:
            f = i // N_MIXERS
            x = x + mx[5] * fourier_mix(hx, fourier_w[f])
            if ctx_needed_after:
                hy = modulate(rms_norm(y, norm_g[i, 1]), my[3], my[4])
                y = y + my[5] * fourier_mix(hy, fourier_w[f])
        x = x + 0.5 * mx[8] * swiglu(modulate(rms_norm(x, norm_g[i, 2]), mx[6], mx[7]),
                                     ffn2_w_gu[i], ffn2_w_d[i])
        if ctx_needed_after:
            y = y + 0.5 * my[8] * swiglu(modulate(rms_norm(y, norm_g[i, 2]), my[6], my[7]),
                                         ffn2_w_gu[i], ffn2_w_d[i])
    return x


DEPTH_2 = 1

CHUNK = 64
SB_BLOCK = 128
SB_HEADS = 8
SB_HEAD_DIM = 64
SB_WIDTH = SB_HEADS * SB_HEAD_DIM
RET_HEADS = 8
RET_QK_DIM = 64
RET_V_DIM = 128
RET_QK_WIDTH = RET_HEADS * RET_QK_DIM
RET_V_WIDTH = RET_HEADS * RET_V_DIM
IN_COLS = 3 * SB_WIDTH + 2 * RET_QK_WIDTH + 2 * RET_V_WIDTH
N_BRANCHES = 2
ROPE_BASE = 10000.0
N_GROUPS = 4
EXPERTS_PER_GROUP = 4
N_EXPERTS = N_GROUPS * EXPERTS_PER_GROUP
TOP_K_IN_GROUP = 2
D_FF_EXPERT = 512


def rms_norm_2(x, g):
    xf = x.astype(jnp.float32)
    y = xf * lax.rsqrt(jnp.mean(xf * xf, axis=-1, keepdims=True) + EPS)
    return (y * g.astype(jnp.float32)).astype(x.dtype)

def to_heads(t, n_heads):
    b, s, _ = t.shape
    return t.reshape(b, s, n_heads, -1).transpose(0, 2, 1, 3)

def from_heads(t):
    b, h, s, d = t.shape
    return t.transpose(0, 2, 1, 3).reshape(b, s, h * d)

def rotary(x, positions):
    half = x.shape[-1] // 2
    inv_freq = ROPE_BASE ** (-jnp.arange(half, dtype=jnp.float32) / half)
    ang = positions.astype(jnp.float32)[:, None] * inv_freq[None, :]
    cos, sin = jnp.cos(ang), jnp.sin(ang)
    x1, x2 = x[..., :half], x[..., half:]
    return jnp.concatenate([x1 * cos - x2 * sin, x2 * cos + x1 * sin], axis=-1)

def stick_breaking_attention(q, k, v):
    s_len, d = q.shape[2], q.shape[3]
    scale = 1.0 / math.sqrt(d)
    outs = []
    for blk in range(s_len // SB_BLOCK):
        q0 = blk * SB_BLOCK
        k_end = q0 + SB_BLOCK
        qb = q[:, :, q0:k_end]
        kb = k[:, :, :k_end]
        vb = v[:, :, :k_end]
        z = jnp.einsum('bhqd,bhkd->bhqk', qb, kb) * scale
        t_idx = q0 + jnp.arange(SB_BLOCK)[:, None]
        s_idx = jnp.arange(k_end)[None, :]
        mask = s_idx < t_idx
        log_keep = jnp.where(mask, jax.nn.log_sigmoid(-z), 0.0)
        suffix = lax.cumsum(log_keep, axis=3, reverse=True) - log_keep
        weights = jnp.where(mask, jnp.exp(jax.nn.log_sigmoid(z) + suffix), 0.0)
        outs.append(jnp.einsum('bhqk,bhkd->bhqd', weights, vb))
    return jnp.concatenate(outs, axis=2)

def retention_chunkwise(q, k, v):
    b, h, s_len, dk = q.shape
    dv = v.shape[-1]
    nc = s_len // CHUNK
    log_gamma = jnp.log(1.0 - 2.0 ** (-5.0 - jnp.arange(h, dtype=jnp.float32)))
    idx = jnp.arange(CHUNK, dtype=jnp.float32)
    dist = jnp.abs(idx[:, None] - idx[None, :])
    d_intra = jnp.exp(log_gamma[:, None, None] * dist)
    qc = q.reshape(b, h, nc, CHUNK, dk)
    kc = k.reshape(b, h, nc, CHUNK, dk)
    vc = v.reshape(b, h, nc, CHUNK, dv)
    scores = jnp.einsum('bhncd,bhnmd->bhncm', qc, kc) * d_intra[None, :, None]
    intra = jnp.einsum('bhncm,bhnme->bhnce', scores, vc)
    k_decay = jnp.exp(log_gamma[:, None] * (CHUNK - 1 - idx)[None, :])
    kv = jnp.einsum('bhnmd,bhnme->bhnde', kc * k_decay[None, :, None, :, None], vc)
    chunk_decay = jnp.exp(log_gamma * CHUNK)[None, :, None, None]

    def step(state, kv_n):
        return state * chunk_decay + kv_n, state

    init = jnp.zeros((b, h, dk, dv), jnp.float32)
    _, prev = lax.scan(step, init, jnp.moveaxis(kv, 2, 0))
    prev = jnp.moveaxis(prev, 0, 2)
    q_decay = jnp.exp(log_gamma[:, None] * (idx + 1.0)[None, :])
    cross = jnp.einsum('bhncd,bhnde->bhnce', qc * q_decay[None, :, None, :, None], prev)
    return (intra + cross).reshape(b, h, s_len, dv)

def hierarchical_moe(xn, w_group_router, b_group_router, w_expert_router, b_expert_router,
                     w_exp_gate, w_exp_up, w_exp_down):
    b, s_len, d = xn.shape
    xt = xn.reshape(b * s_len, d)
    n_tok = xt.shape[0]
    group_logits = (xt @ w_group_router + b_group_router).astype(jnp.float32)
    group_probs = jax.nn.softmax(group_logits, axis=-1)
    p_group, g_sel = lax.top_k(group_probs, 1)
    expert_logits = (xt @ w_expert_router + b_expert_router).astype(jnp.float32)
    expert_logits = expert_logits.reshape(n_tok, N_GROUPS, EXPERTS_PER_GROUP)
    in_group = jnp.take_along_axis(expert_logits, g_sel[:, :, None], axis=1)[:, 0]
    top_vals, top_idx = lax.top_k(in_group, TOP_K_IN_GROUP)
    gate = jax.nn.softmax(top_vals, axis=-1) * p_group
    expert_id = g_sel * EXPERTS_PER_GROUP + top_idx
    combine = jnp.sum(jax.nn.one_hot(expert_id, N_EXPERTS, dtype=jnp.float32) * gate[..., None], axis=1)
    combine = combine.astype(xt.dtype)
    y = jnp.zeros_like(xt)
    for e in range(N_EXPERTS):
        hidden = jax.nn.silu(xt @ w_exp_gate[e]) * (xt @ w_exp_up[e])
        y = y + combine[:, e:e + 1] * (hidden @ w_exp_down[e])
    return y.reshape(b, s_len, d)

def second_inputs(seed: int = 0) -> dict:
    key = jax.random.key(seed)
    ks = jax.random.split(key, 20)
    f32 = jnp.float32

    def w(k, shape, fan_in):
        return jax.random.normal(k, shape, f32) * (fan_in ** -0.5)

    def gain(k, shape):
        return 1.0 + 0.02 * jax.random.normal(k, shape, f32)

    L = DEPTH_2
    return {
        "x": jax.random.normal(ks[0], (BATCH, SEQ, D_MODEL), f32),
        "norm_mix_g": gain(ks[1], (L, D_MODEL)),
        "w_in": w(ks[2], (L, D_MODEL, IN_COLS), D_MODEL),
        "w_gate": w(ks[3], (L, D_MODEL, N_BRANCHES * D_MODEL), D_MODEL),
        "b_gate": 0.02 * jax.random.normal(ks[4], (L, N_BRANCHES * D_MODEL), f32),
        "w_sb_out": w(ks[5], (L, SB_WIDTH, D_MODEL), SB_WIDTH),
        "w_ret_out": w(ks[6], (L, RET_V_WIDTH, D_MODEL), RET_V_WIDTH),
        "ret_norm_g": gain(ks[7], (L, RET_V_WIDTH)),
        "w_out": w(ks[8], (L, D_MODEL, D_MODEL), D_MODEL),
        "norm_ffn_g": gain(ks[9], (L, D_MODEL)),
        "w_group_router": w(ks[10], (L, D_MODEL, N_GROUPS), D_MODEL),
        "b_group_router": 0.01 * jax.random.normal(ks[11], (L, N_GROUPS), f32),
        "w_expert_router": w(ks[12], (L, D_MODEL, N_EXPERTS), D_MODEL),
        "b_expert_router": 0.01 * jax.random.normal(ks[13], (L, N_EXPERTS), f32),
        "w_exp_gate": w(ks[14], (L, N_EXPERTS, D_MODEL, D_FF_EXPERT), D_MODEL),
        "w_exp_up": w(ks[15], (L, N_EXPERTS, D_MODEL, D_FF_EXPERT), D_MODEL),
        "w_exp_down": w(ks[16], (L, N_EXPERTS, D_FF_EXPERT, D_MODEL), D_FF_EXPERT),
        "norm_final_g": gain(ks[17], (D_MODEL,)),
    }

def second_block(x, norm_mix_g, w_in, w_gate, b_gate, w_sb_out, w_ret_out, ret_norm_g, w_out,
              norm_ffn_g, w_group_router, b_group_router, w_expert_router, b_expert_router,
              w_exp_gate, w_exp_up, w_exp_down, norm_final_g):
    h = x
    s_len = x.shape[1]
    positions = jnp.arange(s_len, dtype=jnp.int32)
    split_sizes = [SB_WIDTH, SB_WIDTH, SB_WIDTH, RET_QK_WIDTH, RET_QK_WIDTH, RET_V_WIDTH, RET_V_WIDTH]
    split_at = [int(i) for i in np.cumsum(split_sizes)[:-1]]
    for layer in range(DEPTH_2):
        xn = rms_norm_2(h, norm_mix_g[layer])
        proj = xn @ w_in[layer]
        sb_q, sb_k, sb_v, r_q, r_k, r_v, r_g = jnp.split(proj, split_at, axis=-1)
        y_sb = stick_breaking_attention(to_heads(sb_q, SB_HEADS).astype(jnp.float32),
                                        to_heads(sb_k, SB_HEADS).astype(jnp.float32),
                                        to_heads(sb_v, SB_HEADS).astype(jnp.float32))
        y_sb = from_heads(y_sb).astype(x.dtype) @ w_sb_out[layer]
        rq = rotary(to_heads(r_q, RET_HEADS).astype(jnp.float32), positions)
        rk = rotary(to_heads(r_k, RET_HEADS).astype(jnp.float32), positions) * (RET_QK_DIM ** -0.5)
        rv = to_heads(r_v, RET_HEADS).astype(jnp.float32)
        y_ret = retention_chunkwise(rq, rk, rv)
        y_ret = y_ret * lax.rsqrt(jnp.mean(y_ret * y_ret, axis=-1, keepdims=True) + EPS)
        y_ret = from_heads(y_ret) * ret_norm_g[layer].astype(jnp.float32)
        y_ret = (jax.nn.silu(r_g.astype(jnp.float32)) * y_ret).astype(x.dtype) @ w_ret_out[layer]
        gates = jax.nn.sigmoid(xn @ w_gate[layer] + b_gate[layer])
        g_sb, g_ret = jnp.split(gates, N_BRANCHES, axis=-1)
        h = h + (g_sb * y_sb + g_ret * y_ret) @ w_out[layer]
        hn = rms_norm_2(h, norm_ffn_g[layer])
        h = h + hierarchical_moe(hn, w_group_router[layer], b_group_router[layer],
                                 w_expert_router[layer], b_expert_router[layer],
                                 w_exp_gate[layer], w_exp_up[layer], w_exp_down[layer])
    return rms_norm_2(h, norm_final_g)


def setup_inputs(seed=0):
    out = dict(first_inputs(seed))
    for name, value in second_inputs(seed + 1).items():
        if name != "x":
            out[name + "_2"] = value
    return out


def reference(
    x, c, ctx, c_ctx, norm_g, w_mod, b_mod, ffn1_w_gu, ffn1_w_d, ffn2_w_gu, ffn2_w_d,
    attn_w_qkv, attn_w_o, attn_q_g, attn_k_g, attn_lam_q1, attn_lam_k1, attn_lam_q2,
    attn_lam_k2, attn_sub_g, fourier_w, norm_mix_g_2, w_in_2, w_gate_2, b_gate_2, w_sb_out_2,
    w_ret_out_2, ret_norm_g_2, w_out_2, norm_ffn_g_2, w_group_router_2, b_group_router_2,
    w_expert_router_2, b_expert_router_2, w_exp_gate_2, w_exp_up_2, w_exp_down_2,
    norm_final_g_2,
):
    x = first_block(
        x, c, ctx, c_ctx, norm_g, w_mod, b_mod, ffn1_w_gu, ffn1_w_d, ffn2_w_gu, ffn2_w_d,
        attn_w_qkv, attn_w_o, attn_q_g, attn_k_g, attn_lam_q1, attn_lam_k1, attn_lam_q2,
        attn_lam_k2, attn_sub_g, fourier_w,
    )
    return second_block(
        x, norm_mix_g_2, w_in_2, w_gate_2, b_gate_2, w_sb_out_2, w_ret_out_2, ret_norm_g_2,
        w_out_2, norm_ffn_g_2, w_group_router_2, b_group_router_2, w_expert_router_2,
        b_expert_router_2, w_exp_gate_2, w_exp_up_2, w_exp_down_2, norm_final_g_2,
    )


_drawn_inputs = setup_inputs


def setup_inputs(seed=0):
    import zlib

    import numpy as np

    out = dict(_drawn_inputs(seed))
    spreads = {}
    factors = {'attn_q_g': 3.68,
     'attn_k_g': 4.026,
     'attn_lam_q1': 3.816,
     'attn_lam_k1': 5.071,
     'attn_lam_q2': 3.929,
     'attn_lam_k2': 8.0,
     'norm_mix_g_2': 2.679,
     'b_gate_2': 6.304,
     'ret_norm_g_2': 5.062,
     'norm_ffn_g_2': 3.184,
     'b_group_router_2': 4.149,
     'b_expert_router_2': 4.061,
     'norm_final_g_2': 2.841}
    for name, (base, spread) in spreads.items():
        noise = np.random.default_rng([zlib.crc32(name.encode()), seed]).standard_normal(out[name].shape)
        drawn = base * np.exp(spread * noise) if base else spread * noise
        out[name] = __import__('jax').numpy.asarray(drawn.astype(out[name].dtype))
    for name, factor in factors.items():
        out[name] = (out[name] * factor).astype(out[name].dtype)
    return out
```

```python
from contextlib import ExitStack

import numpy as np

import concourse.bass as bass
from concourse import mybir

F32 = mybir.dt.float32
F32R = mybir.dt.float32r
ALU = mybir.AluOpType
ACT = mybir.ActivationFunctionType
AX_X = mybir.AxisListType.X

P = 128
D = 1024
KD = D // P
SEQ = 256
CTX = 256
BOTH = SEQ + CTX
X_COLS = slice(CTX, BOTH)
D_FF = 2816
N_MOD = 9
EPS = 1e-6
U = 4
HEADS = 8
LAM_INIT = 0.2
THIRDS = (8, 8, 6)
FFN_ROUNDS = sum(2 * t // U for t in THIRDS) + len(THIRDS) * KD // U
MOD_W = 256
MOD_UNITS = N_MOD * D // MOD_W
MOD_FIRST = 2 * D // MOD_W
MOD_ROUNDS = (2 * MOD_UNITS - MOD_FIRST) // U
MOD_BOTH = 4
N_EXPERTS = 16
EXP_FF = 512
BIG = 1e30

DEC_W = SEQ + P

CONST = {}
_at = 0
for _name, _n in (("ident", P), ("ones", P), ("blk64", P), ("rot16", P), ("rot32", P), ("after", P),
                  ("keep", DEC_W), ("first", 4), ("cosA", SEQ), ("sinA", SEQ), ("cosB", SEQ), ("sinB", SEQ)):
    CONST[_name] = (_at, _n)
    _at += _n
N_CONST = _at

VEC = {}
_at = 0
for _name, _n in (("c", 8), ("c_ctx", 8), ("norm_g", 48), ("norm_mix", 8), ("norm_ffn", 8), ("norm_final", 8),
                  ("ret_norm", 8), ("b_gate", 16), ("q_g", 1), ("k_g", 1), ("sub_g", 1)):
    VEC[_name] = _at
    _at += _n
N_VEC = _at
B_MOD = N_VEC
N_COLS = N_VEC + 2 * N_MOD * KD
N_VEC_DMAS = 8 + 4 + 1 + 2


def make_constants():
    c = np.zeros((P, N_CONST), np.float32)

    def put(name, a):
        at, n = CONST[name]
        c[:a.shape[0], at:at + n] = a

    i = np.arange(P)
    put("ident", np.eye(P))
    put("ones", np.ones((P, P)))
    put("blk64", (i[:, None] // 64 == i[None, :] // 64).astype(np.float32))
    for name, half in (("rot16", 16), ("rot32", 32)):
        m = np.zeros((P, P))
        for dst in range(P):
            low = dst % (2 * half) < half
            m[dst + half if low else dst - half, dst] = -1.0 if low else 1.0
        put(name, m)
    put("after", (i[:, None] > i[None, :]).astype(np.float32))
    before = (i[:, None] < i[None, :]).astype(np.float32)
    put("keep", np.concatenate([before, np.ones((P, P)), before], 1))
    put("first", np.tile(np.array([4.0, 3.0, 2.0, 1.0]), (P, 1)))
    t = np.arange(SEQ)
    freq16 = (np.float32(10000.0) ** (-(np.arange(16, dtype=np.float32) / 16))).astype(np.float32)
    j = i % 64
    pos = np.where((j < 32)[:, None], (t // 64)[None, :], (t % 64)[None, :]).astype(np.float32)
    ang = (pos * freq16[j % 16][:, None]).astype(np.float32)
    put("cosA", np.cos(ang.astype(np.float64)))
    put("sinA", np.sin(ang.astype(np.float64)))
    freq32 = (np.float32(10000.0) ** (-(np.arange(32, dtype=np.float32)) / 32)).astype(np.float32)
    ang = (t[None, :].astype(np.float32) * freq32[i % 32][:, None]).astype(np.float32)
    put("cosB", np.cos(ang.astype(np.float64)))
    put("sinB", np.sin(ang.astype(np.float64)))
    gamma = 1.0 - 2.0 ** (-5.0 - np.arange(HEADS, dtype=np.float64))
    s, tt = np.arange(SEQ)[:, None], np.arange(SEQ)[None, :]
    dec = np.where(tt // 64 >= s // 64, 1.0, 0.0)[None] * gamma[:, None, None] ** np.abs(tt - s)[None]
    decay = np.concatenate([dec[:, :P, :], dec[:, P:, P:]], axis=2).transpose(1, 0, 2)
    a = 2 * np.pi * (np.outer(np.arange(256), np.arange(256)) % 256) / 256
    dft_d = (np.concatenate([np.cos(a), np.sin(a)], 1) / 16).reshape(2, P, 512).transpose(1, 0, 2)
    dft_n = (np.stack([np.cos(a), -np.sin(a)], 1) / 16).reshape(2, P, 512).transpose(1, 0, 2)
    sel = np.zeros((N_EXPERTS, N_EXPERTS, P))
    for e in range(N_EXPERTS):
        sel[e, e] = 1.0
    return {
        "consts": c,
        "decay": np.ascontiguousarray(decay.reshape(P, HEADS * DEC_W), np.float32),
        "dft": np.ascontiguousarray(np.concatenate([dft_d.reshape(P, 1024), dft_n.reshape(P, 1024)], 1), np.float32),
        "expert_rows": np.ascontiguousarray(sel.reshape(N_EXPERTS, N_EXPERTS * P), np.float32),
    }


def phases():
    table, r = {}, 0
    for name, rounds, nk in stream():
        table[name] = (r, rounds, nk)
        r += rounds
    return table


def stream():
    def ffn(name):
        for t, size in enumerate(THIRDS):
            yield f"{name}.up{t}", 2 * size // U, KD
            yield f"{name}.down{t}", KD // U, size
    yield from ffn("l0f1")
    yield "k", 2, KD
    yield "q", 2, KD
    yield "v", 2, KD
    yield "wo", 2, KD
    yield from ffn("l0f2")
    yield from ffn("l1f1")
    yield "fourier", 2, KD
    yield from ffn("l1f2")
    yield "sbq", 1, KD
    yield "sbk", 1, KD
    yield "sbv", 1, KD
    yield "rq", 1, KD
    yield "rk", 1, KD
    yield "rv", 2, KD
    yield "rg", 2, KD
    yield "gates", 4, KD
    yield "sbout", 2, 4
    yield "retout", 2, KD
    yield "wout", 2, KD
    yield "moe", 4 * N_EXPERTS, KD


def build(nc, t, out):
    ph = phases()
    names = [s[0] for s in stream()]

    def next_nk(name):
        i = names.index(name) + 1
        return ph[names[i]][2] if i < len(names) else 0

    with ExitStack() as ctx:
        place = [((nc.sbuf_base + 63) // 64) * 64]

        def sb(name, width, dt=F32, parts=P, at=None):
            where = place[0] if at is None else at
            if at is None:
                place[0] += 32 * -(-width // 8)
                assert place[0] <= 229344 - 32, (name, place[0])
            return nc.alloc_sbuf_tensor_at(name, [parts, width], dt, offset=where)

        def sem(name):
            return ctx.enter_context(nc.semaphore(name))

        SLOT = KD * P
        raw = sb("raw", U * SLOT)
        hi = sb("hi", U * SLOT, F32R)
        lo = sb("lo", U * SLOT, F32R)
        xs = sb("xs", KD * BOTH)
        nhi = sb("nhi", KD * BOTH, F32R)
        nlo = sb("nlo", KD * BOTH, F32R)
        cst = sb("cst", N_CONST)
        cols = sb("cols", N_COLS)
        csil = sb("csil", 16)
        modc = sb("modc", 3 * 72)
        acol = sb("acol", 3 * 24)
        gcol = sb("gcol", 3 * 24)
        zcol = sb("zcol", KD)
        epsc = sb("epsc", 1)
        sq = sb("sq", 2 * BOTH)
        rs = sb("rs", BOTH)
        rv_ = sb("rv_", BOTH)
        rstd = sb("rstd", BOTH)
        nt = sb("nt", 2 * BOTH)
        sg = sb("sg", 2 * BOTH)
        hf = sb("hf", 2 * BOTH)
        region = place[0]
        hhi = sb("hhi", KD * BOTH, F32R)
        hlo = sb("hlo", KD * BOTH, F32R)
        modw = sb("modw", 2 * KD * MOD_W)
        macc = sb("macc", U * 2 * MOD_W)
        end_ffn = place[0]
        xraw = sb("xraw", 4 * D, at=region + 4 * KD * BOTH)
        vrow = sb("vrow", 3 * P, at=region)

        class At:
            def __init__(self, start):
                self.at = start

            def __call__(self, name, width, dt=F32, parts=P):
                x = sb(name, width, dt, parts, at=self.at)
                self.at += 32 * -(-width // 8)
                assert self.at <= 229344 - 32, (name, self.at)
                return x

        A = At(region)
        QKW = SEQ + BOTH
        qk = A("qk", HEADS * QKW)
        vv = A("vv", 4 * D)
        ee = A("ee", 2 * 2 * BOTH)
        aT = A("aT", 4 * SEQ)
        lamv = A("lamv", 4 * 64)
        lamt = A("lamt", 2 * 64)
        lams = A("lams", 8)
        mx = A("mx", 4)
        rsum = A("rsum", 4)
        rinv = A("rinv", 4)
        rsum2 = A("rsum2", 4)
        gqk4 = A("gqk4", 4)
        rotg = A("rotg", 2 * P)
        tq = A("tq", QKW)
        tr = A("tr", QKW)
        gqk = A("gqk", 2)
        oT = sb("oT", HEADS * SEQ, at=A.at)
        A.at += 4 * HEADS * SEQ
        assert A.at <= 229344 - 32
        A = At(region)
        xf = A("xf", KD * SEQ)
        dft = A("dft", 2048)
        yt = A("yt", 2 * 4 * 512)
        A = At(region)
        sbq = A("sbq", 4 * SEQ)
        sbk = A("sbk", 4 * SEQ)
        sbv = A("sbv", 2 * 512)
        rq = A("rq", 4 * SEQ)
        rk = A("rk", 4 * SEQ)
        rvt = A("rvt", 2 * D)
        rg = A("rg", KD * SEQ)
        gates = A("gates", 16 * SEQ)
        wz = A("wz", 5 * 2 * DEC_W)
        decay = A("decay", 2 * DEC_W)
        yr = sb("yr", HEADS * SEQ, at=region)
        rvar = sb("rvar", HEADS * SEQ, at=region + 4 * (8 * SEQ + D))
        A = At(end_ffn - 4 * (2 * KD * MOD_W + U * 2 * MOD_W))
        xr = A("xr", KD * SEQ)
        cmb = A("cmb", N_EXPERTS * SEQ)
        sel = A("sel", N_EXPERTS * P, parts=N_EXPERTS)
        wr = A("wr", KD * 20)
        rbias = A("rbias", 20)
        lg = A("lg", 2 * 20)
        tiny = A("tiny", 2 * 64)
        cmbT = A("cmbT", SEQ, parts=N_EXPERTS)
        yt_out = sb("yt_out", 2 * D, at=region)

        ps = ctx.enter_context(nc.psum_tensor("ps", [P, 8 * 512], F32))

        def bank(b, n=512, first=0, parts=slice(0, P)):
            return ps[parts, 512 * b + first:512 * b + first + n]

        modps = bank(7).rearrange("p (b c) -> p b c", c=2)

        landed = [sem(f"landed{u}") for u in range(U)]
        hi_ready = sem("hi_ready")
        lo_ready = sem("lo_ready")
        slab_done = sem("slab_done")
        evacuated = sem("evacuated")
        sg_ready = sem("sg_ready")
        hhi_ready = sem("hhi_ready")
        hlo_ready = sem("hlo_ready")
        mod_landed = [sem(f"mod_landed{s}") for s in range(2)]
        mod_first_done = sem("mod_first_done")
        mod_chain = sem("mod_chain")
        mod_summed = sem("mod_summed")
        mod_copied = sem("mod_copied")
        sq_ready = sem("sq_ready")
        sq_used = sem("sq_used")
        var_ready = sem("var_ready")
        rstd_ready = sem("rstd_ready")
        nt_ready = sem("nt_ready")
        nhi_ready = sem("nhi_ready")
        nlo_ready = sem("nlo_ready")
        in_x = sem("in_x")
        in_vec = sem("in_vec")
        in_const = sem("in_const")
        vec_turned = sem("vec_turned")
        cols_ready = sem("cols_ready")
        csil_ready = sem("csil_ready")
        dve_link = sem("dve_link")
        act_link = sem("act_link")
        out_done = sem("out_done")
        x_rows_turned = sem("x_rows_turned")
        x_turned = sem("x_turned")
        fin_turned = sem("fin_turned")
        fin_copied = sem("fin_copied")

        def x_half(x):
            return x[:, :].rearrange("p (k n) -> p k n", k=KD)[:, :, X_COLS]

        def two(b):
            return ps[:, 512 * b:512 * b + 1024].rearrange("p (a n) -> p a n", a=2)[:, :, 0:DEC_W]

        def wk(i):
            return wz[:, i * 2 * DEC_W:(i + 1) * 2 * DEC_W]

        def wk3(i):
            return wk(i).rearrange("p (a n) -> p a n", a=2)

        TINY = {}

        def tn(h, name, n):
            if name not in TINY:
                TINY[name] = (sum(w for _, w in TINY.values()), n)
            at, n = TINY[name]
            assert at + n <= 64
            return tiny[:, 64 * h + at:64 * h + at + n]

        def fin_copy(eng, k):
            eng.wait_ge(fin_turned, k + 1)
            dst = yt_out[:, :].rearrange("p (h n) -> p h n", h=2)[:, :, k * P:(k + 1) * P]
            nc.vector.tensor_copy(dst, bank(k % 4, SEQ).rearrange("p (h n) -> p h n", h=2)).then_inc(fin_copied, 1)

        def const(name, cols_=None):
            at, n = CONST[name]
            return cst[:, at:at + (n if cols_ is None else cols_)]

        def col(name, k=0):
            at = VEC[name] + k
            return cols[:, at:at + 1]

        def chunk(x, c, width=BOTH, part=slice(0, BOTH)):
            w = (part.stop if part.stop is not None else width) - (part.start or 0)
            return x[:, bass.ds(c * width + (part.start or 0), w)]

        def tok(T):
            return slice(BOTH - T, BOTH)

        def k128(w):
            return w.rearrange("(k p) n -> p k n", p=P)

        def run(eng, rounds, body, peel_first=False):
            first = 0
            if peel_first and rounds > 1:
                body(0, False)
                first = 1
            if rounds - 1 - first >= 2:
                with eng.Fori(first, rounds - 1) as i:
                    body(i, False)
            else:
                for i in range(first, rounds - 1):
                    body(i, False)
            body(rounds - 1, True)

        NORMS = ["l0n0", "l0n1", "l0n2", "l1n0", "l1n1", "l1n2", "mix", "ffn", "final"]

        S = {}

        def stage_sem(name):
            if name not in S:
                S[name] = sem(name)
            return S[name]

        for name in ("in_lam", "in_dft", "in_dec0", "in_dec1", "in_router", "in_rbias", "in_sel",
                     "qk_sq", "qk_ss", "qk_var", "qk_rstd", "qk_done", "rotg_ready", "s_done", "max_done", "exp_done",
                     "a_done", "at_done", "at_copied", "o_done", "o_copied", "lam_sum", "lam_exp", "lam_ready",
                     "on_sq", "on_ss", "on_var", "on_rstd", "on_full", "on_hi", "on_lo",
                     "xf_ready", "y_done", "y_copied", "f_done", "f_copied", "f_hi", "f_lo",
                     "rot_ps", "rot_done", "z_done", "abs_done", "e_done", "sp_done", "lk_done", "suf_done",
                     "arg_done", "w_exp", "w_done", "sbo_done", "sbo_full", "sb_hi", "sb_lo",
                     "rs_done", "rw_done", "ro_done", "ro_sq", "ro_ss", "ro_var", "ro_rstd", "ro_full", "ro_hi", "ro_lo",
                     "gate_raw", "gate_done", "rg_done", "mix_full", "mix_hi", "mix_lo",
                     "rt_ps", "rt_max", "rt_exp", "rt_e2in", "rt_e2", "rt_comb", "rt_turned", "rt_copied",
                     "cmb_ps", "cmb_done", "cu_ready"):
            stage_sem(name)

        block = ctx.enter_context(nc.Block())

        @block.sync
        def _(sp):
            rows = [("c", t["c"]), ("c_ctx", t["c_ctx"].rearrange("(a n) -> a n", a=1)),
                    ("norm_g", t["norm_g"].rearrange("l s n -> (l s) n")), ("norm_mix", t["norm_mix_g_2"]),
                    ("norm_ffn", t["norm_ffn_g_2"]), ("norm_final", t["norm_final_g_2"].rearrange("(a n) -> a n", a=1)),
                    ("ret_norm", t["ret_norm_g_2"]), ("b_gate", t["b_gate_2"])]
            for name, src in rows:
                n = src.shape[0] * src.shape[1] // P
                sp.dma_start(vrow[VEC[name]:VEC[name] + n, 0:P], src.rearrange("a (k p) -> (a k) p", p=P)).then_inc(in_vec, 16)
            for half in range(2):
                for name, src in (("q_g", t["attn_q_g"]), ("k_g", t["attn_k_g"])):
                    sp.dma_start(vrow[VEC[name]:VEC[name] + 1, 64 * half:64 * half + 64], src).then_inc(in_vec, 16)
            sp.dma_start(vrow[VEC["sub_g"]:VEC["sub_g"] + 1, 0:P], t["attn_sub_g"]).then_inc(in_vec, 16)
            for l in range(2):
                sp.dma_start(vrow[0:72, (1 + l) * P:(2 + l) * P], t["b_mod"][l, :].rearrange("(k p) -> k p", p=P)).then_inc(in_vec, 16)
            sp.dma_start(cst[:, :], t["consts"]).then_inc(in_const, 16)

            def mod_unit(l, m, s):
                src = k128(t["w_mod"][l])[:, :, bass.ds(m * MOD_W, MOD_W)]
                dst = modw[:, s * KD * MOD_W:(s + 1) * KD * MOD_W].rearrange("p (k n) -> p k n", k=KD)
                sp.dma_start(dst, src).then_inc(mod_landed[s], 16)

            def x_rows(src, to):
                for h in range(2):
                    sp.dma_start(xraw[:, (2 * to + h) * D:(2 * to + h + 1) * D], src[0, h * P:(h + 1) * P, :]).then_inc(in_x, 16)

            mod_unit(0, 0, 0)
            mod_unit(0, 1, 1)
            x_rows(t["ctx"], 0)
            x_rows(t["x"], 1)
            for m in range(2, MOD_FIRST):
                sp.wait_ge(mod_first_done, m - 1)
                mod_unit(0, m, m % 2)

            def slab(r, u, nk, src, first=False):
                if not first:
                    sp.wait_ge(lo_ready, U * (r - 1) + u + 1)
                sp.dma_start(raw[:, u * SLOT:u * SLOT + nk * P].rearrange("p (k n) -> p k n", k=nk), src).then_inc(landed[u], 16)

            def mod_beside(r, u, lowest):
                n = U * r + u
                both = U * MOD_BOTH
                if lowest == 0 and u < 2:
                    sp.wait_ge(mod_first_done, MOD_FIRST - 1 + u)
                elif U * lowest + u < both + 2:
                    sp.wait_ge(mod_chain, 16 * n - 16)
                else:
                    sp.wait_ge(mod_chain, 8 * n + (8 * both - 8))
                l = 0 if MOD_FIRST + U * lowest < MOD_UNITS else 1
                mod_unit(l, n + (MOD_FIRST - l * MOD_UNITS), u % 2)

            def cols_of(w, c):
                return k128(w)[:, :, bass.ds(c * P, P)]

            MOD_CUTS = ((0, 1, 2, 4), (0, 2, 4), (0, 3))

            def ffn(name, w_gu, w_d, mods=False):
                at = 0
                for th, size in enumerate(THIRDS):
                    r0, rounds, _ = ph[f"{name}.up{th}"]
                    cuts = MOD_CUTS[th] if mods else (0, rounds)
                    for i0, i1 in zip(cuts, cuts[1:]):
                        def up(i):
                            for u in range(U):
                                slab(i + r0, u, KD, cols_of(w_gu, 2 * i + (at + u // 2 + (D_FF // P if u % 2 else 0))),
                                     first=r0 + i1 == 1)
                                if mods and r0 + i0 > 0:
                                    mod_beside(i + (r0 - 1), u, r0 + i0 - 1)
                        if i1 - i0 > 1:
                            with sp.Fori(i0, i1) as i:
                                up(i)
                        else:
                            up(i0)
                    r0, rounds, _ = ph[f"{name}.down{th}"]
                    for i in range(rounds):
                        for u in range(U):
                            c = U * i + u
                            slab(r0 + i, u, size, k128(w_d[at * P:(at + size) * P, :])[:, :, c * P:(c + 1) * P])
                            if mods and r0 + i - 1 < MOD_ROUNDS:
                                mod_beside(r0 + i - 1, u, r0 + i - 1)
                    at += size

            ffn("l0f1", t["ffn1_w_gu"][0], t["ffn1_w_d"][0], mods=True)

            def plain(name, w, c0, nk=KD):
                r0, rounds, _ = ph[name]
                for i in range(rounds):
                    for u in range(U):
                        c = c0 + U * i + u
                        slab(r0 + i, u, nk, k128(w)[:, :, c * P:(c + 1) * P])

            w = t["attn_w_qkv"][0]
            plain("k", w, KD)
            plain("q", w, 0)
            sp.wait_ge(evacuated, 4 * ph["k"][0])
            for i, name in enumerate(("attn_lam_q1", "attn_lam_k1", "attn_lam_q2", "attn_lam_k2")):
                sp.dma_start(lamv[:, 64 * i:64 * i + 64], t[name][0:1, :].to_broadcast([P, 64])).then_inc(S["in_lam"], 16)
            plain("v", w, 2 * KD)
            plain("wo", t["attn_w_o"][0], 0)
            ffn("l0f2", t["ffn2_w_gu"][0], t["ffn2_w_d"][0])
            ffn("l1f1", t["ffn1_w_gu"][1], t["ffn1_w_d"][1])
            plain("fourier", t["fourier_w"][0], 0)
            sp.wait_ge(evacuated, 4 * ph["fourier"][0])
            sp.dma_start(dft[:, :], t["dft"]).then_inc(S["in_dft"], 16)
            ffn("l1f2", t["ffn2_w_gu"][1], t["ffn2_w_d"][1])
            w = t["w_in_2"][0]
            for name, c0 in (("sbq", 0), ("sbk", 4), ("sbv", 8), ("rq", 12), ("rk", 16), ("rv", 20), ("rg", 28)):
                plain(name, w, c0)
            plain("gates", t["w_gate_2"][0], 0)
            plain("sbout", t["w_sb_out_2"][0], 0, 4)
            for h in range(HEADS):
                if h < 2:
                    sp.wait_ge(evacuated, 4 * ph["sbq"][0])
                else:
                    sp.wait_ge(S["rw_done"], h - 1)
                sp.dma_start(decay[:, (h % 2) * DEC_W:(h % 2 + 1) * DEC_W], t["decay"][:, h * DEC_W:(h + 1) * DEC_W]).then_inc(S[f"in_dec{h % 2}"], 16)
            plain("retout", t["w_ret_out_2"][0], 0)
            plain("wout", t["w_out_2"][0], 0)
            sp.wait_ge(S["mix_lo"], KD)
            sp.dma_start(wr[:, :].rearrange("p (k n) -> p k n", k=KD)[:, :, 0:4], k128(t["w_group_router_2"][0])).then_inc(S["in_router"], 16)
            sp.dma_start(wr[:, :].rearrange("p (k n) -> p k n", k=KD)[:, :, 4:20], k128(t["w_expert_router_2"][0])).then_inc(S["in_router"], 16)
            sp.dma_start(rbias[:, 0:4], t["b_group_router_2"][0:1, :].to_broadcast([P, 4])).then_inc(S["in_rbias"], 16)
            sp.dma_start(rbias[:, 4:20], t["b_expert_router_2"][0:1, :].to_broadcast([P, 16])).then_inc(S["in_rbias"], 16)
            sp.dma_start(sel[:, :], t["expert_rows"]).then_inc(S["in_sel"], 16)

            r0 = ph["moe"][0]
            with sp.Fori(0, N_EXPERTS) as e:
                for i in range(2):
                    for u in range(U):
                        w = t["w_exp_up_2"] if u % 2 else t["w_exp_gate_2"]
                        src = w.rearrange("l e (k p) n -> p (l e) k n", p=P)[:, bass.ds(e, 1), :, (2 * i + u // 2) * P:(2 * i + u // 2 + 1) * P]
                        slab(4 * e + (r0 + i), u, KD, src.rearrange("p a k n -> p (a k) n"))
                for i in range(2):
                    for u in range(U):
                        c = U * i + u
                        src = t["w_exp_down_2"].rearrange("l e (k p) n -> p (l e) k n", p=P)[:, bass.ds(e, 1), :, c * P:(c + 1) * P]
                        slab(4 * e + (r0 + 2 + i), u, 4, src.rearrange("p a k n -> p (a k) n"))
            sp.wait_ge(fin_copied, KD)
            for h in range(2):
                sp.dma_start(out[0, h * P:(h + 1) * P, :], yt_out[:, h * D:(h + 1) * D]).then_inc(out_done, 16)
            sp.wait_ge(out_done, 32)

        @block.scalar
        def _(act):
            link_at = [0]

            def link(ins):
                link_at[0] += 1
                ins.then_inc(act_link, 1)
                act.wait_ge(act_link, link_at[0])

            def split_hi(r, u, nk, wait_done=True):
                act.wait_ge(landed[u], 16 * r + 16)
                if wait_done:
                    act.wait_ge(slab_done, U * (r - 1) + u + 1)
                nc.scalar.activation(hi[:, u * SLOT:u * SLOT + nk * P], raw[:, u * SLOT:u * SLOT + nk * P], ACT.Copy).then_inc(hi_ready, 1)

            def plain(name):
                r0, rounds, nk = ph[name]

                def body(i, last):
                    for u in range(U):
                        n_k = next_nk(name) if last else nk
                        if n_k:
                            split_hi(i + (r0 + 1), u, n_k)
                run(act, rounds, body)

            h_at = [0]

            def hidden(r, p, T, h, j):
                act.wait_ge(slab_done, U * r + 2 * p + 2)
                nc.scalar.activation(sg[:, p * BOTH:p * BOTH + T], bank(2 * p, T), ACT.Silu).then_inc(sg_ready, 1)
                act.wait_ge(evacuated, U * r + 2 * p + 2)
                nc.scalar.activation(chunk(hhi, j, part=tok(T)), hf[:, p * BOTH:p * BOTH + T], ACT.Copy).then_inc(hhi_ready, 1)

            def ffn(name, T):
                for th, size in enumerate(THIRDS):
                    key = f"{name}.up{th}"
                    r0, rounds, nk = ph[key]

                    def up(i, last):
                        for u in range(U):
                            split_hi(i + (r0 + 1), u, next_nk(key) if last else nk)
                            if u % 2:
                                hidden(i + r0, u // 2, T, None, 2 * i + u // 2)
                    run(act, rounds, up)
                    plain(f"{name}.down{th}")

            def norm_squares(s, T, after):
                if after:
                    act.wait_ge(evacuated, after)
                for k in range(KD):
                    if s or k >= 2:
                        act.wait_ge(sq_used, KD * s + k - 1)
                    nc.scalar.activation(sq[:, (k % 2) * BOTH:(k % 2) * BOTH + T], chunk(xs, k, part=tok(T)), ACT.Square).then_inc(sq_ready, 1)

            def norm_root(s, T):
                act.wait_ge(var_ready, 2 * s + 2)
                nc.scalar.activation(rstd[:, 0:T], rv_[:, 0:T], ACT.Sqrt).then_inc(rstd_ready, 1)

            def norm_hi(s, T, shift, full=None):
                for k in range(KD):
                    act.wait_ge(nt_ready, KD * s + k + 1)
                    src = nt[:, (k % 2) * BOTH:(k % 2) * BOTH + T]
                    if full is not None:
                        nc.scalar.activation(full[:, k * SEQ:(k + 1) * SEQ], src, ACT.Identity, bias=shift(k)[0]).then_inc(S["xf_ready"], 1)
                    halves = list(zip(shift(k), (T - SEQ, 0)))
                    for b, at in halves:
                        ins = nc.scalar.activation(chunk(nhi, k, part=slice(BOTH - T + at, BOTH - T + at + SEQ)), src[:, at:at + SEQ], ACT.Identity, bias=b)
                    ins.then_inc(nhi_ready, 1)

            def norm(s, T, after, shift, full=None):
                norm_squares(s, T, after)
                norm_root(s, T)
                norm_hi(s, T, shift, full)

            def mod_shift(sets, s):
                return lambda k: [modc[:, 72 * c + 24 * s + k:72 * c + 24 * s + k + 1] for c in sets]

            act.wait_ge(cols_ready, 1)
            nc.scalar.activation(csil[:, :], cols[:, 0:16], ACT.Silu).then_inc(csil_ready, 1)
            act.wait_ge(x_turned, 8)
            norm_squares(0, BOTH, 0)
            norm_root(0, BOTH)
            for u in range(U):
                split_hi(0, u, KD, wait_done=False)
            norm_hi(0, BOTH, mod_shift((0, 1), 0))
            ffn("l0f1", BOTH)
            norm(1, BOTH, U * ph["k"][0], mod_shift((0, 1), 1))
            plain("k")
            plain("q")
            plain("v")

            act.wait_ge(S["lam_sum"], 1)
            nc.scalar.activation(lams[:, 2:4], lams[:, 0:2], ACT.Exp).then_inc(S["lam_exp"], 1)
            act.wait_ge(evacuated, U * ph["wo"][0])
            for h in range(HEADS):
                if h:
                    act.wait_ge(S["qk_ss"], h)
                nc.scalar.activation(sq[:, 0:QKW], qk[:, h * QKW:(h + 1) * QKW], ACT.Square).then_inc(S["qk_sq"], 1)
                act.wait_ge(S["qk_var"], 2 * h + 2)
                nc.scalar.activation(tq[:, :], tr[:, :], ACT.Sqrt).then_inc(S["qk_rstd"], 1)
            for h in range(HEADS):
                for ti in range(4):
                    act.wait_ge(S["max_done"], 4 * h + ti + 1)
                    if h:
                        act.wait_ge(S["at_done"], h)
                    nc.scalar.activation(ee[:, ti * BOTH:(ti + 1) * BOTH], bank(4 + ti), ACT.Exp, bias=mx[:, ti:ti + 1],
                                         scale=0.125, accum_out=rsum[:, ti:ti + 1]).then_inc(S["exp_done"], 1)
                act.wait_ge(S["at_done"], h + 1)
                if h:
                    act.wait_ge(S["o_done"], h)
                for b in range(2):
                    nc.scalar.activation(aT[:, 512 * b:512 * b + 512], bank(b), ACT.Copy).then_inc(S["at_copied"], 1)
            act.wait_ge(S["o_copied"], HEADS)
            nc.scalar.activation(qk[:, 4096:6144], oT[:, :], ACT.Square).then_inc(S["on_sq"], 1)
            act.wait_ge(S["on_var"], 2)
            nc.scalar.activation(qk[:, 0:2048], qk[:, 2048:4096], ACT.Sqrt).then_inc(S["on_rstd"], 1)
            act.wait_ge(S["on_full"], 1)
            nc.scalar.activation(x_half(nhi), oT[:, :].rearrange("p (k n) -> p k n", k=KD), ACT.Copy).then_inc(S["on_hi"], 1)
            plain("wo")
            norm(2, SEQ, U * ph["l0f2.up0"][0], mod_shift((0,), 2))
            ffn("l0f2", SEQ)
            norm(3, SEQ, U * ph["l1f1.up0"][0], mod_shift((2,), 0))
            ffn("l1f1", SEQ)

            norm(4, SEQ, U * ph["fourier"][0], mod_shift((2,), 1), full=xf)
            for i in range(8):
                act.wait_ge(S["y_done"], i + 1)
                nc.scalar.activation(yt[:, 512 * i:512 * i + 512], bank(i % 4), ACT.Copy).then_inc(S["y_copied"], 1)
            for c in range(KD):
                act.wait_ge(S["f_done"], c + 1)
                nc.scalar.activation(chunk(nhi, c, part=X_COLS), bank(4 + c % 4, SEQ), ACT.Copy).then_inc(S["f_hi"], 1)
            plain("fourier")
            norm(5, SEQ, U * ph["l1f2.up0"][0], mod_shift((2,), 2))
            ffn("l1f2", SEQ)

            norm(6, SEQ, U * ph["sbq"][0], lambda k: [zcol[:, 0:1]])
            for name in ("sbq", "sbk", "sbv", "rq", "rk", "rv", "rg", "gates"):
                plain(name)
            act.wait_ge(evacuated, U * ph["sbout"][0])
            nc.scalar.activation(rg[:, :], rg[:, :], ACT.Silu).then_inc(S["rg_done"], 1)
            nc.scalar.activation(gates[:, :], gates[:, :], ACT.Sigmoid).then_inc(S["gate_done"], 1)
            for c in range(4):
                z = two(2 * (c % 2))
                if c:
                    act.wait_ge(S["w_done"], c)
                act.wait_ge(S["z_done"], c + 1)
                link(nc.scalar.activation(wk3(0), z, ACT.Abs, scale=0.125))
                link(nc.scalar.activation(wk(1), wk(0), ACT.Exp, scale=-1.0))
                nc.scalar.activation(wk(0), wk(1), ACT.Ln, bias=const("ones", 1)).then_inc(S["sp_done"], 1)
                act.wait_ge(S["arg_done"], c + 1)
                nc.scalar.activation(wk(0), wk(1), ACT.Exp).then_inc(S["w_exp"], 1)
                act.wait_ge(S["sbo_done"], c + 1)
                nc.scalar.activation(chunk(nhi, c, part=slice(0, SEQ)), bank(2 * (c % 2), SEQ), ACT.Copy).then_inc(S["sb_hi"], 1)
            act.wait_ge(S["ro_done"], HEADS)
            act.wait_ge(S["ro_full"], HEADS)
            nc.scalar.activation(rvt[:, :], yr[:, :], ACT.Square).then_inc(S["ro_sq"], 1)
            act.wait_ge(S["ro_var"], 2)
            nc.scalar.activation(rvar[:, :], rvt[:, :], ACT.Sqrt).then_inc(S["ro_rstd"], 1)
            for h in range(HEADS):
                act.wait_ge(S["mix_full"], h + 1)
                nc.scalar.activation(chunk(nhi, h, part=X_COLS), yr[:, h * SEQ:(h + 1) * SEQ], ACT.Copy).then_inc(S["ro_hi"], 1)
            plain("sbout")
            plain("retout")
            for c in range(KD):
                act.wait_ge(S["gate_raw"], c + 1)
                nc.scalar.activation(chunk(nhi, c, part=X_COLS), gates[:, c * SEQ:(c + 1) * SEQ], ACT.Copy).then_inc(S["mix_hi"], 1)
            plain("wout")

            norm(7, SEQ, U * ph["moe"][0], lambda k: [zcol[:, 0:1]], full=xr)
            for h in range(2):
                act.wait_ge(S["rt_max"], h + 1)
                nc.scalar.activation(tn(h, "e", 4), lg[:, 20 * h:20 * h + 4], ACT.Exp, bias=tn(h, "negm", 1), accum_out=tn(h, "sum", 1)).then_inc(S["rt_exp"], 1)
                act.wait_ge(S["rt_e2in"], h + 1)
                nc.scalar.activation(tn(h, "e2", 1), tn(h, "d", 1), ACT.Exp).then_inc(S["rt_e2"], 1)
            for b in range(N_EXPERTS // 2):
                act.wait_ge(S["cmb_ps"], 2 * b + 2)
                nc.scalar.activation(cmb[:, 512 * b:512 * b + 512], bank(4 + b % 4), ACT.Copy).then_inc(S["cmb_done"], 1)

            r0 = ph["moe"][0]

            def expert(e, last):
                for i in range(2):
                    for u in range(U):
                        split_hi(4 * e + (r0 + i + 1), u, KD if i == 0 else 4)
                        if u % 2:
                            hidden(4 * e + (r0 + i), u // 2, SEQ, None, 2 * i + u // 2)
                for i in range(2):
                    for u in range(U):
                        if i == 0 or not last:
                            split_hi(4 * e + (r0 + 2 + i + 1), u, 4 if i == 0 else KD)
            run(act, N_EXPERTS, expert)

            norm_squares(8, SEQ, U * (ph["moe"][0] + ph["moe"][1]))
            norm_root(8, SEQ)

        @block.vector
        def _(dve):
            link_at = [0]

            def link(ins):
                link_at[0] += 1
                ins.then_inc(dve_link, 1)
                dve.wait_ge(dve_link, link_at[0])

            v = nc.vector

            def split_lo(r, u, nk):
                dve.wait_ge(hi_ready, U * r + u + 1)
                s = slice(u * SLOT, u * SLOT + nk * P)
                v.tensor_tensor(lo[:, s], raw[:, s], hi[:, s].bitcast(F32), ALU.subtract).then_inc(lo_ready, 1)

            def plain(name, evac, rounds_mod=None):
                r0, rounds, nk = ph[name]

                def body(i, last):
                    for u in range(U):
                        if rounds_mod is not None and not (isinstance(i, int) and r0 + i >= MOD_ROUNDS):
                            mod_beside(i + r0, u, rounds_mod)
                        dve.wait_ge(slab_done, U * i + (U * r0 + u + 1))
                        n_k = next_nk(name) if last else nk
                        if n_k:
                            split_lo(i + (r0 + 1), u, n_k)
                        evac(u, U * i + u)
                run(dve, rounds, body)

            def mod_beside(r, u, lowest):
                n = U * r + u
                dve.wait_ge(mod_landed[u % 2], 8 * (n + MOD_FIRST - u % 2) + 16)
                if lowest:
                    dve.wait_ge(mod_summed, n - 3)
                w = modw[:, (u % 2) * KD * MOD_W:(u % 2 + 1) * KD * MOD_W]
                both = lowest < MOD_BOTH
                conds = 2 if both else 1
                base = 16 * n if both else 8 * n + 8 * U * MOD_BOTH
                for k in range(KD):
                    for c in range(conds):
                        acc = macc[:, (2 * u + c) * MOD_W:(2 * u + c + 1) * MOD_W]
                        wk_ = w[:, k * MOD_W:(k + 1) * MOD_W]
                        s = csil[:, KD * c + k:KD * c + k + 1]
                        if k == 0:
                            ins = v.tensor_scalar(acc, wk_, s, None, ALU.mult)
                        else:
                            dve.wait_ge(mod_chain, base + (conds * (k - 1) + c + 1))
                            ins = v.scalar_tensor_tensor(out=acc, in0=wk_, scalar=s, in1=acc, op0=ALU.mult, op1=ALU.add)
                        ins.then_inc(mod_chain, 1)

            def hidden(r, p, T, h, j, weigh=None):
                f = hf[:, p * BOTH:p * BOTH + T]
                up = bank(2 * p + 1, T)
                if weigh is not None:
                    dve.wait_ge(slab_done, U * r + 2 * p + 2)
                    dve.wait_ge(hlo_ready, h - 1)
                    v.tensor_tensor(f, up, weigh, ALU.mult).then_inc(S["cu_ready"], 1)
                    up = f
                    dve.wait_ge(S["cu_ready"], h + 1 - moe_h0)
                dve.wait_ge(sg_ready, h + 1)
                if not (isinstance(h, int) and h < 2):
                    dve.wait_ge(hlo_ready, h - 1)
                v.tensor_tensor(f, sg[:, p * BOTH:p * BOTH + T], up, ALU.mult).then_inc(evacuated, 2)
                dve.wait_ge(hhi_ready, h + 1)
                v.tensor_tensor(chunk(hlo, j, part=tok(T)), f, chunk(hhi, j, part=tok(T)).bitcast(F32), ALU.subtract).then_inc(hlo_ready, 1)

            h_at = [0]
            moe_h0 = 4 * sum(THIRDS)

            def ffn(name, T, gate, mods=None):
                for th, size in enumerate(THIRDS):
                    key = f"{name}.up{th}"
                    r0, rounds, nk = ph[key]

                    def up(i, last):
                        for u in range(U):
                            if mods is not None:
                                mod_beside(i + r0, u, 0 if isinstance(i, int) and r0 + i == 0 else max(r0, 1))
                            dve.wait_ge(slab_done, U * i + (U * r0 + u + 1))
                            split_lo(i + (r0 + 1), u, next_nk(key) if last else nk)
                            if u % 2:
                                hidden(i + r0, u // 2, T, 2 * i + (h_at[0] + u // 2), 2 * i + u // 2)
                    run(dve, rounds, up, peel_first=mods is not None and r0 == 0)
                    h_at[0] += size
                    if mods is not None:
                        mods(th)
                    plain(f"{name}.down{th}", add_to_x(T, gate), rounds_mod=ph[f"{name}.down{th}"][0] if mods is not None else None)

            def add_to_x(T, gate):
                def evac(u, c):
                    g = gate(c)
                    for i, (col_, at) in enumerate(zip(g, (T - SEQ, 0))):
                        x = chunk(xs, c, part=slice(BOTH - T + at, BOTH - T + at + SEQ))
                        ins = v.scalar_tensor_tensor(out=x, in0=bank(u, SEQ, at), scalar=col_, in1=x, op0=ALU.mult, op1=ALU.add)
                    ins.then_inc(evacuated, 1)
                return evac

            def gates_of(sets, s):
                return lambda c: [gcol[:, bass.ds(24 * k + 8 * s + c, 1)] for k in sets]

            def norm_var(s, T):
                dve.wait_ge(sq_used, KD * s + KD)
                v.tensor_scalar(rs[:, 0:T], bank(4, T), 1.0 / D, EPS, ALU.mult, ALU.add).then_inc(var_ready, 1)
                dve.wait_ge(var_ready, 2 * s + 1)
                v.reciprocal(rv_[:, 0:T], rs[:, 0:T]).then_inc(var_ready, 1)

            def norm_apply(s, T, gain, shift):
                dve.wait_ge(rstd_ready, s + 1)

                def lo_of(k):
                    dve.wait_ge(nhi_ready, KD * s + k + 1)
                    for b, at in zip(shift(k), (T - SEQ, 0)):
                        part = slice(BOTH - T + at, BOTH - T + at + SEQ)
                        f = nt[:, (k % 2) * BOTH + at:(k % 2) * BOTH + at + SEQ]
                        ins = v.scalar_tensor_tensor(out=chunk(nlo, k, part=part), in0=f, scalar=b,
                                                     in1=chunk(nhi, k, part=part).bitcast(F32), op0=ALU.add, op1=ALU.subtract)
                    ins.then_inc(nlo_ready, 1)

                for k in range(KD):
                    if k >= 2:
                        dve.wait_ge(nlo_ready, KD * s + k - 1)
                    for a, at in zip(gain(k), (T - SEQ, 0)):
                        ins = v.scalar_tensor_tensor(out=nt[:, (k % 2) * BOTH + at:(k % 2) * BOTH + at + SEQ],
                                                     in0=chunk(xs, k, part=slice(BOTH - T + at, BOTH - T + at + SEQ)), scalar=a,
                                                     in1=rstd[:, at:at + SEQ], op0=ALU.mult, op1=ALU.mult)
                    ins.then_inc(nt_ready, 1)
                    if k:
                        lo_of(k - 1)
                lo_of(KD - 1)

            def mod_gain(sets, s):
                return lambda k: [acol[:, 24 * c + 8 * s + k:24 * c + 8 * s + k + 1] for c in sets]

            def mod_shift(sets, s):
                return lambda k: [modc[:, 72 * c + 24 * s + k:72 * c + 24 * s + k + 1] for c in sets]

            def vec_gain(name):
                return lambda k: [col(name, k)]

            def no_shift(k):
                return [zcol[:, 0:1]]

            def take_mod(sets, l, b0, b1, last=True):
                for i, (k, cond) in enumerate(sets):
                    ins = v.tensor_tensor(modc[:, 72 * k + b0:72 * k + b1], modps[:, 72 * l + b0:72 * l + b1, cond],
                                          cols[:, B_MOD + 72 * l + b0:B_MOD + 72 * l + b1], ALU.add)
                    if i == len(sets) - 1:
                        ins.then_inc(mod_copied, 1)
                    else:
                        link(ins)

            def gain_cols(sets, l, s):
                for k, _ in sets:
                    link(v.scalar_tensor_tensor(out=acol[:, 24 * k + 8 * s:24 * k + 8 * s + 8],
                                                in0=modc[:, 72 * k + 24 * s + 8:72 * k + 24 * s + 16], scalar=1.0,
                                                in1=cols[:, VEC["norm_g"] + 24 * l + 8 * s:VEC["norm_g"] + 24 * l + 8 * s + 8],
                                                op0=ALU.add, op1=ALU.mult))

            def gate_cols(sets, s):
                for k, _ in sets:
                    link(v.tensor_scalar(gcol[:, 24 * k + 8 * s:24 * k + 8 * s + 8], modc[:, 72 * k + 24 * s + 16:72 * k + 24 * s + 24],
                                         1.0 if s == 1 else 0.5, None, ALU.mult))

            XC = ((0, 0), (1, 1))

            def after_third(th):
                if th == 0:
                    dve.wait_ge(mod_summed, U * MOD_BOTH - 1)
                    take_mod(XC, 0, 16, 40)
                    dve.wait_ge(mod_copied, 2)
                    gate_cols(XC, 0)
                    gain_cols(XC, 0, 1)
                elif th == 1:
                    dve.wait_ge(mod_summed, U * 10 - 1)
                    take_mod(((0, 0),), 0, 40, 72)
                    dve.wait_ge(mod_copied, 3)
                    gate_cols(((0, 0),), 1)
                    gain_cols(((0, 0),), 0, 2)
                    gate_cols(((0, 0),), 2)

            v.memset(zcol[:, :], 0.0).then_inc(dve_link, 1)
            link_at[0] += 1
            dve.wait_ge(vec_turned, 1)
            v.tensor_copy(cols[:, :], bank(6, N_COLS)).then_inc(cols_ready, 1)
            for i in range(8):
                dve.wait_ge(x_rows_turned, i + 1)
                half, tc = i % 2, i // 2
                dst = xs[:, :].rearrange("p (k n) -> p k n", k=KD)[:, 4 * half:4 * half + 4, tc * P:(tc + 1) * P]
                v.tensor_copy(dst, bank(i % 4).rearrange("p (k n) -> p k n", k=4)).then_inc(x_turned, 1)
            norm_var(0, BOTH)
            dve.wait_ge(mod_first_done, MOD_FIRST)
            dve.wait_ge(cols_ready, 1)
            take_mod(XC, 0, 0, 16)
            dve.wait_ge(mod_copied, 1)
            gain_cols(XC, 0, 0)
            norm_apply(0, BOTH, mod_gain((0, 1), 0), mod_shift((0, 1), 0))
            for u in range(U):
                split_lo(0, u, KD)
            ffn("l0f1", BOTH, gates_of((0, 1), 0), mods=after_third)
            dve.wait_ge(mod_summed, U * MOD_ROUNDS)
            take_mod(((2, 0),), 1, 0, 72)
            dve.wait_ge(mod_copied, 4)
            for s in range(3):
                gain_cols(((2, 0),), 1, s)
                gate_cols(((2, 0),), s)

            def norm(s, T, gain, shift):
                norm_var(s, T)
                norm_apply(s, T, gain, shift)

            norm(1, BOTH, mod_gain((0, 1), 1), mod_shift((0, 1), 1))

            def keep(dst_of, width):
                def evac(u, c):
                    v.tensor_copy(dst_of(c), bank(u, width)).then_inc(evacuated, 1)
                return evac

            plain("k", keep(lambda c: qk[:, bass.ds(c * QKW + SEQ, BOTH)], BOTH))
            plain("q", keep(lambda c: qk[:, bass.ds(c * QKW, SEQ)], SEQ))

            def keep_v(u, c):
                dst = vv[:, :].rearrange("p (t n) -> p t n", t=4)[:, :, c * P:(c + 1) * P]
                v.tensor_copy(dst, bank(u).rearrange("p (t n) -> p t n", t=4)).then_inc(evacuated, 1)

            plain("v", keep_v)

            dve.wait_ge(S["in_lam"], 64)
            lam2 = lamv[:, :].rearrange("p (a b n) -> p a b n", a=2, b=2)
            link(v.tensor_tensor(lamt[:, :].rearrange("p (a n) -> p a n", a=2), lam2[:, :, 0, :], lam2[:, :, 1, :], ALU.mult))
            v.reduce_sum(lams[:, 0:2], lamt[:, :].rearrange("p (a n) -> p a n", a=2), AX_X).then_inc(S["lam_sum"], 1)
            dve.wait_ge(S["lam_exp"], 1)
            link(v.tensor_tensor(lams[:, 4:5], lams[:, 3:4], lams[:, 2:3], ALU.subtract))
            link(v.tensor_scalar(lams[:, 5:6], lams[:, 4:5], -LAM_INIT, None, ALU.add))
            for i, name in enumerate(("q_g", "k_g")):
                v.tensor_scalar(rotg[:, i * P:(i + 1) * P], const("rot16"), col(name), None, ALU.mult).then_inc(S["rotg_ready"], 1)
            for h in range(HEADS):
                q_ = qk[:, h * QKW:h * QKW + SEQ]
                kc = qk[:, h * QKW + SEQ:h * QKW + 2 * SEQ]
                kx = qk[:, h * QKW + 2 * SEQ:(h + 1) * QKW]
                dve.wait_ge(S["qk_ss"], h + 1)
                v.tensor_scalar(tq[:, :], ps[:, 6 * 512 + SEQ:8 * 512], 1.0 / 64, EPS, ALU.mult, ALU.add).then_inc(S["qk_var"], 1)
                dve.wait_ge(S["qk_var"], 2 * h + 1)
                v.reciprocal(tr[:, :], tq[:, :]).then_inc(S["qk_var"], 1)
                sin2 = const("sinA").unsqueeze(1).to_broadcast([P, 2, SEQ])
                v.tensor_tensor(nt[:, 0:512].rearrange("p (a n) -> p a n", a=2), bank(4).rearrange("p (a n) -> p a n", a=2), sin2, ALU.mult)
                v.scalar_tensor_tensor(out=nt[:, 512:768], in0=q_, scalar=col("q_g"), in1=const("cosA"), op0=ALU.mult, op1=ALU.mult)
                link(v.scalar_tensor_tensor(out=nt[:, 768:1024], in0=kx, scalar=col("k_g"), in1=const("cosA"), op0=ALU.mult, op1=ALU.mult))
                link(v.tensor_tensor(nt[:, 0:512], nt[:, 0:512], nt[:, 512:1024], ALU.add))
                dve.wait_ge(S["qk_rstd"], h + 1)
                v.tensor_tensor(q_, nt[:, 0:256], tq[:, 0:SEQ], ALU.mult)
                v.tensor_tensor(kx, nt[:, 256:512], tq[:, 2 * SEQ:QKW], ALU.mult)
                v.scalar_tensor_tensor(out=kc, in0=kc, scalar=col("k_g"), in1=tq[:, SEQ:2 * SEQ], op0=ALU.mult, op1=ALU.mult).then_inc(S["qk_done"], 1)

            def rows_max(h):
                for ti in range(4):
                    dve.wait_ge(S["s_done"], 4 * h + ti + 1)
                    if h:
                        dve.wait_ge(S["exp_done"], 4 * h - 3 + ti)
                    link(v.reduce_max(gqk4[:, ti:ti + 1], bank(4 + ti), AX_X))
                    v.tensor_scalar(mx[:, ti:ti + 1], gqk4[:, ti:ti + 1], -0.125, None, ALU.mult).then_inc(S["max_done"], 1)

            rows_max(0)
            for h in range(HEADS):
                dve.wait_ge(S["exp_done"], 4 * h + 4)
                link(v.reciprocal(rinv[:, :], rsum[:, :]))
                link(v.tensor_scalar(rsum2[:, :], rinv[:, :], lams[:, 5:6], None, ALU.mult))
                for q in range(2):
                    e0 = ee[:, 2 * q * BOTH:(2 * q + 1) * BOTH]
                    e1 = ee[:, (2 * q + 1) * BOTH:(2 * q + 2) * BOTH]
                    link(v.tensor_scalar(e0, e0, rinv[:, 2 * q:2 * q + 1], None, ALU.mult))
                    v.scalar_tensor_tensor(out=e0, in0=e1, scalar=rsum2[:, 2 * q + 1:2 * q + 2], in1=e0, op0=ALU.mult, op1=ALU.add).then_inc(S["a_done"], 1)
                if h + 1 < HEADS:
                    rows_max(h + 1)
                dve.wait_ge(S["o_done"], h + 1)
                v.tensor_copy(oT[:, h * SEQ:(h + 1) * SEQ], bank(2 + h % 2, SEQ)).then_inc(S["o_copied"], 1)
            dve.wait_ge(S["on_ss"], 1)
            v.tensor_scalar(qk[:, 0:2048], ps[:, 4 * 512:8 * 512], 1.0 / P, EPS, ALU.mult, ALU.add).then_inc(S["on_var"], 1)
            dve.wait_ge(S["on_var"], 1)
            v.reciprocal(qk[:, 2048:4096], qk[:, 0:2048]).then_inc(S["on_var"], 1)
            link(v.tensor_scalar(gqk[:, 0:1], col("sub_g"), 1.0 - LAM_INIT, None, ALU.mult))
            dve.wait_ge(S["on_rstd"], 1)
            v.scalar_tensor_tensor(out=oT[:, :], in0=oT[:, :], scalar=gqk[:, 0:1], in1=qk[:, 0:2048], op0=ALU.mult, op1=ALU.mult).then_inc(S["on_full"], 1)
            dve.wait_ge(S["on_hi"], 1)
            v.tensor_tensor(x_half(nlo), oT[:, :].rearrange("p (k n) -> p k n", k=KD), x_half(nhi).bitcast(F32), ALU.subtract).then_inc(S["on_lo"], 1)

            plain("wo", add_to_x(SEQ, gates_of((0,), 1)))
            norm(2, SEQ, mod_gain((0,), 2), mod_shift((0,), 2))
            ffn("l0f2", SEQ, gates_of((0,), 2))
            norm(3, SEQ, mod_gain((2,), 0), mod_shift((2,), 0))
            ffn("l1f1", SEQ, gates_of((2,), 0))

            norm(4, SEQ, mod_gain((2,), 1), mod_shift((2,), 1))
            for c in range(KD):
                dve.wait_ge(S["f_hi"], c + 1)
                v.tensor_tensor(chunk(nlo, c, part=X_COLS), bank(4 + c % 4, SEQ), chunk(nhi, c, part=X_COLS).bitcast(F32), ALU.subtract).then_inc(S["f_lo"], 1)
            plain("fourier", add_to_x(SEQ, gates_of((2,), 1)))
            norm(5, SEQ, mod_gain((2,), 2), mod_shift((2,), 2))
            ffn("l1f2", SEQ, gates_of((2,), 2))

            norm(6, SEQ, vec_gain("norm_mix"), no_shift)

            def chunks_of(x):
                return keep(lambda c: x[:, bass.ds(c * SEQ, SEQ)], SEQ)

            def rows_of(x, width):
                def evac(u, c):
                    dst = x[:, :].rearrange("p (t n) -> p t n", t=2)[:, :, c * P:(c + 1) * P]
                    v.tensor_copy(dst, bank(u, SEQ).rearrange("p (t n) -> p t n", t=2)).then_inc(evacuated, 1)
                return evac

            def gate_in(u, c):
                v.tensor_scalar(gates[:, bass.ds(c * SEQ, SEQ)], bank(u, SEQ), cols[:, bass.ds(c + VEC["b_gate"], 1)], None, ALU.add).then_inc(evacuated, 1)

            plain("sbq", chunks_of(sbq))
            plain("sbk", chunks_of(sbk))
            plain("sbv", rows_of(sbv, 512))
            plain("rq", chunks_of(rq))
            plain("rk", chunks_of(rk))
            plain("rv", rows_of(rvt, D))
            plain("rg", chunks_of(rg))
            plain("gates", gate_in)

            keep2 = const("keep").unsqueeze(1).to_broadcast([P, 2, DEC_W])
            for c in range(4):
                z = two(2 * (c % 2))
                dve.wait_ge(S["sp_done"], c + 1)
                link(v.tensor_scalar(wk3(2), z, 0.125, None, ALU.mult))
                link(v.scalar_tensor_tensor(out=wk(3), in0=wk(2), scalar=0.0, in1=wk(0), op0=ALU.max, op1=ALU.add))
                v.tensor_tensor(wk3(4), wk3(3), keep2, ALU.mult).then_inc(S["lk_done"], 1)
                link(v.tensor_tensor(wk(2), wk(2), wk(3), ALU.subtract))
                dve.wait_ge(S["suf_done"], c + 1)
                v.tensor_tensor(wk3(1), wk3(2), two(4 + 2 * (c % 2)), ALU.subtract).then_inc(S["arg_done"], 1)
                dve.wait_ge(S["w_exp"], c + 1)
                v.tensor_tensor(wk3(3), wk3(0), keep2, ALU.mult).then_inc(S["lk_done"], 1)
                dve.wait_ge(S["sb_hi"], c + 1)
                v.tensor_tensor(chunk(nlo, c, part=slice(0, SEQ)), bank(2 * (c % 2), SEQ), chunk(nhi, c, part=slice(0, SEQ)).bitcast(F32), ALU.subtract).then_inc(S["w_done"], 1)

            for i in range(8):
                x = (rq if i < 4 else rk)[:, (i % 4) * SEQ:(i % 4 + 1) * SEQ]
                dve.wait_ge(S["rot_ps"], i + 1)
                if i:
                    dve.wait_ge(S["rot_done"], i)
                link(v.tensor_tensor(nt[:, 0:SEQ], bank(4 + i % 4, SEQ), const("sinB"), ALU.mult))
                link(v.tensor_tensor(nt[:, SEQ:2 * SEQ], x, const("cosB"), ALU.mult))
                v.tensor_tensor(x, nt[:, 0:SEQ], nt[:, SEQ:2 * SEQ], ALU.add).then_inc(S["rot_done"], 1)
            for h in range(HEADS):
                dve.wait_ge(S["rs_done"], h + 1)
                dve.wait_ge(S[f"in_dec{h % 2}"], 16 * (h // 2 + 1))
                if h >= 2:
                    dve.wait_ge(S["ro_done"], h - 1)
                v.scalar_tensor_tensor(out=wk(0)[:, (h % 2) * DEC_W:(h % 2 + 1) * DEC_W], in0=bank(h % 2, DEC_W), scalar=0.125,
                                       in1=decay[:, (h % 2) * DEC_W:(h % 2 + 1) * DEC_W], op0=ALU.mult, op1=ALU.mult).then_inc(S["rw_done"], 1)
                if h:
                    dve.wait_ge(S["ro_done"], h)
                    v.tensor_copy(yr[:, (h - 1) * SEQ:h * SEQ], bank(2 + (h - 1) % 2, SEQ)).then_inc(S["ro_full"], 1)
            dve.wait_ge(S["ro_done"], HEADS)
            v.tensor_copy(yr[:, 7 * SEQ:8 * SEQ], bank(3, SEQ)).then_inc(S["ro_full"], 1)
            dve.wait_ge(S["ro_ss"], 1)
            v.tensor_scalar(rvar[:, :], ps[:, 4 * 512:8 * 512], 1.0 / P, EPS, ALU.mult, ALU.add).then_inc(S["ro_var"], 1)
            dve.wait_ge(S["ro_var"], 1)
            v.reciprocal(rvt[:, :], rvar[:, :]).then_inc(S["ro_var"], 1)
            dve.wait_ge(S["ro_rstd"], 1)
            dve.wait_ge(S["rg_done"], 1)
            for h in range(HEADS):
                y = yr[:, h * SEQ:(h + 1) * SEQ]
                link(v.scalar_tensor_tensor(out=y, in0=y, scalar=col("ret_norm", h), in1=rvar[:, h * SEQ:(h + 1) * SEQ], op0=ALU.mult, op1=ALU.mult))
                v.tensor_tensor(y, y, rg[:, h * SEQ:(h + 1) * SEQ], ALU.mult).then_inc(S["mix_full"], 1)
                dve.wait_ge(S["ro_hi"], h + 1)
                v.tensor_tensor(chunk(nlo, h, part=X_COLS), y, chunk(nhi, h, part=X_COLS).bitcast(F32), ALU.subtract).then_inc(S["ro_lo"], 1)

            def gated(first):
                def evac(u, c):
                    g = gates[:, (first + c) * SEQ:(first + c + 1) * SEQ]
                    v.tensor_tensor(g, bank(u, SEQ), g, ALU.mult).then_inc(evacuated, 1)
                return evac

            dve.wait_ge(S["gate_done"], 1)
            plain("sbout", gated(0))
            plain("retout", gated(KD))
            dve.wait_ge(evacuated, U * ph["wout"][0])
            for c in range(KD):
                g = gates[:, c * SEQ:(c + 1) * SEQ]
                v.tensor_tensor(g, g, gates[:, (KD + c) * SEQ:(KD + c + 1) * SEQ], ALU.add).then_inc(S["gate_raw"], 1)
                dve.wait_ge(S["mix_hi"], c + 1)
                v.tensor_tensor(chunk(nlo, c, part=X_COLS), g, chunk(nhi, c, part=X_COLS).bitcast(F32), ALU.subtract).then_inc(S["mix_lo"], 1)
            plain("wout", add_to_x(SEQ, lambda c: [1.0]))

            norm(7, SEQ, vec_gain("norm_ffn"), no_shift)
            dve.wait_ge(S["in_rbias"], 32)
            for h in range(2):
                def best(x, out_, n):
                    link(v.reduce_max(n, x, AX_X))
                    link(v.tensor_scalar(tn(h, "eq", 4), x, n, None, ALU.is_ge))
                    link(v.tensor_tensor(tn(h, "eq", 4), tn(h, "eq", 4), const("first"), ALU.mult))
                    link(v.reduce_max(tn(h, "m", 1), tn(h, "eq", 4), AX_X))
                    link(v.tensor_scalar(out_, tn(h, "eq", 4), tn(h, "m", 1), None, ALU.is_ge))

                l = lg[:, 20 * h:20 * h + 20]
                dve.wait_ge(S["rt_ps"], h + 1)
                link(v.tensor_tensor(l, bank(h, 20), rbias[:, :], ALU.add))
                best(l[:, 0:4], tn(h, "group", 4), tn(h, "v", 1))
                v.tensor_scalar(tn(h, "negm", 1), tn(h, "v", 1), -1.0, None, ALU.mult).then_inc(S["rt_max"], 1)
                dve.wait_ge(S["rt_exp"], h + 1)
                link(v.reduce_max(tn(h, "pg", 1), tn(h, "e", 4), AX_X))
                link(v.reciprocal(tn(h, "r", 1), tn(h, "sum", 1)))
                link(v.tensor_tensor(tn(h, "pg", 1), tn(h, "pg", 1), tn(h, "r", 1), ALU.mult))
                link(v.tensor_scalar(tn(h, "in", 4), l[:, 4:8], tn(h, "group", 4)[:, 0:1], None, ALU.mult))
                for g in range(1, 4):
                    link(v.scalar_tensor_tensor(out=tn(h, "in", 4), in0=l[:, 4 + 4 * g:8 + 4 * g], scalar=tn(h, "group", 4)[:, g:g + 1],
                                                in1=tn(h, "in", 4), op0=ALU.mult, op1=ALU.add))
                best(tn(h, "in", 4), tn(h, "one", 4), tn(h, "v", 1))
                link(v.scalar_tensor_tensor(out=tn(h, "in", 4), in0=tn(h, "one", 4), scalar=-BIG, in1=tn(h, "in", 4), op0=ALU.mult, op1=ALU.add))
                best(tn(h, "in", 4), tn(h, "two", 4), tn(h, "v2", 1))
                v.tensor_tensor(tn(h, "d", 1), tn(h, "v2", 1), tn(h, "v", 1), ALU.subtract).then_inc(S["rt_e2in"], 1)
                dve.wait_ge(S["rt_e2"], h + 1)
                link(v.tensor_scalar(tn(h, "r", 1), tn(h, "e2", 1), 1.0, None, ALU.add))
                link(v.reciprocal(tn(h, "sum", 1), tn(h, "r", 1)))
                link(v.tensor_tensor(tn(h, "g1", 1), tn(h, "sum", 1), tn(h, "pg", 1), ALU.mult))
                link(v.tensor_tensor(tn(h, "g2", 1), tn(h, "g1", 1), tn(h, "e2", 1), ALU.mult))
                link(v.tensor_scalar(tn(h, "one", 4), tn(h, "one", 4), tn(h, "g1", 1), None, ALU.mult))
                link(v.scalar_tensor_tensor(out=tn(h, "one", 4), in0=tn(h, "two", 4), scalar=tn(h, "g2", 1), in1=tn(h, "one", 4), op0=ALU.mult, op1=ALU.add))
                for g in range(4):
                    ins = v.tensor_scalar(tn(h, "comb", 16)[:, 4 * g:4 * g + 4], tn(h, "one", 4), tn(h, "group", 4)[:, g:g + 1], None, ALU.mult)
                ins.then_inc(S["rt_comb"], 1)
            dve.wait_ge(S["rt_turned"], 2)
            v.tensor_copy(cmbT[:, :], bank(2, SEQ, parts=slice(0, N_EXPERTS))).then_inc(S["rt_copied"], 1)
            dve.wait_ge(S["cmb_done"], N_EXPERTS // 2)

            r0 = ph["moe"][0]
            evac = add_to_x(SEQ, lambda c: [1.0])

            def expert(e, last):
                for i in range(2):
                    for u in range(U):
                        dve.wait_ge(slab_done, 16 * e + (U * (r0 + i) + u + 1))
                        split_lo(4 * e + (r0 + i + 1), u, KD if i == 0 else 4)
                        if u % 2:
                            hidden(4 * e + (r0 + i), u // 2, SEQ, 4 * e + (moe_h0 + 2 * i + u // 2), 2 * i + u // 2,
                                   weigh=cmb[:, bass.ds(e * SEQ, SEQ)])
                for i in range(2):
                    for u in range(U):
                        dve.wait_ge(slab_done, 16 * e + (U * (r0 + 2 + i) + u + 1))
                        if i == 0 or not last:
                            split_lo(4 * e + (r0 + 2 + i + 1), u, 4 if i == 0 else KD)
                        evac(u, U * i + u)
            run(dve, N_EXPERTS, expert)

            norm_var(8, SEQ)
            dve.wait_ge(rstd_ready, 9)
            for k in range(KD):
                f = nt[:, (k % 2) * BOTH:(k % 2) * BOTH + SEQ]
                if k >= 2:
                    dve.wait_ge(fin_turned, k - 1)
                v.scalar_tensor_tensor(out=f, in0=chunk(xs, k, part=X_COLS), scalar=col("norm_final", k), in1=rstd[:, 0:SEQ],
                                       op0=ALU.mult, op1=ALU.mult).then_inc(nt_ready, 1)
                if k:
                    fin_copy(dve, k - 1)
            fin_copy(dve, KD - 1)

        @block.tensor
        def _(pe):
            def w_hi(u, k):
                return hi[:, u * SLOT + k * P:u * SLOT + (k + 1) * P]

            def w_lo(u, k):
                return lo[:, u * SLOT + k * P:u * SLOT + (k + 1) * P]

            def ready(r, u, first=False):
                pe.wait_ge(lo_ready, U * r + u + 1)
                if not first:
                    pe.wait_ge(evacuated, U * (r - 1) + u + 1)

            def slab(r, u, nk, T, xh, xl, part, first=False):
                ready(r, u, first)
                for k in range(nk):
                    h_, l_ = chunk(xh, k, part=part), chunk(xl, k, part=part)
                    pe.matmul(bank(u, T), w_hi(u, k), h_, start=(k == 0), stop=False)
                    pe.matmul(bank(u, T), w_hi(u, k), l_, start=False, stop=False)
                    ins = pe.matmul(bank(u, T), w_lo(u, k), h_, start=False, stop=(k == nk - 1))
                ins.then_inc(slab_done, 1)

            def slab_rows(r, u, T):
                ready(r, u)
                for b in range(T // P):
                    part = slice(BOTH - T + b * P, BOTH - T + (b + 1) * P)
                    for k in range(KD):
                        o = bank(u, P, b * P)
                        h_, l_ = chunk(nhi, k, part=part), chunk(nlo, k, part=part)
                        pe.matmul(o, h_, w_hi(u, k), start=(k == 0), stop=False)
                        pe.matmul(o, h_, w_lo(u, k), start=False, stop=False)
                        ins = pe.matmul(o, l_, w_hi(u, k), start=False, stop=(k == KD - 1))
                ins.then_inc(slab_done, 1)

            def rounds_of(i0, i1, body):
                if i1 - i0 > 1:
                    with pe.Fori(i0, i1) as i:
                        body(i)
                else:
                    body(i0)

            def plain(name, T=SEQ, rows=False, xh=nhi, xl=nlo, part=None):
                r0, rounds, nk = ph[name]

                def body(i):
                    for u in range(U):
                        if rows:
                            slab_rows(i + r0, u, T)
                        else:
                            slab(i + r0, u, nk, T, xh, xl, part or tok(T))
                rounds_of(0, rounds, body)

            def sum_mod(r, u, both, copied):
                n = U * r + (u - 1)
                a = (u - 1) % U
                pe.wait_ge(mod_copied, copied)
                pe.wait_ge(mod_chain, 16 * n + 16 if both else 8 * n + (8 * U * MOD_BOTH + 8))
                for c in range(2 if both else 1):
                    for b in range(2):
                        at = (2 * a + c) * MOD_W + b * P
                        ins = pe.matmul(ps[:, bass.ds(4 * n + (7 * 512 + 4 * MOD_FIRST + 2 * b + c), 1)], macc[:, at:at + P], const("ones", 1),
                                        start=True, stop=True)
                ins.then_inc(mod_summed, 1)

            h_at = [0]

            def ffn(name, T, mods=False):
                for th, size in enumerate(THIRDS):
                    r0, rounds, nk = ph[f"{name}.up{th}"]

                    def up(i, first=False):
                        for u in range(U):
                            slab(i + r0, u, nk, T, nhi, nlo, tok(T), first)
                            if mods and not (first and u == 0):
                                sum_mod(i + r0, u, r0 == 0, (1, 2, 3)[th])
                    if mods and th == 0:
                        up(0, True)
                        rounds_of(1, rounds, up)
                    else:
                        rounds_of(0, rounds, up)
                    h_at[0] += size
                    pe.wait_ge(hlo_ready, h_at[0])
                    r0, rounds, nk = ph[f"{name}.down{th}"]

                    def down(i):
                        for u in range(U):
                            slab(i + r0, u, nk, T, hhi, hlo, tok(T))
                            if mods and U * (r0 + i) + u <= U * MOD_ROUNDS:
                                sum_mod(i + r0, u, U * (r0 + i) + u <= U * MOD_BOTH, (2, 3, 3)[th])
                    if mods:
                        for i in range(rounds):
                            down(i)
                    else:
                        rounds_of(0, rounds, down)

            def norm_sum(s, T):
                for k in range(KD):
                    pe.wait_ge(sq_ready, KD * s + k + 1)
                    pe.matmul(bank(4, T), const("ones"), sq[:, (k % 2) * BOTH:(k % 2) * BOTH + T], start=(k == 0), stop=(k == KD - 1)).then_inc(sq_used, 1)

            def norm(s, T):
                norm_sum(s, T)
                pe.wait_ge(nlo_ready, KD * (s + 1))

            pe.wait_ge(in_vec, 16 * N_VEC_DMAS)
            pe.wait_ge(in_const, 16)
            pe.transpose(bank(6, N_VEC), vrow[0:N_VEC, 0:P], const("ident")[0:N_VEC, 0:N_VEC])
            for l in range(2):
                ins = pe.transpose(bank(6, 72, N_VEC + 72 * l), vrow[0:72, (1 + l) * P:(2 + l) * P], const("ident")[0:72, 0:72])
            ins.then_inc(vec_turned, 1)

            def mod_first(m):
                pe.wait_ge(mod_landed[m % 2], 16 * (m // 2 + 1))
                for b in range(2):
                    for k in range(KD):
                        at = (m % 2) * KD * MOD_W + k * MOD_W + b * P
                        ins = pe.matmul(modps[:, 2 * m + b, :], modw[:, at:at + P], csil[:, :].rearrange("p (c k) -> p k c", c=2)[:, k, :],
                                        start=(k == 0), stop=(k == KD - 1))
                ins.then_inc(mod_first_done, 1)

            pe.wait_ge(csil_ready, 1)
            mod_first(0)
            mod_first(1)
            pe.wait_ge(in_x, 64)
            for i in range(8):
                half, tc = i % 2, i // 2
                if i >= 4:
                    pe.wait_ge(x_turned, i - 3)
                for k in range(4):
                    at = tc * D + (4 * half + k) * P
                    ins = pe.transpose(bank(i % 4, P, k * P), xraw[:, at:at + P], const("ident"))
                ins.then_inc(x_rows_turned, 1)
            norm_sum(0, BOTH)
            for m in range(2, MOD_FIRST):
                mod_first(m)
            pe.wait_ge(nlo_ready, KD)
            ffn("l0f1", BOTH, mods=True)
            norm(1, BOTH)
            plain("k", BOTH)
            plain("q")
            plain("v", BOTH, rows=True)

            pe.wait_ge(S["rotg_ready"], 2)
            for h in range(HEADS):
                pe.wait_ge(S["qk_sq"], h + 1)
                if h:
                    pe.wait_ge(S["qk_done"], h)
                pe.matmul(bank(6, SEQ, SEQ), const("blk64"), sq[:, 0:SEQ], start=True, stop=True)
                pe.matmul(bank(7, BOTH), const("blk64"), sq[:, SEQ:QKW], start=True, stop=True)
                pe.matmul(bank(4, SEQ), rotg[:, 0:P], qk[:, h * QKW:h * QKW + SEQ], start=True, stop=True)
                pe.matmul(bank(4, SEQ, SEQ), rotg[:, P:2 * P], qk[:, h * QKW + 2 * SEQ:(h + 1) * QKW], start=True, stop=True).then_inc(S["qk_ss"], 1)
            pe.wait_ge(S["qk_done"], HEADS)

            def scores(h):
                for ti in range(4):
                    q, c = ti // 2, ti % 2
                    if h:
                        pe.wait_ge(S["exp_done"], 4 * (h - 1) + ti + 1)
                    s = slice(64 * c, 64 * c + 64)
                    pe.matmul(bank(4 + ti), qk[s, h * QKW + q * P:h * QKW + (q + 1) * P], qk[s, h * QKW + SEQ:(h + 1) * QKW],
                              start=True, stop=True).then_inc(S["s_done"], 1)

            scores(0)
            for h in range(HEADS):
                if h + 1 < HEADS:
                    scores(h + 1)
                if h:
                    pe.wait_ge(S["at_copied"], 2 * h)
                for q in range(2):
                    pe.wait_ge(S["a_done"], 2 * h + q + 1)
                    for kc in range(4):
                        ins = pe.transpose(bank(kc // 2, P, (kc % 2) * SEQ + q * P), ee[:, 2 * q * BOTH + kc * P:2 * q * BOTH + (kc + 1) * P], const("ident"))
                ins.then_inc(S["at_done"], 1)
                pe.wait_ge(S["at_copied"], 2 * h + 2)
                if h >= 2:
                    pe.wait_ge(S["o_copied"], h - 1)
                for kc in range(4):
                    ins = pe.matmul(bank(2 + h % 2, SEQ), vv[:, kc * D + h * P:kc * D + (h + 1) * P], aT[:, kc * SEQ:(kc + 1) * SEQ],
                                    start=(kc == 0), stop=(kc == 3))
                ins.then_inc(S["o_done"], 1)
            pe.wait_ge(S["on_sq"], 1)
            for b in range(4):
                ins = pe.matmul(bank(4 + b), const("ones"), qk[:, 4096 + 512 * b:4096 + 512 * b + 512], start=True, stop=True)
            ins.then_inc(S["on_ss"], 1)
            pe.wait_ge(S["on_lo"], 1)
            plain("wo")
            norm(2, SEQ)
            ffn("l0f2", SEQ)
            norm(3, SEQ)
            ffn("l1f1", SEQ)

            norm(4, SEQ)
            pe.wait_ge(S["in_dft"], 16)
            for tc in range(2):
                for g in range(4):
                    i = 4 * tc + g
                    if i >= 4:
                        pe.wait_ge(S["y_copied"], i - 3)
                    for k in range(2):
                        at = (2 * g + k) * SEQ + tc * P
                        ins = pe.matmul(bank(i % 4), xf[:, at:at + P], dft[:, 512 * k:512 * k + 512], start=(k == 0), stop=(k == 1))
                    ins.then_inc(S["y_done"], 1)
            pe.wait_ge(S["y_copied"], 8)
            for c in range(KD):
                if c >= 4:
                    pe.wait_ge(S["f_lo"], c - 3)
                for j in range(4):
                    tc, sine = j // 2, j % 2
                    at = (4 * tc + c // 2) * 512 + SEQ * sine + (c % 2) * P
                    ins = pe.matmul(bank(4 + c % 4, SEQ), yt[:, at:at + P], dft[:, 1024 + 512 * tc + SEQ * sine:1024 + 512 * tc + SEQ * (sine + 1)],
                                    start=(j == 0), stop=(j == 3))
                ins.then_inc(S["f_done"], 1)
            pe.wait_ge(S["f_lo"], KD)
            plain("fourier")
            norm(5, SEQ)
            ffn("l1f2", SEQ)

            norm(6, SEQ)
            plain("sbq")
            plain("sbk")
            plain("sbv", rows=True)
            plain("rq")
            plain("rk")
            plain("rv", rows=True)
            plain("rg")
            plain("gates")
            pe.wait_ge(evacuated, U * ph["sbout"][0])

            def pair_scores(o, k_, q_, j, c):
                s = slice(64 * j, 64 * j + 64)
                pe.matmul(bank(o, SEQ), k_[s, c * SEQ:c * SEQ + P], q_[s, c * SEQ:(c + 1) * SEQ], start=True, stop=True)
                return pe.matmul(bank(o, P, SEQ), k_[s, c * SEQ + P:(c + 1) * SEQ], q_[s, c * SEQ + P:(c + 1) * SEQ], start=True, stop=True)

            for c in range(4):
                b = 2 * (c % 2)
                if c >= 2:
                    pe.wait_ge(S["w_done"], c - 1)
                for j in range(2):
                    ins = pair_scores(b + j, sbk, sbq, j, c)
                ins.then_inc(S["z_done"], 1)
                pe.wait_ge(S["lk_done"], 2 * c + 1)
                for j in range(2):
                    m = wk(4)[:, j * DEC_W:(j + 1) * DEC_W]
                    pe.matmul(bank(4 + b + j, SEQ), const("after"), m[:, 0:SEQ], start=True, stop=False)
                    pe.matmul(bank(4 + b + j, P, P), const("ones"), m[:, SEQ:DEC_W], start=False, stop=True)
                    ins = pe.matmul(bank(4 + b + j, P, SEQ), const("after"), m[:, SEQ:DEC_W], start=True, stop=True)
                ins.then_inc(S["suf_done"], 1)
                pe.wait_ge(S["lk_done"], 2 * c + 2)
                for j in range(2):
                    h = 2 * c + j
                    w = wk(3)[:, j * DEC_W:(j + 1) * DEC_W]
                    o = slice(64 * j, 64 * j + 64)
                    pe.matmul(bank(b, SEQ, parts=o), sbv[:, h * 64:h * 64 + 64], w[:, 0:SEQ], start=True, stop=False)
                    ins = pe.matmul(bank(b, P, P, parts=o), sbv[:, 512 + h * 64:512 + h * 64 + 64], w[:, SEQ:DEC_W], start=False, stop=True)
                ins.then_inc(S["sbo_done"], 1)
            pe.wait_ge(S["w_done"], 4)
            for i in range(8):
                if i >= 4:
                    pe.wait_ge(S["rot_done"], i - 3)
                x = (rq if i < 4 else rk)[:, (i % 4) * SEQ:(i % 4 + 1) * SEQ]
                pe.matmul(bank(4 + i % 4, SEQ), const("rot32"), x, start=True, stop=True).then_inc(S["rot_ps"], 1)
            pe.wait_ge(S["rot_done"], 8)

            def ret_scores(h):
                if h >= 2:
                    pe.wait_ge(S["rw_done"], h - 1)
                pair_scores(h % 2, rk, rq, h % 2, h // 2).then_inc(S["rs_done"], 1)

            ret_scores(0)
            for h in range(HEADS):
                if h + 1 < HEADS:
                    ret_scores(h + 1)
                pe.wait_ge(S["rw_done"], h + 1)
                if h >= 2:
                    pe.wait_ge(S["ro_full"], h - 1)
                w = wk(0)[:, (h % 2) * DEC_W:(h % 2 + 1) * DEC_W]
                pe.matmul(bank(2 + h % 2, SEQ), rvt[:, h * P:(h + 1) * P], w[:, 0:SEQ], start=True, stop=False)
                pe.matmul(bank(2 + h % 2, P, P), rvt[:, D + h * P:D + (h + 1) * P], w[:, SEQ:DEC_W], start=False, stop=True).then_inc(S["ro_done"], 1)
            pe.wait_ge(S["ro_sq"], 1)
            for b in range(4):
                ins = pe.matmul(bank(4 + b), const("ones"), rvt[:, 512 * b:512 * b + 512], start=True, stop=True)
            ins.then_inc(S["ro_ss"], 1)
            plain("sbout", part=slice(0, SEQ))
            pe.wait_ge(S["ro_lo"], HEADS)
            plain("retout")
            pe.wait_ge(S["mix_lo"], KD)
            plain("wout")

            norm(7, SEQ)
            pe.wait_ge(S["in_router"], 32)
            for h in range(2):
                for k in range(KD):
                    ins = pe.matmul(bank(h, 20), xr[:, k * SEQ + h * P:k * SEQ + (h + 1) * P], wr[:, 20 * k:20 * k + 20], start=(k == 0), stop=(k == KD - 1))
                ins.then_inc(S["rt_ps"], 1)
            for h in range(2):
                pe.wait_ge(S["rt_comb"], h + 1)
                pe.transpose(bank(2, P, h * P, parts=slice(0, N_EXPERTS)), tn(h, "comb", 16), const("ident")).then_inc(S["rt_turned"], 1)
            pe.wait_ge(S["rt_copied"], 1)
            pe.wait_ge(S["in_sel"], 16)
            for e in range(N_EXPERTS):
                if e >= 8 and e % 2 == 0:
                    pe.wait_ge(S["cmb_done"], e // 2 - 3)
                pe.matmul(bank(4 + e // 2 % 4, SEQ, (e % 2) * SEQ), sel[:, e * P:(e + 1) * P], cmbT[:, :], start=True, stop=True).then_inc(S["cmb_ps"], 1)

            r0 = ph["moe"][0]
            with pe.Fori(0, N_EXPERTS) as e:
                for i in range(2):
                    for u in range(U):
                        slab(4 * e + (r0 + i), u, KD, SEQ, nhi, nlo, X_COLS)
                pe.wait_ge(hlo_ready, 4 * e + (4 * sum(THIRDS) + 4))
                for i in range(2):
                    for u in range(U):
                        slab(4 * e + (r0 + 2 + i), u, 4, SEQ, hhi, hlo, X_COLS)
            norm_sum(8, SEQ)
            for k in range(KD):
                pe.wait_ge(nt_ready, KD * 8 + k + 1)
                if k >= 4:
                    pe.wait_ge(fin_copied, k - 3)
                f = nt[:, (k % 2) * BOTH:(k % 2) * BOTH + SEQ]
                for h in range(2):
                    ins = pe.transpose(bank(k % 4, P, h * P), f[:, h * P:(h + 1) * P], const("ident"))
                ins.then_inc(fin_turned, 1)


_INS = ["x", "c", "ctx", "c_ctx", "norm_g", "w_mod", "b_mod", "ffn1_w_gu", "ffn1_w_d", "ffn2_w_gu", "ffn2_w_d",
        "attn_w_qkv", "attn_w_o", "attn_q_g", "attn_k_g", "attn_lam_q1", "attn_lam_k1", "attn_lam_q2", "attn_lam_k2",
        "attn_sub_g", "fourier_w", "norm_mix_g_2", "w_in_2", "w_gate_2", "b_gate_2", "w_sb_out_2", "w_ret_out_2",
        "ret_norm_g_2", "w_out_2", "norm_ffn_g_2", "w_group_router_2", "b_group_router_2", "w_expert_router_2",
        "b_expert_router_2", "w_exp_gate_2", "w_exp_up_2", "w_exp_down_2", "norm_final_g_2"]


def kernel(**inputs):
    import numpy as _np
    import concourse.bacc as _bacc
    from concourse import mybir as _mybir
    from concourse.bass_utils import run_bass_kernel_spmd as _run

    nc = _bacc.Bacc("TRN2", target_bir_lowering=False, num_devices=1)
    arrays, tensors = {}, {}
    for name in _INS:
        a = _np.ascontiguousarray(inputs[name])
        arrays[f"in_{name}"] = a
        tensors[name] = nc.dram_tensor(f"in_{name}", a.shape, _mybir.dt.from_np(a.dtype), kind="ExternalInput").ap()
    for name, a in make_constants().items():
        arrays[f"const_{name}"] = a
        tensors[name] = nc.dram_tensor(f"const_{name}", a.shape, _mybir.dt.float32, kind="ExternalInput").ap()
    out = nc.dram_tensor("out_0", (1, SEQ, D), _mybir.dt.float32, kind="ExternalOutput").ap()
    build(nc, tensors, out)
    r = _run(nc, [arrays], core_ids=[0])
    return r.results[0]["out_0"]
```

```python
from contextlib import ExitStack

import numpy as np

import concourse.bass as bass
from concourse import mybir

F32 = mybir.dt.float32
F32R = mybir.dt.float32r
ALU = mybir.AluOpType
ACT = mybir.ActivationFunctionType
AX_X = mybir.AxisListType.X

P = 128
D = 1024
KD = D // P
SEQ = 256
CTX = 256
BOTH = SEQ + CTX
X_COLS = slice(CTX, BOTH)
D_FF = 2816
N_MOD = 9
EPS = 1e-6
U = 4
HEADS = 8
LAM_INIT = 0.2
THIRDS = (8, 8, 6)
MOD_W = 256
MOD_UNITS = N_MOD * D // MOD_W
MOD_NEED = 2 * D // MOD_W
MOD_FIRST = 3 * D // MOD_W
MOD_BOTH = 2 * D // MOD_W
MOD_JOBS = 2 * MOD_UNITS - MOD_FIRST + MOD_BOTH
MOD_HELD = 2 * U
MOD_SHIFT = MOD_HELD // U
MOD_SCALED = 6
MOD_AHEAD = 5
MOD_LAG = 3
N_EXPERTS = 16
EXP_FF = 512
BIG = 1e30

DEC_W = SEQ + P

CONST = {}
_at = 0
for _name, _n in (("ident", P), ("ones", P), ("blk64", P), ("rot16", P), ("rot32", P), ("after", P),
                  ("half_sums", 2 * HEADS * HEADS), ("head_sums", HEADS * HEADS), ("keep", DEC_W), ("first", 4), ("cosA", SEQ), ("sinA", SEQ), ("cosB", SEQ), ("sinB", SEQ)):
    CONST[_name] = (_at, _n)
    _at += _n
N_CONST = _at

VEC = {}
_at = 0
for _name, _n in (("c", 8), ("c_ctx", 8), ("norm_g", 48), ("norm_mix", 8), ("norm_ffn", 8), ("norm_final", 8),
                  ("ret_norm", 8), ("b_gate", 16), ("q_g", 1), ("k_g", 1), ("sub_g", 1)):
    VEC[_name] = _at
    _at += _n
N_VEC = _at
B_MOD = N_VEC
N_COLS = N_VEC + 2 * N_MOD * KD
N_VEC_DMAS = 8 + 4 + 1 + 2


def make_constants():
    c = np.zeros((P, N_CONST), np.float32)

    def put(name, a):
        at, n = CONST[name]
        c[:a.shape[0], at:at + n] = a

    i = np.arange(P)
    put("ident", np.eye(P))
    put("ones", np.ones((P, P)))
    put("blk64", (i[:, None] // 64 == i[None, :] // 64).astype(np.float32))
    for name, half in (("rot16", 16), ("rot32", 32)):
        m = np.zeros((P, P))
        for dst in range(P):
            low = dst % (2 * half) < half
            m[dst + half if low else dst - half, dst] = -1.0 if low else 1.0
        put(name, m)
    put("after", (i[:, None] > i[None, :]).astype(np.float32))
    before = (i[:, None] < i[None, :]).astype(np.float32)
    put("keep", np.concatenate([before, np.ones((P, P)), before], 1))
    put("first", np.tile(np.array([4.0, 3.0, 2.0, 1.0]), (P, 1)))
    halves = np.zeros((P, HEADS, 2 * HEADS))
    heads = np.zeros((P, HEADS, HEADS))
    for h in range(HEADS):
        halves[i, h, 2 * h + i // 64] = 1.0
        heads[:, h, h] = 1.0
    put("half_sums", halves.reshape(P, -1))
    put("head_sums", heads.reshape(P, -1))
    t = np.arange(SEQ)
    freq16 = (np.float32(10000.0) ** (-(np.arange(16, dtype=np.float32) / 16))).astype(np.float32)
    j = i % 64
    pos = np.where((j < 32)[:, None], (t // 64)[None, :], (t % 64)[None, :]).astype(np.float32)
    ang = (pos * freq16[j % 16][:, None]).astype(np.float32)
    put("cosA", np.cos(ang.astype(np.float64)))
    put("sinA", np.sin(ang.astype(np.float64)))
    freq32 = (np.float32(10000.0) ** (-(np.arange(32, dtype=np.float32)) / 32)).astype(np.float32)
    ang = (t[None, :].astype(np.float32) * freq32[i % 32][:, None]).astype(np.float32)
    put("cosB", np.cos(ang.astype(np.float64)))
    put("sinB", np.sin(ang.astype(np.float64)))
    gamma = 1.0 - 2.0 ** (-5.0 - np.arange(HEADS, dtype=np.float64))
    s, tt = np.arange(SEQ)[:, None], np.arange(SEQ)[None, :]
    dec = np.where(tt // 64 >= s // 64, 1.0, 0.0)[None] * gamma[:, None, None] ** np.abs(tt - s)[None]
    decay = np.concatenate([dec[:, :P, :], dec[:, P:, P:]], axis=2).transpose(1, 0, 2)
    a = 2 * np.pi * (np.outer(np.arange(256), np.arange(256)) % 256) / 256
    dft_d = (np.concatenate([np.cos(a), np.sin(a)], 1) / 16).reshape(2, P, 512).transpose(1, 0, 2)
    dft_n = (np.stack([np.cos(a), -np.sin(a)], 1) / 16).reshape(2, P, 512).transpose(1, 0, 2)
    sel = np.zeros((N_EXPERTS, N_EXPERTS, P))
    for e in range(N_EXPERTS):
        sel[e, e] = 1.0
    return {
        "consts": c,
        "decay": np.ascontiguousarray(decay.reshape(P, HEADS * DEC_W), np.float32),
        "dft": np.ascontiguousarray(np.concatenate([dft_d.reshape(P, 1024), dft_n.reshape(P, 1024)], 1), np.float32),
        "half_rows": np.ascontiguousarray(halves.transpose(2, 1, 0).reshape(2 * HEADS, HEADS * P), np.float32),
        "expert_rows": np.ascontiguousarray(sel.reshape(N_EXPERTS, N_EXPERTS * P), np.float32),
    }


def phases():
    table, r = {}, 0
    for name, rounds, nk in stream():
        table[name] = (r, rounds, nk)
        r += rounds
    return table


def stream():
    def ffn(name):
        for t, size in enumerate(THIRDS):
            yield f"{name}.up{t}", 2 * size // U, KD
            yield f"{name}.down{t}", KD // U, size
    yield from ffn("l0f1")
    yield "k", 2, KD
    yield "q", 2, KD
    yield "v", 2, KD
    yield "wo", 2, KD
    yield from ffn("l0f2")
    yield from ffn("l1f1")
    yield "fourier", 2, KD
    yield from ffn("l1f2")
    yield "sbq", 1, KD
    yield "sbk", 1, KD
    yield "sbv", 1, KD
    yield "rq", 1, KD
    yield "rk", 1, KD
    yield "rv", 2, KD
    yield "rg", 2, KD
    yield "gates", 4, KD
    yield "sbout", 2, 4
    yield "retout", 2, KD
    yield "wout", 2, KD
    yield "moe", 4 * N_EXPERTS, KD


def build(nc, t, out):
    ph = phases()
    names = [s[0] for s in stream()]

    def next_nk(name):
        i = names.index(name) + 1
        return ph[names[i]][2] if i < len(names) else 0

    with ExitStack() as ctx:
        place = [((nc.sbuf_base + 63) // 64) * 64]

        def sb(name, width, dt=F32, parts=P, at=None):
            where = place[0] if at is None else at
            if at is None:
                place[0] += 32 * -(-width // 8)
                assert place[0] <= 229344 - 32, (name, place[0])
            return nc.alloc_sbuf_tensor_at(name, [parts, width], dt, offset=where)

        def sem(name):
            return ctx.enter_context(nc.semaphore(name))

        SLOT = KD * P
        raw = sb("raw", U * SLOT)
        hi_at = place[0]
        hi = sb("hi", U * SLOT, F32R)
        lo = sb("lo", U * SLOT, F32R)
        xs = sb("xs", KD * BOTH)
        nhi_at = place[0]
        nhi = sb("nhi", KD * BOTH, F32R)
        nlo = sb("nlo", KD * BOTH, F32R)
        cst = sb("cst", N_CONST)
        cols = sb("cols", N_COLS)
        csil = sb("csil", 16)
        modc = sb("modc", 3 * 72)
        acol = sb("acol", 3 * 24)
        gcol = sb("gcol", 3 * 24)
        zcol = sb("zcol", KD)
        head_rows = sb("head_rows", HEADS * P, parts=HEADS)
        epsc = sb("epsc", 1)
        rootc = sb("rootc", 1)
        sq = sb("sq", 2 * BOTH)
        sqsum = sb("sqsum", BOTH)
        rs = sb("rs", BOTH)
        rv_ = sb("rv_", BOTH)
        rstd = sb("rstd", BOTH)
        nt = sb("nt", 2 * BOTH)
        sg = sb("sg", 2 * BOTH)
        hf = sb("hf", 2 * BOTH)
        region = place[0]
        hhi = sb("hhi", KD * BOTH, F32R)
        hlo = sb("hlo", KD * BOTH, F32R)
        modw_at = place[0]
        modw = sb("modw", U * KD * MOD_W)
        macc = sb("macc", U * MOD_W)
        mrow = sb("mrow", 2 * MOD_W, parts=2)
        end_ffn = place[0]
        xraw = sb("xraw", 4 * D, at=region + 4 * KD * BOTH)
        MOD_BYTES = 4 * KD * MOD_W
        early_at = [hi_at + MOD_BYTES * m for m in range(4)] + [nhi_at + MOD_BYTES * m for m in range(4)]
        early_at += [modw_at + MOD_BYTES, modw_at + 3 * MOD_BYTES, region + 4 * KD * BOTH, region + 4 * KD * BOTH + MOD_BYTES]
        mod_early = [sb(f"mod_early{m}", KD * MOD_W, at=early_at[m]) for m in range(MOD_FIRST)]
        vrow = sb("vrow", 3 * P, at=region)

        class At:
            def __init__(self, start):
                self.at = start

            def __call__(self, name, width, dt=F32, parts=P):
                x = sb(name, width, dt, parts, at=self.at)
                self.at += 32 * -(-width // 8)
                assert self.at <= 229344 - 32, (name, self.at)
                return x

        A = At(region)
        QKW = SEQ + BOTH
        qk = A("qk", HEADS * QKW)
        vv = A("vv", 4 * D)
        ee = A("ee", 2 * 2 * BOTH)
        half_rows = sb("half_rows", HEADS * P, parts=2 * HEADS, at=A.at)
        aT = A("aT", 4 * SEQ)
        lamv = A("lamv", 4 * 64)
        lamt = A("lamt", 2 * 64)
        lams = A("lams", 8)
        mx = A("mx", 4)
        rsum = A("rsum", 4)
        rinv = A("rinv", 4)
        rsum2 = A("rsum2", 4)
        gqk4 = A("gqk4", 4)
        rotg = A("rotg", 2 * P)
        tq = A("tq", QKW)
        tr = A("tr", QKW)
        gqk = A("gqk", 2)
        oT = sb("oT", HEADS * SEQ, at=A.at)
        A.at += 4 * HEADS * SEQ
        assert A.at <= 229344 - 32
        A = At(region)
        xf = A("xf", KD * SEQ)
        dft = A("dft", 2048)
        yt = A("yt", 2 * 4 * 512)
        A = At(region)
        sbq = A("sbq", 4 * SEQ)
        sbk = A("sbk", 4 * SEQ)
        sbv = A("sbv", 2 * 512)
        rq = A("rq", 4 * SEQ)
        rk = A("rk", 4 * SEQ)
        rvt = A("rvt", 2 * D)
        rg = A("rg", KD * SEQ)
        gates = A("gates", 16 * SEQ)
        wz = A("wz", 5 * 2 * DEC_W)
        decay = A("decay", 2 * DEC_W)
        yr = sb("yr", HEADS * SEQ, at=region)
        rvar = sb("rvar", HEADS * SEQ, at=region + 4 * (8 * SEQ + D))
        A = At(modw_at)
        xr = A("xr", KD * SEQ)
        cmb = A("cmb", N_EXPERTS * SEQ)
        sel = A("sel", N_EXPERTS * P, parts=N_EXPERTS)
        wr = A("wr", KD * 20)
        rbias = A("rbias", 20)
        lg = A("lg", 2 * 20)
        tiny = A("tiny", 2 * 64)
        cmbT = A("cmbT", SEQ, parts=N_EXPERTS)
        yt_out = sb("yt_out", 2 * D, at=region)

        ps = ctx.enter_context(nc.psum_tensor("ps", [P, 8 * 512], F32))

        def bank(b, n=512, first=0, parts=slice(0, P)):
            return ps[parts, 512 * b + first:512 * b + first + n]

        modps = bank(7).rearrange("p (b c) -> p b c", c=2)

        landed = [sem(f"landed{u}") for u in range(U)]
        hi_ready = sem("hi_ready")
        lo_ready = sem("lo_ready")
        slab_done = sem("slab_done")
        evacuated = sem("evacuated")
        sg_ready = sem("sg_ready")
        hhi_ready = sem("hhi_ready")
        hlo_ready = sem("hlo_ready")
        mod_landed = [sem(f"mod_landed{s}") for s in range(U)]
        mod_early_landed = [sem(f"mod_early_landed{m}") for m in range(MOD_FIRST)]
        mod_first_done = sem("mod_first_done")
        mod_rows = sem("mod_rows")
        mod_rows_copied = sem("mod_rows_copied")
        mod_scaled = sem("mod_scaled")
        mod_link = sem("mod_link")
        mod_jobs = sem("mod_jobs")
        mod_summed = sem("mod_summed")
        mod_copied = sem("mod_copied")
        sq_ready = sem("sq_ready")
        sq_used = sem("sq_used")
        sq_summed = sem("sq_summed")
        var_ready = sem("var_ready")
        rstd_ready = sem("rstd_ready")
        nt_ready = sem("nt_ready")
        nhi_ready = sem("nhi_ready")
        nlo_ready = sem("nlo_ready")
        in_x = sem("in_x")
        in_vec = sem("in_vec")
        in_const = sem("in_const")
        vec_turned = sem("vec_turned")
        cols_ready = sem("cols_ready")
        csil_ready = sem("csil_ready")
        eps_ready = sem("eps_ready")
        dve_link = sem("dve_link")
        act_link = sem("act_link")
        out_done = sem("out_done")
        x_rows_turned = sem("x_rows_turned")
        x_turned = sem("x_turned")
        fin_turned = sem("fin_turned")
        fin_copied = sem("fin_copied")

        def x_half(x):
            return x[:, :].rearrange("p (k n) -> p k n", k=KD)[:, :, X_COLS]

        def two(b):
            return ps[:, 512 * b:512 * b + 1024].rearrange("p (a n) -> p a n", a=2)[:, :, 0:DEC_W]

        def wk(i):
            return wz[:, i * 2 * DEC_W:(i + 1) * 2 * DEC_W]

        def wk3(i):
            return wk(i).rearrange("p (a n) -> p a n", a=2)

        TINY = {}

        def tn(h, name, n):
            if name not in TINY:
                TINY[name] = (sum(w for _, w in TINY.values()), n)
            at, n = TINY[name]
            assert at + n <= 64
            return tiny[:, 64 * h + at:64 * h + at + n]

        def fin_copy(eng, k):
            eng.wait_ge(fin_turned, k + 1)
            dst = yt_out[:, :].rearrange("p (h n) -> p h n", h=2)[:, :, k * P:(k + 1) * P]
            nc.vector.tensor_copy(dst, bank(k % 4, SEQ).rearrange("p (h n) -> p h n", h=2)).then_inc(fin_copied, 1)

        def const(name, cols_=None):
            at, n = CONST[name]
            return cst[:, at:at + (n if cols_ is None else cols_)]

        def col(name, k=0):
            at = VEC[name] + k
            return cols[:, at:at + 1]

        def chunk(x, c, width=BOTH, part=slice(0, BOTH)):
            w = (part.stop if part.stop is not None else width) - (part.start or 0)
            return x[:, bass.ds(c * width + (part.start or 0), w)]

        def qk_sum_at(part, h):
            if part == "k":
                return max(2 * h, 1)
            return min(2 * h + 3, 2 * HEADS)

        def tok(T):
            return slice(BOTH - T, BOTH)

        def k128(w):
            return w.rearrange("(k p) n -> p k n", p=P)

        def run(eng, rounds, body, peel_first=False):
            first = 0
            if peel_first and rounds > 1:
                body(0, False)
                first = 1
            if rounds - 1 - first >= 2:
                with eng.Fori(first, rounds - 1) as i:
                    body(i, False)
            else:
                for i in range(first, rounds - 1):
                    body(i, False)
            body(rounds - 1, True)

        NORMS = ["l0n0", "l0n1", "l0n2", "l1n0", "l1n1", "l1n2", "mix", "ffn", "final"]

        S = {}

        def stage_sem(name):
            if name not in S:
                S[name] = sem(name)
            return S[name]

        for name in ("in_lam", "in_halves", "in_heads", "qk_summed", "in_dft", "in_dec0", "in_dec1", "in_router", "in_rbias", "in_sel",
                     "qk_sq", "qk_ss", "qk_var", "qk_rstd", "qk_done", "rotg_ready", "s_done", "max_done", "exp_done",
                     "a_done", "at_done", "at_copied", "o_done", "o_copied", "lam_sum", "lam_exp", "lam_ready",
                     "on_sq", "on_ss", "on_spread", "on_var", "on_rstd", "on_full", "on_hi", "on_lo",
                     "xf_ready", "y_done", "y_copied", "f_done", "f_copied", "f_hi", "f_lo",
                     "rot_ps", "rot_done", "z_done", "abs_done", "e_done", "sp_done", "lk_done", "suf_done",
                     "arg_done", "w_exp", "w_done", "sbo_done", "sbo_full", "sb_hi", "sb_lo",
                     "rs_done", "rw_done", "ro_done", "ro_sq", "ro_ss", "ro_var", "ro_rstd", "ro_full", "ro_hi", "ro_lo",
                     "gate_raw", "gate_done", "rg_done", "mix_full", "mix_hi", "mix_lo",
                     "rt_ps", "rt_max", "rt_exp", "rt_e2in", "rt_e2", "rt_comb", "rt_turned", "rt_copied",
                     "cmb_ps", "cmb_done", "cu_ready"):
            stage_sem(name)

        def vector_rows():
            pairs = []
            for name, src in (("c", t["c"]), ("c_ctx", t["c_ctx"].rearrange("(a n) -> a n", a=1)),
                              ("norm_g", t["norm_g"].rearrange("l s n -> (l s) n")), ("norm_mix", t["norm_mix_g_2"]),
                              ("norm_ffn", t["norm_ffn_g_2"]), ("norm_final", t["norm_final_g_2"].rearrange("(a n) -> a n", a=1)),
                              ("ret_norm", t["ret_norm_g_2"]), ("b_gate", t["b_gate_2"])):
                n = src.shape[0] * src.shape[1] // P
                pairs.append((vrow[VEC[name]:VEC[name] + n, 0:P], src.rearrange("a (k p) -> (a k) p", p=P)))
            for half in range(2):
                for name, src in (("q_g", t["attn_q_g"]), ("k_g", t["attn_k_g"])):
                    pairs.append((vrow[VEC[name]:VEC[name] + 1, 64 * half:64 * half + 64], src))
            pairs.append((vrow[VEC["sub_g"]:VEC["sub_g"] + 1, 0:P], t["attn_sub_g"]))
            for l in range(2):
                pairs.append((vrow[0:72, (1 + l) * P:(2 + l) * P], t["b_mod"][l, :].rearrange("(k p) -> k p", p=P)))
            return pairs

        block = ctx.enter_context(nc.Block())

        @block.sync
        def _(sp):
            def mod_unit(l, m, dst, landed_):
                sp.dma_start(dst.rearrange("p (k n) -> p k n", k=KD), k128(t["w_mod"][l])[:, :, bass.ds(m * MOD_W, MOD_W)]).then_inc(landed_, 16)

            for dst, src in vector_rows()[:N_VEC_DMAS // 2]:
                sp.dma_start(dst, src).then_inc(in_vec, 16)
            for i, src in enumerate((t["ctx"], t["x"])):
                for h in range(2):
                    sp.dma_start(xraw[:, (2 * i + h) * D:(2 * i + h + 1) * D], src[0, h * P:(h + 1) * P, :]).then_inc(in_x, 16)
            for m in range(MOD_NEED):
                mod_unit(0, m, mod_early[m][:, :], mod_early_landed[m])

            def slab(r, u, nk, src, first=False):
                if not first:
                    sp.wait_ge(lo_ready, U * (r - 1) + u + 1)
                sp.dma_start(raw[:, u * SLOT:u * SLOT + nk * P].rearrange("p (k n) -> p k n", k=nk), src).then_inc(landed[u], 16)

            def cols_of(w, c):
                return k128(w)[:, :, bass.ds(c * P, P)]

            MOD_CUTS = ((0, 1, 2, 3, 4), (0, 3, 4), (0, 3))

            def mod_load(r, u, lowest, jobs=range(MOD_JOBS - MOD_HELD)):
                job = U * lowest + u - MOD_AHEAD

                def unit(l, m, slot):
                    mod_unit(l, m, modw[:, slot * KD * MOD_W:(slot + 1) * KD * MOD_W], mod_landed[slot])

                if job not in jobs:
                    return
                if job < 2 * MOD_BOTH:
                    q = job // 2
                    if job % 2 == 0:
                        if q >= 2:
                            sp.wait_ge(mod_jobs, 2 * (q - 1))
                        unit(0, MOD_FIRST + q, 2 * (q % 2))
                    return
                slot = (u - MOD_AHEAD) % U
                if job < 2 * MOD_BOTH + U:
                    if slot % 2:
                        sp.wait_ge(mod_first_done, MOD_NEED + 2)
                    else:
                        sp.wait_ge(mod_jobs, 2 * MOD_BOTH - 2 + slot)
                else:
                    sp.wait_ge(mod_jobs, U * r + (u - MOD_AHEAD - U + 1))
                first = MOD_FIRST - MOD_BOTH
                l = 1 if job + first >= MOD_UNITS else 0
                unit(l, U * r + (u - MOD_AHEAD + first - l * MOD_UNITS), slot)

            def ffn(name, w_gu, w_d, mods=False):
                at = 0
                for th, size in enumerate(THIRDS):
                    r0, rounds, _ = ph[f"{name}.up{th}"]
                    cuts = MOD_CUTS[th] if mods else (0, rounds)
                    for i0, i1 in zip(cuts, cuts[1:]):
                        def up(i):
                            for u in range(U):
                                slab(i + r0, u, KD, cols_of(w_gu, 2 * i + (at + u // 2 + (D_FF // P if u % 2 else 0))),
                                     first=r0 + i1 == 1)
                                if mods:
                                    mod_load(i + r0, u, r0 + i0)
                        if i1 - i0 > 1:
                            with sp.Fori(i0, i1) as i:
                                up(i)
                        else:
                            up(i0)
                        if mods and r0 + i0 == 0:
                            for m in range(MOD_NEED, MOD_FIRST):
                                if m == MOD_NEED + 2:
                                    sp.wait_ge(x_rows_turned, 8)
                                mod_unit(0, m, mod_early[m][:, :], mod_early_landed[m])
                    r0, rounds, _ = ph[f"{name}.down{th}"]
                    for i in range(rounds):
                        for u in range(U):
                            c = U * i + u
                            slab(r0 + i, u, size, k128(w_d[at * P:(at + size) * P, :])[:, :, c * P:(c + 1) * P])
                            if mods:
                                mod_load(r0 + i, u, r0 + i)
                    at += size

            ffn("l0f1", t["ffn1_w_gu"][0], t["ffn1_w_d"][0], mods=True)

            def plain(name, w, c0, nk=KD, mods=False):
                r0, rounds, _ = ph[name]
                for i in range(rounds):
                    for u in range(U):
                        c = c0 + U * i + u
                        slab(r0 + i, u, nk, k128(w)[:, :, c * P:(c + 1) * P])
                        if mods:
                            r = r0 + i - MOD_SHIFT
                            mod_load(r, u, r, range(MOD_JOBS - MOD_HELD, MOD_JOBS))

            w = t["attn_w_qkv"][0]
            plain("k", w, KD, mods=True)
            plain("q", w, 0, mods=True)
            sp.wait_ge(evacuated, 4 * ph["k"][0])
            sp.wait_ge(mod_jobs, MOD_JOBS)
            for i, name in enumerate(("attn_lam_q1", "attn_lam_k1", "attn_lam_q2", "attn_lam_k2")):
                sp.dma_start(lamv[:, 64 * i:64 * i + 64], t[name][0:1, :].to_broadcast([P, 64])).then_inc(S["in_lam"], 16)
            sp.dma_start(half_rows[:, :], t["half_rows"]).then_inc(S["in_halves"], 16)
            plain("v", w, 2 * KD)
            plain("wo", t["attn_w_o"][0], 0)
            ffn("l0f2", t["ffn2_w_gu"][0], t["ffn2_w_d"][0])
            ffn("l1f1", t["ffn1_w_gu"][1], t["ffn1_w_d"][1])
            plain("fourier", t["fourier_w"][0], 0)
            sp.wait_ge(evacuated, 4 * ph["fourier"][0])
            sp.dma_start(dft[:, :], t["dft"]).then_inc(S["in_dft"], 16)
            ffn("l1f2", t["ffn2_w_gu"][1], t["ffn2_w_d"][1])
            w = t["w_in_2"][0]
            for name, c0 in (("sbq", 0), ("sbk", 4), ("sbv", 8), ("rq", 12), ("rk", 16), ("rv", 20), ("rg", 28)):
                plain(name, w, c0)
            plain("gates", t["w_gate_2"][0], 0)
            plain("sbout", t["w_sb_out_2"][0], 0, 4)
            for h in range(HEADS):
                if h < 2:
                    sp.wait_ge(evacuated, 4 * ph["sbq"][0])
                else:
                    sp.wait_ge(S["rw_done"], h - 1)
                sp.dma_start(decay[:, (h % 2) * DEC_W:(h % 2 + 1) * DEC_W], t["decay"][:, h * DEC_W:(h + 1) * DEC_W]).then_inc(S[f"in_dec{h % 2}"], 16)
            plain("retout", t["w_ret_out_2"][0], 0)
            plain("wout", t["w_out_2"][0], 0)
            sp.wait_ge(S["mix_lo"], KD)
            sp.dma_start(wr[:, :].rearrange("p (k n) -> p k n", k=KD)[:, :, 0:4], k128(t["w_group_router_2"][0])).then_inc(S["in_router"], 16)
            sp.dma_start(wr[:, :].rearrange("p (k n) -> p k n", k=KD)[:, :, 4:20], k128(t["w_expert_router_2"][0])).then_inc(S["in_router"], 16)
            sp.dma_start(rbias[:, 0:4], t["b_group_router_2"][0:1, :].to_broadcast([P, 4])).then_inc(S["in_rbias"], 16)
            sp.dma_start(rbias[:, 4:20], t["b_expert_router_2"][0:1, :].to_broadcast([P, 16])).then_inc(S["in_rbias"], 16)
            sp.dma_start(sel[:, :], t["expert_rows"]).then_inc(S["in_sel"], 16)

            r0 = ph["moe"][0]
            with sp.Fori(0, N_EXPERTS) as e:
                for i in range(2):
                    for u in range(U):
                        w = t["w_exp_up_2"] if u % 2 else t["w_exp_gate_2"]
                        src = w.rearrange("l e (k p) n -> p (l e) k n", p=P)[:, bass.ds(e, 1), :, (2 * i + u // 2) * P:(2 * i + u // 2 + 1) * P]
                        slab(4 * e + (r0 + i), u, KD, src.rearrange("p a k n -> p (a k) n"))
                for i in range(2):
                    for u in range(U):
                        c = U * i + u
                        src = t["w_exp_down_2"].rearrange("l e (k p) n -> p (l e) k n", p=P)[:, bass.ds(e, 1), :, c * P:(c + 1) * P]
                        slab(4 * e + (r0 + 2 + i), u, 4, src.rearrange("p a k n -> p (a k) n"))
            sp.wait_ge(fin_copied, KD)
            for h in range(2):
                sp.dma_start(out[0, h * P:(h + 1) * P, :], yt_out[:, h * D:(h + 1) * D]).then_inc(out_done, 16)
            sp.wait_ge(out_done, 32)

        @block.scalar
        def _(act):
            link_at = [0]

            def link(ins):
                link_at[0] += 1
                ins.then_inc(act_link, 1)
                act.wait_ge(act_link, link_at[0])

            def split_hi(r, u, nk, wait_done=True):
                act.wait_ge(landed[u], 16 * r + 16)
                if wait_done:
                    act.wait_ge(slab_done, U * (r - 1) + u + 1)
                nc.scalar.activation(hi[:, u * SLOT:u * SLOT + nk * P], raw[:, u * SLOT:u * SLOT + nk * P], ACT.Copy).then_inc(hi_ready, 1)

            def plain(name, side=None, squares=None, mods=None):
                r0, rounds, nk = ph[name]

                def body(i, last):
                    for u in range(U):
                        if mods is not None:
                            if i == u == 0:
                                mod_scale(r0 - mods, 0, r0 - mods)
                            if U * i + u + 1 < U * rounds:
                                mod_scale(r0 - mods + i + (u + 1) // U, (u + 1) % U, r0 - mods + i)
                        if squares and i == 0 and u == 0:
                            nc.scalar.activation(rootc[:, :], epsc[:, :], ACT.Sqrt)
                        if squares:
                            square(squares[0], squares[1], U * i + u, U * (r0 + i) + u + 1)
                        n_k = next_nk(name) if last else nk
                        if n_k:
                            split_hi(i + (r0 + 1), u, n_k)
                        if side:
                            side(U * i + u)
                if side or squares or mods is not None:
                    for i in range(rounds):
                        body(i, i == rounds - 1)
                else:
                    run(act, rounds, body)

            def mod_scale(r, u, lowest):
                if U * lowest < 2 * MOD_BOTH:
                    return
                act.wait_ge(mod_landed[u], 16 * r + 16 * (1 - 2 * MOD_BOTH // U + (0 if u % 2 else MOD_BOTH // 2)))
                for k in range(MOD_SCALED):
                    at = (u * KD + k) * MOD_W
                    ins = nc.scalar.activation(modw[:, at:at + MOD_W], modw[:, at:at + MOD_W], ACT.Copy, scale=csil[:, k:k + 1])
                ins.then_inc(mod_scaled, 1)

            def hidden_pair(r, p, T, j, split0, split1):
                act.wait_ge(slab_done, U * r + 2 * p + 2)
                nc.scalar.activation(sg[:, p * BOTH:p * BOTH + T], bank(2 * p, T), ACT.Silu).then_inc(sg_ready, 1)
                split0()
                act.wait_ge(evacuated, U * r + 2 * p + 2)
                nc.scalar.activation(chunk(hhi, j, part=tok(T)), hf[:, p * BOTH:p * BOTH + T], ACT.Copy).then_inc(hhi_ready, 1)
                split1()

            def ffn(name, T, squares=None, mods=False):
                for th, size in enumerate(THIRDS):
                    key = f"{name}.up{th}"
                    r0, rounds, nk = ph[key]

                    def up(i, last):
                        n_k = next_nk(key) if last else nk
                        for p in range(2):
                            def split(u):
                                split_hi(i + (r0 + 1), u, n_k)
                                if mods:
                                    mod_scale(i + r0, u, r0)
                            hidden_pair(i + r0, p, T, 2 * i + p, lambda: split(2 * p), lambda: split(2 * p + 1))
                    run(act, rounds, up)
                    plain(f"{name}.down{th}", squares=squares if th == len(THIRDS) - 1 else None,
                          mods=0 if mods and th < len(THIRDS) - 1 else None)

            def square(s, T, k, after):
                if after:
                    act.wait_ge(evacuated, after)
                if k == 1 and s:
                    act.wait_ge(sq_summed, s)
                if k >= 2:
                    act.wait_ge(sq_used, (KD - 1) * s + k - 1)
                nc.scalar.activation(sq[:, (k % 2) * BOTH:(k % 2) * BOTH + T], chunk(xs, k, part=tok(T)), ACT.Square).then_inc(sq_ready, 1)

            def norm_root(s, T):
                act.wait_ge(var_ready, 2 * s + 2)
                nc.scalar.activation(rstd[:, 0:T], rv_[:, 0:T], ACT.Sqrt).then_inc(rstd_ready, 1)

            def norm_hi(s, T, shift, full=None, between=None):
                for k in range(KD):
                    if between:
                        between(k)
                    act.wait_ge(nt_ready, KD * s + k + 1)
                    src = nt[:, (k % 2) * BOTH:(k % 2) * BOTH + T]
                    if full is not None:
                        nc.scalar.activation(full[:, k * SEQ:(k + 1) * SEQ], src, ACT.Identity, bias=shift(k)[0]).then_inc(S["xf_ready"], 1)
                    halves = list(zip(shift(k), (T - SEQ, 0)))
                    for b, at in halves:
                        ins = nc.scalar.activation(chunk(nhi, k, part=slice(BOTH - T + at, BOTH - T + at + SEQ)), src[:, at:at + SEQ], ACT.Identity, bias=b)
                    ins.then_inc(nhi_ready, 1)

            def norm(s, T, shift, full=None):
                norm_root(s, T)
                norm_hi(s, T, shift, full)

            def mod_shift(sets, s):
                return lambda k: [modc[:, 72 * c + 24 * s + k:72 * c + 24 * s + k + 1] for c in sets]

            act.dma_start(cst[:, :], t["consts"]).then_inc(in_const, 16)
            act.dma_start(head_rows[:, :], t["expert_rows"][0:HEADS, 0:HEADS * P]).then_inc(S["in_heads"], 16)
            for dst, src in vector_rows()[N_VEC_DMAS // 2:]:
                act.dma_start(dst, src).then_inc(in_vec, 16)

            act.wait_ge(cols_ready, 1)
            nc.scalar.activation(csil[:, :], cols[:, 0:16], ACT.Silu).then_inc(csil_ready, 1)
            act.wait_ge(eps_ready, 1)
            nc.scalar.activation(rootc[:, :], epsc[:, :], ACT.Sqrt)
            act.wait_ge(x_turned, 8)
            for k in range(KD):
                square(0, BOTH, k, 0)

            def mod_row_copy(m):
                act.wait_ge(mod_rows, m + 1)
                if m >= 2:
                    act.wait_ge(mod_first_done, m - 1)
                nc.scalar.activation(mrow[:, (m % 2) * MOD_W:(m % 2 + 1) * MOD_W], bank(5 + m % 2, MOD_W, parts=slice(0, 2)), ACT.Copy).then_inc(mod_rows_copied, 1)

            for m in range(MOD_NEED):
                mod_row_copy(m)
                if m == 1:
                    norm_root(0, BOTH)
                if m == 5:
                    act.wait_ge(mod_first_done, 4)
                if m >= 5:
                    split_hi(0, m - 5, KD, wait_done=False)
            split_hi(0, 3, KD, wait_done=False)

            norm_hi(0, BOTH, mod_shift((0, 1), 0), between=lambda k: mod_row_copy(MOD_NEED + k // 2) if k % 2 == 0 else None)
            ffn("l0f1", BOTH, squares=(1, BOTH), mods=True)
            norm(1, BOTH, mod_shift((0, 1), 1))
            plain("k", mods=MOD_SHIFT)
            def qk_square(part, h):
                n = BOTH if part == "k" else SEQ
                if part == "k":
                    src, dst = qk[:, h * QKW + SEQ:(h + 1) * QKW], sq[:, (h % 2) * BOTH:(h % 2 + 1) * BOTH]
                    act.wait_ge(evacuated, U * ph["q"][0])
                else:
                    src, dst = qk[:, h * QKW:h * QKW + SEQ], nt[:, (h % 2) * SEQ:(h % 2 + 1) * SEQ]
                    act.wait_ge(evacuated, U * ph["q"][0] + h + 1)
                if h >= 2:
                    act.wait_ge(S["qk_summed"], qk_sum_at(part, h - 2))
                nc.scalar.activation(dst, src, ACT.Square).then_inc(S["qk_sq"], 1)

            def qk_squares(c):
                qk_square("k", c)
                if c:
                    qk_square("q", c - 1)

            plain("q", side=qk_squares)
            qk_square("q", HEADS - 1)
            act.wait_ge(S["qk_var"], 2)
            nc.scalar.activation(tq[0:2 * HEADS, :], tr[0:2 * HEADS, :], ACT.Sqrt).then_inc(S["qk_rstd"], 1)
            plain("v")

            act.wait_ge(S["lam_sum"], 1)
            nc.scalar.activation(lams[:, 2:4], lams[:, 0:2], ACT.Exp).then_inc(S["lam_exp"], 1)

            def o_square(h):
                act.wait_ge(S["o_copied"], h + 1)
                nc.scalar.activation(qk[:, h * QKW:h * QKW + SEQ], oT[:, h * SEQ:(h + 1) * SEQ], ACT.Square).then_inc(S["on_sq"], 1)

            for h in range(HEADS):
                for ti in range(4):
                    act.wait_ge(S["max_done"], 4 * h + ti + 1)
                    if h:
                        act.wait_ge(S["at_done"], h)
                    nc.scalar.activation(ee[:, ti * BOTH:(ti + 1) * BOTH], bank(4 + ti), ACT.Exp, bias=mx[:, ti:ti + 1],
                                         scale=0.125, accum_out=rsum[:, ti:ti + 1]).then_inc(S["exp_done"], 1)
                act.wait_ge(S["at_done"], h + 1)
                if h:
                    act.wait_ge(S["o_done"], h)
                for b in range(2):
                    nc.scalar.activation(aT[:, 512 * b:512 * b + 512], bank(b), ACT.Copy).then_inc(S["at_copied"], 1)
                if h:
                    o_square(h - 1)
            o_square(HEADS - 1)
            act.wait_ge(S["on_var"], 2)
            nc.scalar.activation(tq[0:HEADS, 0:SEQ], tr[0:HEADS, 0:SEQ], ACT.Sqrt).then_inc(S["on_rstd"], 1)
            for h in range(HEADS):
                act.wait_ge(S["on_full"], h + 1)
                nc.scalar.activation(chunk(nhi, h, part=X_COLS), oT[:, h * SEQ:(h + 1) * SEQ], ACT.Copy).then_inc(S["on_hi"], 1)
            plain("wo", squares=(2, SEQ))
            norm(2, SEQ, mod_shift((0,), 2))
            ffn("l0f2", SEQ, squares=(3, SEQ))
            norm(3, SEQ, mod_shift((2,), 0))
            ffn("l1f1", SEQ, squares=(4, SEQ))

            norm(4, SEQ, mod_shift((2,), 1), full=xf)
            for i in range(8):
                act.wait_ge(S["y_done"], i + 1)
                nc.scalar.activation(yt[:, 512 * i:512 * i + 512], bank(i % 4), ACT.Copy).then_inc(S["y_copied"], 1)
            for c in range(KD):
                act.wait_ge(S["f_done"], c + 1)
                nc.scalar.activation(chunk(nhi, c, part=X_COLS), bank(4 + c % 4, SEQ), ACT.Copy).then_inc(S["f_hi"], 1)
            plain("fourier", squares=(5, SEQ))
            norm(5, SEQ, mod_shift((2,), 2))
            ffn("l1f2", SEQ, squares=(6, SEQ))

            norm(6, SEQ, lambda k: [zcol[:, 0:1]])
            for name in ("sbq", "sbk", "sbv", "rq", "rk", "rv", "rg", "gates"):
                plain(name)
            act.wait_ge(evacuated, U * ph["sbout"][0])
            nc.scalar.activation(rg[:, :], rg[:, :], ACT.Silu).then_inc(S["rg_done"], 1)
            nc.scalar.activation(gates[:, :], gates[:, :], ACT.Sigmoid).then_inc(S["gate_done"], 1)
            for c in range(4):
                z = two(2 * (c % 2))
                if c:
                    act.wait_ge(S["w_done"], c)
                act.wait_ge(S["z_done"], c + 1)
                link(nc.scalar.activation(wk3(0), z, ACT.Abs, scale=0.125))
                link(nc.scalar.activation(wk(1), wk(0), ACT.Exp, scale=-1.0))
                nc.scalar.activation(wk(0), wk(1), ACT.Ln, bias=const("ones", 1)).then_inc(S["sp_done"], 1)
                act.wait_ge(S["arg_done"], c + 1)
                nc.scalar.activation(wk(0), wk(1), ACT.Exp).then_inc(S["w_exp"], 1)
                act.wait_ge(S["sbo_done"], c + 1)
                nc.scalar.activation(chunk(nhi, c, part=slice(0, SEQ)), bank(2 * (c % 2), SEQ), ACT.Copy).then_inc(S["sb_hi"], 1)
            act.wait_ge(S["ro_done"], HEADS)
            act.wait_ge(S["ro_full"], HEADS)
            nc.scalar.activation(rvt[:, :], yr[:, :], ACT.Square).then_inc(S["ro_sq"], 1)
            act.wait_ge(S["ro_var"], 2)
            nc.scalar.activation(rvar[:, :], rvt[:, :], ACT.Sqrt).then_inc(S["ro_rstd"], 1)
            for h in range(HEADS):
                act.wait_ge(S["mix_full"], h + 1)
                nc.scalar.activation(chunk(nhi, h, part=X_COLS), yr[:, h * SEQ:(h + 1) * SEQ], ACT.Copy).then_inc(S["ro_hi"], 1)
            plain("sbout")
            plain("retout")
            for c in range(KD):
                act.wait_ge(S["gate_raw"], c + 1)
                nc.scalar.activation(chunk(nhi, c, part=X_COLS), gates[:, c * SEQ:(c + 1) * SEQ], ACT.Copy).then_inc(S["mix_hi"], 1)
            plain("wout", squares=(7, SEQ))

            norm(7, SEQ, lambda k: [zcol[:, 0:1]], full=xr)
            for h in range(2):
                act.wait_ge(S["rt_max"], h + 1)
                nc.scalar.activation(tn(h, "e", 4), lg[:, 20 * h:20 * h + 4], ACT.Exp, bias=tn(h, "negm", 1), accum_out=tn(h, "sum", 1)).then_inc(S["rt_exp"], 1)
                act.wait_ge(S["rt_e2in"], h + 1)
                nc.scalar.activation(tn(h, "e2", 1), tn(h, "d", 1), ACT.Exp).then_inc(S["rt_e2"], 1)
            for b in range(N_EXPERTS // 2):
                act.wait_ge(S["cmb_ps"], 2 * b + 2)
                nc.scalar.activation(cmb[:, 512 * b:512 * b + 512], bank(4 + b % 4), ACT.Copy).then_inc(S["cmb_done"], 1)

            r0 = ph["moe"][0]

            def expert(e, last):
                for i in range(2):
                    n_k = KD if i == 0 else 4
                    for p in range(2):
                        hidden_pair(4 * e + (r0 + i), p, SEQ, 2 * i + p, lambda: split_hi(4 * e + (r0 + i + 1), 2 * p, n_k),
                                    lambda: split_hi(4 * e + (r0 + i + 1), 2 * p + 1, n_k))
                for i in range(2):
                    for u in range(U):
                        if last:
                            square(8, SEQ, U * i + u, U * (4 * e + r0 + 2 + i) + u + 1)
                        if i == 0 or not last:
                            split_hi(4 * e + (r0 + 2 + i + 1), u, 4 if i == 0 else KD)
            run(act, N_EXPERTS, expert)

            norm_root(8, SEQ)

        @block.vector
        def _(dve):
            link_at = [0]

            def link(ins):
                link_at[0] += 1
                ins.then_inc(dve_link, 1)
                dve.wait_ge(dve_link, link_at[0])

            v = nc.vector

            def split_lo(r, u, nk):
                dve.wait_ge(hi_ready, U * r + u + 1)
                s = slice(u * SLOT, u * SLOT + nk * P)
                v.tensor_tensor(lo[:, s], raw[:, s], hi[:, s].bitcast(F32), ALU.subtract).then_inc(lo_ready, 1)

            def add_square(s, T, k):
                dve.wait_ge(sq_ready, KD * s + k + 1)
                acc, x = sqsum[:, 0:T], sq[:, (k % 2) * BOTH:(k % 2) * BOTH + T]
                if k == 1:
                    if s:
                        dve.wait_ge(sq_summed, s)
                    v.tensor_tensor(acc, sq[:, 0:T], x, ALU.add).then_inc(sq_used, 2)
                else:
                    dve.wait_ge(sq_used, (KD - 1) * s + k)
                    v.tensor_tensor(acc, acc, x, ALU.add).then_inc(sq_used, 1)

            def plain(name, evac, mods=None, side=None, squares=None):
                r0, rounds, nk = ph[name]

                def body(i, last):
                    for u in range(U):
                        if mods is not None:
                            mod_job(i + r0 - mods, u, r0 - mods)
                        dve.wait_ge(slab_done, U * i + (U * r0 + u + 1))
                        evac(u, U * i + u)
                        if squares and U * i + u >= 2:
                            add_square(squares[0], squares[1], U * i + u - 1)
                        n_k = next_nk(name) if last else nk
                        if n_k:
                            split_lo(i + (r0 + 1), u, n_k)
                        if side:
                            side(U * i + u)
                if mods is not None or side or squares:
                    for i in range(rounds):
                        body(i, i == rounds - 1)
                else:
                    run(dve, rounds, body)

            def rows_pairs(name, evac, side=None, before=None):
                r0, rounds, nk = ph[name]
                for i in range(rounds):
                    for p in range(2):
                        if before:
                            before(2 * i + p)
                        dve.wait_ge(slab_done, U * (r0 + i) + 2 * p + 2)
                        evac(p, 2 * i + p)
                        for u in (2 * p, 2 * p + 1):
                            split_lo(i + (r0 + 1), u, nk if i < rounds - 1 else next_nk(name))
                        if side:
                            side(2 * i + p)

            def mod_job(r, u, lowest):
                def acc(u):
                    return macc[:, u * MOD_W:(u + 1) * MOD_W]

                if U * lowest < 2 * MOD_BOTH:
                    if u % 2 == 0:
                        return
                    p = u // 2
                    dve.wait_ge(mod_landed[2 * p], 16 * r + 16)
                    if lowest:
                        dve.wait_ge(mod_summed, U * r + (u - (U - 1)))
                    base = 4 * (KD - 1) * r + 2 * (KD - 1) * p
                    for k in range(KD):
                        wk_ = modw[:, (2 * p * KD + k) * MOD_W:(2 * p * KD + k + 1) * MOD_W]
                        for cond in range(2):
                            a, c = acc(u - 1 + cond), csil[:, KD * cond + k:KD * cond + k + 1]
                            if k == 0:
                                ins = v.tensor_scalar(a, wk_, c, None, ALU.mult)
                            else:
                                dve.wait_ge(mod_link, base + 2 * k + (cond - 1))
                                ins = v.scalar_tensor_tensor(out=a, in0=wk_, scalar=c, in1=a, op0=ALU.mult, op1=ALU.add)
                            if k < KD - 1:
                                ins.then_inc(mod_link, 1)
                    ins.then_inc(mod_jobs, 2)
                    return
                job = U * r + u
                rest = KD - MOD_SCALED
                w = modw[:, u * KD * MOD_W:(u + 1) * KD * MOD_W]
                dve.wait_ge(mod_scaled, job + (1 - 2 * MOD_BOTH))
                for k in range(rest):
                    wk_ = w[:, (MOD_SCALED + k) * MOD_W:(MOD_SCALED + k + 1) * MOD_W]
                    v.scalar_tensor_tensor(out=wk_, in0=wk_, scalar=csil[:, MOD_SCALED + k:MOD_SCALED + k + 1], in1=w[:, k * MOD_W:(k + 1) * MOD_W],
                                           op0=ALU.mult, op1=ALU.add).then_inc(mod_link, 1)
                dve.wait_ge(mod_link, rest * job + (rest + 2 * MOD_BOTH * (KD - 1 - rest)))
                dve.wait_ge(mod_summed, job - (U - 1))
                v.reduce_sum(acc(u), w[:, rest * MOD_W:].rearrange("p (k n) -> p n k", n=MOD_W), AX_X).then_inc(mod_jobs, 1)

            def hidden_pair(r, p, T, h, j, split0, split1, weigh=None):
                f = hf[:, p * BOTH:p * BOTH + T]
                up = bank(2 * p + 1, T)
                if not (isinstance(h, int) and h < 2):
                    dve.wait_ge(hlo_ready, h - 1)
                if weigh is not None:
                    dve.wait_ge(slab_done, U * r + 2 * p + 2)
                    v.tensor_tensor(f, up, weigh, ALU.mult).then_inc(S["cu_ready"], 1)
                    up = f
                    dve.wait_ge(S["cu_ready"], h + 1 - moe_h0)
                dve.wait_ge(sg_ready, h + 1)
                v.tensor_tensor(f, sg[:, p * BOTH:p * BOTH + T], up, ALU.mult).then_inc(evacuated, 2)
                split0()
                dve.wait_ge(hhi_ready, h + 1)
                v.tensor_tensor(chunk(hlo, j, part=tok(T)), f, chunk(hhi, j, part=tok(T)).bitcast(F32), ALU.subtract).then_inc(hlo_ready, 1)
                split1()

            h_at = [0]
            moe_h0 = 4 * sum(THIRDS)

            def ffn(name, T, gate, squares, mods=False):
                for th, size in enumerate(THIRDS):
                    key = f"{name}.up{th}"
                    r0, rounds, nk = ph[key]

                    def up(i, last):
                        n_k = next_nk(key) if last else nk
                        for p in range(2):
                            def split(u):
                                split_lo(i + (r0 + 1), u, n_k)
                                if mods:
                                    mod_job(i + r0, u, i if isinstance(i, int) and r0 == 0 else max(r0, 1))
                            hidden_pair(i + r0, p, T, 2 * i + (h_at[0] + p), 2 * i + p, lambda: split(2 * p), lambda: split(2 * p + 1))
                    run(dve, rounds, up, peel_first=mods and th == 0)
                    h_at[0] += size
                    plain(f"{name}.down{th}", add_to_x(T, gate), mods=0 if mods and th < len(THIRDS) - 1 else None,
                          squares=(squares, T) if th == len(THIRDS) - 1 else None)

            def add_to_x(T, gate):
                def evac(u, c):
                    g = gate(c)
                    for i, (col_, at) in enumerate(zip(g, (T - SEQ, 0))):
                        x = chunk(xs, c, part=slice(BOTH - T + at, BOTH - T + at + SEQ))
                        ins = v.scalar_tensor_tensor(out=x, in0=bank(u, SEQ, at), scalar=col_, in1=x, op0=ALU.mult, op1=ALU.add)
                    ins.then_inc(evacuated, 1)
                return evac

            def gates_of(sets, s):
                return lambda c: [gcol[:, bass.ds(24 * k + 8 * s + c, 1)] for k in sets]

            def norm_var(s, T):
                dve.wait_ge(sq_summed, s + 1)
                v.tensor_scalar(rs[:, 0:T], bank(4, T), 1.0 / D, EPS, ALU.mult, ALU.add).then_inc(var_ready, 1)
                dve.wait_ge(var_ready, 2 * s + 1)
                v.reciprocal(rv_[:, 0:T], rs[:, 0:T]).then_inc(var_ready, 1)

            def norm_apply(s, T, gain, shift):
                dve.wait_ge(rstd_ready, s + 1)

                def lo_of(k):
                    dve.wait_ge(nhi_ready, KD * s + k + 1)
                    for b, at in zip(shift(k), (T - SEQ, 0)):
                        part = slice(BOTH - T + at, BOTH - T + at + SEQ)
                        f = nt[:, (k % 2) * BOTH + at:(k % 2) * BOTH + at + SEQ]
                        ins = v.scalar_tensor_tensor(out=chunk(nlo, k, part=part), in0=f, scalar=b,
                                                     in1=chunk(nhi, k, part=part).bitcast(F32), op0=ALU.add, op1=ALU.subtract)
                    ins.then_inc(nlo_ready, 1)

                for k in range(KD):
                    if k >= 2:
                        dve.wait_ge(nlo_ready, KD * s + k - 1)
                    for a, at in zip(gain(k), (T - SEQ, 0)):
                        ins = v.scalar_tensor_tensor(out=nt[:, (k % 2) * BOTH + at:(k % 2) * BOTH + at + SEQ],
                                                     in0=chunk(xs, k, part=slice(BOTH - T + at, BOTH - T + at + SEQ)), scalar=a,
                                                     in1=rstd[:, at:at + SEQ], op0=ALU.mult, op1=ALU.mult)
                    ins.then_inc(nt_ready, 1)
                    if k:
                        lo_of(k - 1)
                lo_of(KD - 1)

            def mod_gain(sets, s):
                return lambda k: [acol[:, 24 * c + 8 * s + k:24 * c + 8 * s + k + 1] for c in sets]

            def mod_shift(sets, s):
                return lambda k: [modc[:, 72 * c + 24 * s + k:72 * c + 24 * s + k + 1] for c in sets]

            def vec_gain(name):
                return lambda k: [col(name, k)]

            def no_shift(k):
                return [zcol[:, 0:1]]

            def take_mod(sets, l, b0, b1, last=True):
                for i, (k, cond) in enumerate(sets):
                    ins = v.tensor_tensor(modc[:, 72 * k + b0:72 * k + b1], modps[:, 72 * l + b0:72 * l + b1, cond],
                                          cols[:, B_MOD + 72 * l + b0:B_MOD + 72 * l + b1], ALU.add)
                    if i == len(sets) - 1:
                        ins.then_inc(mod_copied, 1)
                    else:
                        link(ins)

            def gain_cols(sets, l, s):
                for k, _ in sets:
                    link(v.scalar_tensor_tensor(out=acol[:, 24 * k + 8 * s:24 * k + 8 * s + 8],
                                                in0=modc[:, 72 * k + 24 * s + 8:72 * k + 24 * s + 16], scalar=1.0,
                                                in1=cols[:, VEC["norm_g"] + 24 * l + 8 * s:VEC["norm_g"] + 24 * l + 8 * s + 8],
                                                op0=ALU.add, op1=ALU.mult))

            def gate_cols(sets, s):
                for k, _ in sets:
                    link(v.tensor_scalar(gcol[:, 24 * k + 8 * s:24 * k + 8 * s + 8], modc[:, 72 * k + 24 * s + 16:72 * k + 24 * s + 24],
                                         1.0 if s == 1 else 0.5, None, ALU.mult))

            XC = ((0, 0), (1, 1))

            link(v.memset(zcol[:, :], 0.0))
            v.memset(epsc[:, :], EPS).then_inc(eps_ready, 1)
            dve.wait_ge(vec_turned, 1)
            v.tensor_copy(cols[:, :], bank(6, N_COLS)).then_inc(cols_ready, 1)
            for i in range(8):
                dve.wait_ge(x_rows_turned, i + 1)
                half, tc = i % 2, i // 2
                dst = xs[:, :].rearrange("p (k n) -> p k n", k=KD)[:, 4 * half:4 * half + 4, tc * P:(tc + 1) * P]
                v.tensor_copy(dst, bank(i % 4).rearrange("p (k n) -> p k n", k=4)).then_inc(x_turned, 1)
            for k in range(1, KD - 1):
                add_square(0, BOTH, k)
            norm_var(0, BOTH)
            for u in range(U):
                split_lo(0, u, KD)
            dve.wait_ge(mod_first_done, MOD_NEED)
            dve.wait_ge(cols_ready, 1)
            take_mod(XC, 0, 0, 16)
            dve.wait_ge(mod_copied, 1)
            gain_cols(XC, 0, 0)
            norm_apply(0, BOTH, mod_gain((0, 1), 0), mod_shift((0, 1), 0))
            dve.wait_ge(mod_first_done, MOD_FIRST)
            take_mod(XC, 0, 16, 24)
            dve.wait_ge(mod_copied, 2)
            gate_cols(XC, 0)
            ffn("l0f1", BOTH, gates_of((0, 1), 0), 1, mods=True)
            norm_var(1, BOTH)
            dve.wait_ge(mod_summed, MOD_JOBS - MOD_HELD)
            take_mod(XC, 0, 24, 40)
            dve.wait_ge(mod_copied, 3)
            take_mod(((0, 0),), 0, 40, 72)
            dve.wait_ge(mod_copied, 4)
            gain_cols(XC, 0, 1)
            norm_apply(1, BOTH, mod_gain((0, 1), 1), mod_shift((0, 1), 1))
            gate_cols(((0, 0),), 1)
            gain_cols(((0, 0),), 0, 2)
            gate_cols(((0, 0),), 2)
            def norm(s, T, gain, shift):
                norm_var(s, T)
                norm_apply(s, T, gain, shift)

            def keep(dst_of, width):
                def evac(u, c):
                    v.tensor_copy(dst_of(c), bank(u, width)).then_inc(evacuated, 1)
                return evac

            plain("k", keep(lambda c: qk[:, bass.ds(c * QKW + SEQ, BOTH)], BOTH), mods=MOD_SHIFT)
            dve.wait_ge(mod_summed, MOD_JOBS)
            take_mod(((2, 0),), 1, 0, 72)
            dve.wait_ge(mod_copied, 5)
            for s in range(3):
                gain_cols(((2, 0),), 1, s)
                gate_cols(((2, 0),), s)

            plain("q", keep(lambda c: qk[:, bass.ds(c * QKW, SEQ)], SEQ))

            def keep_v(p, c):
                for h in range(2):
                    dst = vv[:, 2 * h * D:2 * (h + 1) * D].rearrange("p (t n) -> p t n", t=2)[:, :, c * 2 * P:(c + 1) * 2 * P]
                    v.tensor_copy(dst, bank(2 * p + h).rearrange("p (t n) -> p t n", t=2)).then_inc(evacuated, 1)

            for i, name in enumerate(("q_g", "k_g")):
                v.tensor_scalar(rotg[:, i * P:(i + 1) * P], const("rot16"), col(name), None, ALU.mult).then_inc(S["rotg_ready"], 1)
            dve.wait_ge(S["qk_summed"], 2 * HEADS)
            v.tensor_scalar(tq[0:2 * HEADS, :], ps[0:2 * HEADS, 5 * 512:5 * 512 + QKW], 1.0 / 64, EPS, ALU.mult, ALU.add).then_inc(S["qk_var"], 1)
            dve.wait_ge(S["qk_var"], 1)
            v.reciprocal(tr[0:2 * HEADS, :], tq[0:2 * HEADS, :]).then_inc(S["qk_var"], 1)

            def qk_head(h):
                q_ = qk[:, h * QKW:h * QKW + SEQ]
                kc = qk[:, h * QKW + SEQ:h * QKW + 2 * SEQ]
                kx = qk[:, h * QKW + 2 * SEQ:(h + 1) * QKW]
                dve.wait_ge(S["qk_ss"], h + 1)
                if h:
                    dve.wait_ge(S["qk_done"], h)
                sin2 = const("sinA").unsqueeze(1).to_broadcast([P, 2, SEQ])
                v.tensor_tensor(nt[:, 0:512].rearrange("p (a n) -> p a n", a=2), bank(4).rearrange("p (a n) -> p a n", a=2), sin2, ALU.mult)
                v.scalar_tensor_tensor(out=nt[:, 512:768], in0=q_, scalar=col("q_g"), in1=const("cosA"), op0=ALU.mult, op1=ALU.mult)
                link(v.scalar_tensor_tensor(out=nt[:, 768:1024], in0=kx, scalar=col("k_g"), in1=const("cosA"), op0=ALU.mult, op1=ALU.mult))
                link(v.tensor_tensor(nt[:, 0:512], nt[:, 0:512], nt[:, 512:1024], ALU.add))
                v.tensor_tensor(q_, nt[:, 0:256], bank(6, SEQ, SEQ), ALU.mult)
                v.tensor_tensor(kx, nt[:, 256:512], bank(7, SEQ, SEQ), ALU.mult)
                v.scalar_tensor_tensor(out=kc, in0=kc, scalar=col("k_g"), in1=bank(7, SEQ), op0=ALU.mult, op1=ALU.mult).then_inc(S["qk_done"], 1)

            def qk_heads(c):
                for h in ((0,), (1, 2), (3, 4), (5, 6, 7))[c]:
                    qk_head(h)

            rows_pairs("v", keep_v, before=qk_heads)

            dve.wait_ge(S["in_lam"], 64)
            lam2 = lamv[:, :].rearrange("p (a b n) -> p a b n", a=2, b=2)
            link(v.tensor_tensor(lamt[:, :].rearrange("p (a n) -> p a n", a=2), lam2[:, :, 0, :], lam2[:, :, 1, :], ALU.mult))
            v.reduce_sum(lams[:, 0:2], lamt[:, :].rearrange("p (a n) -> p a n", a=2), AX_X).then_inc(S["lam_sum"], 1)
            dve.wait_ge(S["lam_exp"], 1)
            link(v.tensor_tensor(lams[:, 4:5], lams[:, 3:4], lams[:, 2:3], ALU.subtract))
            link(v.tensor_scalar(lams[:, 5:6], lams[:, 4:5], -LAM_INIT, None, ALU.add))
            def rows_max(h):
                for ti in range(4):
                    dve.wait_ge(S["s_done"], 4 * h + ti + 1)
                    if h:
                        dve.wait_ge(S["exp_done"], 4 * h - 3 + ti)
                    link(v.reduce_max(gqk4[:, ti:ti + 1], bank(4 + ti), AX_X))
                    v.tensor_scalar(mx[:, ti:ti + 1], gqk4[:, ti:ti + 1], -0.125, None, ALU.mult).then_inc(S["max_done"], 1)

            rows_max(0)
            for h in range(HEADS):
                dve.wait_ge(S["exp_done"], 4 * h + 4)
                link(v.reciprocal(rinv[:, :], rsum[:, :]))
                link(v.tensor_scalar(rsum2[:, :], rinv[:, :], lams[:, 5:6], None, ALU.mult))
                for q in range(2):
                    e0 = ee[:, 2 * q * BOTH:(2 * q + 1) * BOTH]
                    e1 = ee[:, (2 * q + 1) * BOTH:(2 * q + 2) * BOTH]
                    link(v.tensor_scalar(e0, e0, rinv[:, 2 * q:2 * q + 1], None, ALU.mult))
                    v.scalar_tensor_tensor(out=e0, in0=e1, scalar=rsum2[:, 2 * q + 1:2 * q + 2], in1=e0, op0=ALU.mult, op1=ALU.add).then_inc(S["a_done"], 1)
                if h + 1 < HEADS:
                    rows_max(h + 1)
                dve.wait_ge(S["o_done"], h + 1)
                v.tensor_copy(oT[:, h * SEQ:(h + 1) * SEQ], bank(2 + h % 2, SEQ)).then_inc(S["o_copied"], 1)
            link(v.tensor_scalar(gqk[:, 0:1], col("sub_g"), 1.0 - LAM_INIT, None, ALU.mult))
            dve.wait_ge(S["on_ss"], 1)
            v.tensor_scalar(tq[0:HEADS, 0:SEQ], bank(4, SEQ, parts=slice(0, HEADS)), 1.0 / P, EPS, ALU.mult, ALU.add).then_inc(S["on_var"], 1)
            dve.wait_ge(S["on_var"], 1)
            v.reciprocal(tr[0:HEADS, 0:SEQ], tq[0:HEADS, 0:SEQ]).then_inc(S["on_var"], 1)

            def o_lo(h):
                dve.wait_ge(S["on_hi"], h + 1)
                v.tensor_tensor(chunk(nlo, h, part=X_COLS), oT[:, h * SEQ:(h + 1) * SEQ], chunk(nhi, h, part=X_COLS).bitcast(F32), ALU.subtract).then_inc(S["on_lo"], 1)

            for h in range(HEADS):
                o = oT[:, h * SEQ:(h + 1) * SEQ]
                dve.wait_ge(S["on_spread"], h + 1)
                v.scalar_tensor_tensor(out=o, in0=o, scalar=gqk[:, 0:1], in1=bank(4 + h % 4, SEQ), op0=ALU.mult, op1=ALU.mult).then_inc(S["on_full"], 1)
                if h:
                    o_lo(h - 1)
            o_lo(HEADS - 1)

            plain("wo", add_to_x(SEQ, gates_of((0,), 1)), squares=(2, SEQ))
            norm(2, SEQ, mod_gain((0,), 2), mod_shift((0,), 2))
            ffn("l0f2", SEQ, gates_of((0,), 2), 3)
            norm(3, SEQ, mod_gain((2,), 0), mod_shift((2,), 0))
            ffn("l1f1", SEQ, gates_of((2,), 0), 4)

            norm(4, SEQ, mod_gain((2,), 1), mod_shift((2,), 1))
            for c in range(KD):
                dve.wait_ge(S["f_hi"], c + 1)
                v.tensor_tensor(chunk(nlo, c, part=X_COLS), bank(4 + c % 4, SEQ), chunk(nhi, c, part=X_COLS).bitcast(F32), ALU.subtract).then_inc(S["f_lo"], 1)
            plain("fourier", add_to_x(SEQ, gates_of((2,), 1)), squares=(5, SEQ))
            norm(5, SEQ, mod_gain((2,), 2), mod_shift((2,), 2))
            ffn("l1f2", SEQ, gates_of((2,), 2), 6)

            norm(6, SEQ, vec_gain("norm_mix"), no_shift)

            def chunks_of(x):
                return keep(lambda c: x[:, bass.ds(c * SEQ, SEQ)], SEQ)

            def rows_of(x, width):
                def evac(p, c):
                    dst = x[:, :].rearrange("p (t n) -> p t n", t=2)[:, :, c * 2 * P:(c + 1) * 2 * P]
                    v.tensor_copy(dst, bank(2 * p).rearrange("p (t n) -> p t n", t=2)).then_inc(evacuated, 2)
                return evac

            def gate_in(u, c):
                v.tensor_scalar(gates[:, bass.ds(c * SEQ, SEQ)], bank(u, SEQ), cols[:, bass.ds(c + VEC["b_gate"], 1)], None, ALU.add).then_inc(evacuated, 1)

            plain("sbq", chunks_of(sbq))
            plain("sbk", chunks_of(sbk))
            rows_pairs("sbv", rows_of(sbv, 512))
            plain("rq", chunks_of(rq))
            plain("rk", chunks_of(rk))
            rows_pairs("rv", rows_of(rvt, D))
            plain("rg", chunks_of(rg))
            plain("gates", gate_in)

            keep2 = const("keep").unsqueeze(1).to_broadcast([P, 2, DEC_W])
            for c in range(4):
                z = two(2 * (c % 2))
                dve.wait_ge(S["sp_done"], c + 1)
                link(v.tensor_scalar(wk3(2), z, 0.125, None, ALU.mult))
                link(v.scalar_tensor_tensor(out=wk(3), in0=wk(2), scalar=0.0, in1=wk(0), op0=ALU.max, op1=ALU.add))
                v.tensor_tensor(wk3(4), wk3(3), keep2, ALU.mult).then_inc(S["lk_done"], 1)
                link(v.tensor_tensor(wk(2), wk(2), wk(3), ALU.subtract))
                dve.wait_ge(S["suf_done"], c + 1)
                v.tensor_tensor(wk3(1), wk3(2), two(4 + 2 * (c % 2)), ALU.subtract).then_inc(S["arg_done"], 1)
                dve.wait_ge(S["w_exp"], c + 1)
                v.tensor_tensor(wk3(3), wk3(0), keep2, ALU.mult).then_inc(S["lk_done"], 1)
                dve.wait_ge(S["sb_hi"], c + 1)
                v.tensor_tensor(chunk(nlo, c, part=slice(0, SEQ)), bank(2 * (c % 2), SEQ), chunk(nhi, c, part=slice(0, SEQ)).bitcast(F32), ALU.subtract).then_inc(S["w_done"], 1)

            for i in range(8):
                x = (rq if i < 4 else rk)[:, (i % 4) * SEQ:(i % 4 + 1) * SEQ]
                dve.wait_ge(S["rot_ps"], i + 1)
                if i:
                    dve.wait_ge(S["rot_done"], i)
                link(v.tensor_tensor(nt[:, 0:SEQ], bank(4 + i % 4, SEQ), const("sinB"), ALU.mult))
                link(v.tensor_tensor(nt[:, SEQ:2 * SEQ], x, const("cosB"), ALU.mult))
                v.tensor_tensor(x, nt[:, 0:SEQ], nt[:, SEQ:2 * SEQ], ALU.add).then_inc(S["rot_done"], 1)
            for h in range(HEADS):
                dve.wait_ge(S["rs_done"], h + 1)
                dve.wait_ge(S[f"in_dec{h % 2}"], 16 * (h // 2 + 1))
                if h >= 2:
                    dve.wait_ge(S["ro_done"], h - 1)
                v.scalar_tensor_tensor(out=wk(0)[:, (h % 2) * DEC_W:(h % 2 + 1) * DEC_W], in0=bank(h % 2, DEC_W), scalar=0.125,
                                       in1=decay[:, (h % 2) * DEC_W:(h % 2 + 1) * DEC_W], op0=ALU.mult, op1=ALU.mult).then_inc(S["rw_done"], 1)
                if h:
                    dve.wait_ge(S["ro_done"], h)
                    v.tensor_copy(yr[:, (h - 1) * SEQ:h * SEQ], bank(2 + (h - 1) % 2, SEQ)).then_inc(S["ro_full"], 1)
            dve.wait_ge(S["ro_done"], HEADS)
            v.tensor_copy(yr[:, 7 * SEQ:8 * SEQ], bank(3, SEQ)).then_inc(S["ro_full"], 1)
            dve.wait_ge(S["ro_ss"], 1)
            v.tensor_scalar(rvar[:, :], ps[:, 4 * 512:8 * 512], 1.0 / P, EPS, ALU.mult, ALU.add).then_inc(S["ro_var"], 1)
            dve.wait_ge(S["ro_var"], 1)
            v.reciprocal(rvt[:, :], rvar[:, :]).then_inc(S["ro_var"], 1)
            dve.wait_ge(S["ro_rstd"], 1)
            dve.wait_ge(S["rg_done"], 1)
            for h in range(HEADS):
                y = yr[:, h * SEQ:(h + 1) * SEQ]
                link(v.scalar_tensor_tensor(out=y, in0=y, scalar=col("ret_norm", h), in1=rvar[:, h * SEQ:(h + 1) * SEQ], op0=ALU.mult, op1=ALU.mult))
                v.tensor_tensor(y, y, rg[:, h * SEQ:(h + 1) * SEQ], ALU.mult).then_inc(S["mix_full"], 1)
                dve.wait_ge(S["ro_hi"], h + 1)
                v.tensor_tensor(chunk(nlo, h, part=X_COLS), y, chunk(nhi, h, part=X_COLS).bitcast(F32), ALU.subtract).then_inc(S["ro_lo"], 1)

            def gated(first):
                def evac(u, c):
                    g = gates[:, (first + c) * SEQ:(first + c + 1) * SEQ]
                    v.tensor_tensor(g, bank(u, SEQ), g, ALU.mult).then_inc(evacuated, 1)
                return evac

            dve.wait_ge(S["gate_done"], 1)
            plain("sbout", gated(0))
            plain("retout", gated(KD))
            dve.wait_ge(evacuated, U * ph["wout"][0])
            for c in range(KD):
                g = gates[:, c * SEQ:(c + 1) * SEQ]
                v.tensor_tensor(g, g, gates[:, (KD + c) * SEQ:(KD + c + 1) * SEQ], ALU.add).then_inc(S["gate_raw"], 1)
                dve.wait_ge(S["mix_hi"], c + 1)
                v.tensor_tensor(chunk(nlo, c, part=X_COLS), g, chunk(nhi, c, part=X_COLS).bitcast(F32), ALU.subtract).then_inc(S["mix_lo"], 1)
            plain("wout", add_to_x(SEQ, lambda c: [1.0]), squares=(7, SEQ))

            norm(7, SEQ, vec_gain("norm_ffn"), no_shift)
            dve.wait_ge(S["in_rbias"], 32)
            for h in range(2):
                def best(x, out_, n):
                    link(v.reduce_max(n, x, AX_X))
                    link(v.tensor_scalar(tn(h, "eq", 4), x, n, None, ALU.is_ge))
                    link(v.tensor_tensor(tn(h, "eq", 4), tn(h, "eq", 4), const("first"), ALU.mult))
                    link(v.reduce_max(tn(h, "m", 1), tn(h, "eq", 4), AX_X))
                    link(v.tensor_scalar(out_, tn(h, "eq", 4), tn(h, "m", 1), None, ALU.is_ge))

                l = lg[:, 20 * h:20 * h + 20]
                dve.wait_ge(S["rt_ps"], h + 1)
                link(v.tensor_tensor(l, bank(h, 20), rbias[:, :], ALU.add))
                best(l[:, 0:4], tn(h, "group", 4), tn(h, "v", 1))
                v.tensor_scalar(tn(h, "negm", 1), tn(h, "v", 1), -1.0, None, ALU.mult).then_inc(S["rt_max"], 1)
                dve.wait_ge(S["rt_exp"], h + 1)
                link(v.reduce_max(tn(h, "pg", 1), tn(h, "e", 4), AX_X))
                link(v.reciprocal(tn(h, "r", 1), tn(h, "sum", 1)))
                link(v.tensor_tensor(tn(h, "pg", 1), tn(h, "pg", 1), tn(h, "r", 1), ALU.mult))
                link(v.tensor_scalar(tn(h, "in", 4), l[:, 4:8], tn(h, "group", 4)[:, 0:1], None, ALU.mult))
                for g in range(1, 4):
                    link(v.scalar_tensor_tensor(out=tn(h, "in", 4), in0=l[:, 4 + 4 * g:8 + 4 * g], scalar=tn(h, "group", 4)[:, g:g + 1],
                                                in1=tn(h, "in", 4), op0=ALU.mult, op1=ALU.add))
                best(tn(h, "in", 4), tn(h, "one", 4), tn(h, "v", 1))
                link(v.scalar_tensor_tensor(out=tn(h, "in", 4), in0=tn(h, "one", 4), scalar=-BIG, in1=tn(h, "in", 4), op0=ALU.mult, op1=ALU.add))
                best(tn(h, "in", 4), tn(h, "two", 4), tn(h, "v2", 1))
                v.tensor_tensor(tn(h, "d", 1), tn(h, "v2", 1), tn(h, "v", 1), ALU.subtract).then_inc(S["rt_e2in"], 1)
                dve.wait_ge(S["rt_e2"], h + 1)
                link(v.tensor_scalar(tn(h, "r", 1), tn(h, "e2", 1), 1.0, None, ALU.add))
                link(v.reciprocal(tn(h, "sum", 1), tn(h, "r", 1)))
                link(v.tensor_tensor(tn(h, "g1", 1), tn(h, "sum", 1), tn(h, "pg", 1), ALU.mult))
                link(v.tensor_tensor(tn(h, "g2", 1), tn(h, "g1", 1), tn(h, "e2", 1), ALU.mult))
                link(v.tensor_scalar(tn(h, "one", 4), tn(h, "one", 4), tn(h, "g1", 1), None, ALU.mult))
                link(v.scalar_tensor_tensor(out=tn(h, "one", 4), in0=tn(h, "two", 4), scalar=tn(h, "g2", 1), in1=tn(h, "one", 4), op0=ALU.mult, op1=ALU.add))
                for g in range(4):
                    ins = v.tensor_scalar(tn(h, "comb", 16)[:, 4 * g:4 * g + 4], tn(h, "one", 4), tn(h, "group", 4)[:, g:g + 1], None, ALU.mult)
                ins.then_inc(S["rt_comb"], 1)
            dve.wait_ge(S["rt_turned"], 2)
            v.tensor_copy(cmbT[:, :], bank(2, SEQ, parts=slice(0, N_EXPERTS))).then_inc(S["rt_copied"], 1)
            dve.wait_ge(S["cmb_done"], N_EXPERTS // 2)

            r0 = ph["moe"][0]
            evac = add_to_x(SEQ, lambda c: [1.0])

            def expert(e, last):
                for i in range(2):
                    n_k = KD if i == 0 else 4
                    for p in range(2):
                        hidden_pair(4 * e + (r0 + i), p, SEQ, 4 * e + (moe_h0 + 2 * i + p), 2 * i + p,
                                    lambda: split_lo(4 * e + (r0 + i + 1), 2 * p, n_k),
                                    lambda: split_lo(4 * e + (r0 + i + 1), 2 * p + 1, n_k), weigh=cmb[:, bass.ds(e * SEQ, SEQ)])
                for i in range(2):
                    for u in range(U):
                        dve.wait_ge(slab_done, 16 * e + (U * (r0 + 2 + i) + u + 1))
                        evac(u, U * i + u)
                        if last and U * i + u >= 2:
                            add_square(8, SEQ, U * i + u - 1)
                        if i == 0 or not last:
                            split_lo(4 * e + (r0 + 2 + i + 1), u, 4 if i == 0 else KD)
            run(dve, N_EXPERTS, expert)

            norm_var(8, SEQ)
            dve.wait_ge(rstd_ready, 9)
            for k in range(KD):
                f = nt[:, (k % 2) * BOTH:(k % 2) * BOTH + SEQ]
                if k >= 2:
                    dve.wait_ge(fin_turned, k - 1)
                v.scalar_tensor_tensor(out=f, in0=chunk(xs, k, part=X_COLS), scalar=col("norm_final", k), in1=rstd[:, 0:SEQ],
                                       op0=ALU.mult, op1=ALU.mult).then_inc(nt_ready, 1)
                if k:
                    fin_copy(dve, k - 1)
            fin_copy(dve, KD - 1)

        @block.tensor
        def _(pe):
            def w_hi(u, k):
                return hi[:, u * SLOT + k * P:u * SLOT + (k + 1) * P]

            def w_lo(u, k):
                return lo[:, u * SLOT + k * P:u * SLOT + (k + 1) * P]

            def ready(r, u, first=False):
                pe.wait_ge(lo_ready, U * r + u + 1)
                if not first:
                    pe.wait_ge(evacuated, U * (r - 1) + u + 1)

            def slab(r, u, nk, T, xh, xl, part, first=False):
                ready(r, u, first)
                for k in range(nk):
                    h_, l_ = chunk(xh, k, part=part), chunk(xl, k, part=part)
                    pe.matmul(bank(u, T), w_hi(u, k), h_, start=(k == 0), stop=False)
                    pe.matmul(bank(u, T), w_hi(u, k), l_, start=False, stop=False)
                    ins = pe.matmul(bank(u, T), w_lo(u, k), h_, start=False, stop=(k == nk - 1))
                ins.then_inc(slab_done, 1)

            def first_pair(r, nk, T, xh, xl, part, chunk_ready, first=False):
                for u in range(2):
                    ready(r, u, first)
                for k in range(nk):
                    chunk_ready(k)
                    h_, l_ = chunk(xh, k, part=part), chunk(xl, k, part=part)
                    for u in range(2):
                        pe.matmul(bank(u, T), w_hi(u, k), h_, start=(k == 0), stop=False)
                        pe.matmul(bank(u, T), w_hi(u, k), l_, start=False, stop=False)
                        ins = pe.matmul(bank(u, T), w_lo(u, k), h_, start=False, stop=(k == nk - 1))
                        if k == nk - 1:
                            ins.then_inc(slab_done, 1)

            def rows_pairs(name, T, side=None):
                r0, rounds, _ = ph[name]

                def two_slabs(x, p, k):
                    return x[:, 2 * p * SLOT:2 * (p + 1) * SLOT].rearrange("p (u n) -> p u n", u=2)[:, :, k * P:(k + 1) * P]

                for i in range(rounds):
                    for p in range(2):
                        ready(r0 + i, 2 * p + 1)
                        for b in range(T // P):
                            part = slice(BOTH - T + b * P, BOTH - T + (b + 1) * P)
                            o = bank(2 * p + b // 2, 2 * P, 2 * P * (b % 2)).rearrange("p (u n) -> p u n", u=2)
                            for k in range(KD):
                                h_, l_ = chunk(nhi, k, part=part), chunk(nlo, k, part=part)
                                pe.matmul(o, h_, two_slabs(hi, p, k), start=(k == 0), stop=False)
                                pe.matmul(o, h_, two_slabs(lo, p, k), start=False, stop=False)
                                ins = pe.matmul(o, l_, two_slabs(hi, p, k), start=False, stop=(k == KD - 1))
                            if b == T // P - 1:
                                ins.then_inc(slab_done, 2)
                            if side:
                                side(2 * i + p, b)

            def rounds_of(i0, i1, body):
                if i1 - i0 > 1:
                    with pe.Fori(i0, i1) as i:
                        body(i)
                elif i1 > i0:
                    body(i0)

            def plain(name, T=SEQ, xh=nhi, xl=nlo, part=None, squares=None, chunk_ready=None, side=None):
                r0, rounds, nk = ph[name]

                def body(i, first=False):
                    for u in range(U):
                        if chunk_ready and first and u < 2:
                            if u == 0:
                                first_pair(r0, nk, T, xh, xl, part or tok(T), chunk_ready)
                        else:
                            slab(i + r0, u, nk, T, xh, xl, part or tok(T))
                        if side:
                            side(U * i + u)
                if side:
                    for i in range(rounds):
                        body(i, i == 0)
                elif chunk_ready:
                    body(0, True)
                    rounds_of(1, rounds, body)
                else:
                    rounds_of(0, rounds, body)
                if squares:
                    norm_sum(*squares)

            def mod_first_rows(m):
                pe.wait_ge(mod_early_landed[m], 16)
                for k in range(KD):
                    ins = pe.matmul(bank(5 + m % 2, MOD_W, parts=slice(0, 2)), csil[:, :].rearrange("p (c k) -> p k c", c=2)[:, k, :],
                                    mod_early[m][:, k * MOD_W:(k + 1) * MOD_W], start=(k == 0), stop=(k == KD - 1))
                ins.then_inc(mod_rows, 1)

            def mod_first_turn(m):
                pe.wait_ge(mod_rows_copied, m + 1)
                if m == MOD_NEED:
                    pe.wait_ge(mod_copied, 1)
                for b in range(2):
                    at = (m % 2) * MOD_W + b * P
                    ins = pe.matmul(bank(7, 2, 4 * m + 2 * b), mrow[:, at:at + P], const("ident", 2)[0:2, :], start=True, stop=True)
                ins.then_inc(mod_first_done, 1)

            def mod_sum(r, u, lowest, jobs=range(MOD_JOBS - MOD_HELD)):
                n = U * lowest + u - MOD_LAG
                if n not in jobs:
                    return
                a = (u - MOD_LAG) % U
                if n == 0:
                    pe.wait_ge(mod_copied, 2)
                both = n < 2 * MOD_BOTH
                pe.wait_ge(mod_jobs, U * r + (u - MOD_LAG + 1 + (1 if both and n % 2 == 0 else 0)))
                if both:
                    s = (u - MOD_LAG) % 2
                    at = 2 * U * r + (2 * (u - MOD_LAG - s) + 4 * MOD_FIRST + s)
                else:
                    at = 4 * U * r + 4 * (u - MOD_LAG + MOD_FIRST - MOD_BOTH)
                for b in range(2):
                    w = macc[:, a * MOD_W + b * P:a * MOD_W + (b + 1) * P]
                    ins = pe.matmul(ps[:, bass.ds(at + (7 * 512 + 2 * b), 1)], w, const("ones", 1), start=True, stop=True)
                ins.then_inc(mod_summed, 1)

            h_at = [0]

            def ffn(name, T, norm, mods=False, squares=None):
                for th, size in enumerate(THIRDS):
                    r0, rounds, nk = ph[f"{name}.up{th}"]

                    def up(i, lowest=0, first=False):
                        for u in range(U):
                            start = isinstance(i, int) and r0 + i == 0
                            if first and u < 2:
                                if u == 0:
                                    first_pair(r0, nk, T, nhi, nlo, tok(T), normed(norm), start)
                            else:
                                slab(i + r0, u, nk, T, nhi, nlo, tok(T), start)
                            if mods:
                                mod_sum(i + r0, u, r0 + lowest)
                    if th == 0:
                        up(0, 0, True)
                        rounds_of(1, rounds, lambda i: up(i, 1))
                    elif mods and th == 1:
                        for i in range(rounds):
                            up(i, i)
                    else:
                        rounds_of(0, rounds, up)
                    r0, rounds, nk = ph[f"{name}.down{th}"]
                    for i in range(rounds):
                        for u in range(U):
                            c = U * i + u
                            if c < 2:
                                if c == 0:
                                    first_pair(r0, nk, T, hhi, hlo, tok(T), lambda k: pe.wait_ge(hlo_ready, h_at[0] + k + 1))
                            else:
                                slab(r0 + i, u, nk, T, hhi, hlo, tok(T))
                            if mods:
                                mod_sum(r0 + i, u, r0 + i)
                    h_at[0] += size
                if squares:
                    norm_sum(*squares)

            def norm_sum(s, T):
                pe.wait_ge(sq_used, (KD - 1) * (s + 1))
                pe.matmul(bank(4, T), const("ones"), sqsum[:, 0:T], start=True, stop=False)
                pe.wait_ge(sq_ready, KD * (s + 1))
                last = (KD - 1) % 2 * BOTH
                pe.matmul(bank(4, T), const("ones"), sq[:, last:last + T], start=False, stop=True).then_inc(sq_summed, 1)

            def normed(s):
                return lambda k: pe.wait_ge(nlo_ready, KD * s + k + 1)

            pe.wait_ge(in_vec, 16 * N_VEC_DMAS)
            pe.wait_ge(in_const, 16)
            pe.transpose(bank(6, N_VEC), vrow[0:N_VEC, 0:P], const("ident")[0:N_VEC, 0:N_VEC])
            for l in range(2):
                ins = pe.transpose(bank(6, 72, N_VEC + 72 * l), vrow[0:72, (1 + l) * P:(2 + l) * P], const("ident")[0:72, 0:72])
            ins.then_inc(vec_turned, 1)

            pe.wait_ge(csil_ready, 1)
            pe.wait_ge(in_x, 64)
            for i in range(8):
                half, tc = i % 2, i // 2
                if i >= 4:
                    pe.wait_ge(x_turned, i - 3)
                for k in range(4):
                    at = tc * D + (4 * half + k) * P
                    ins = pe.transpose(bank(i % 4, P, k * P), xraw[:, at:at + P], const("ident"))
                ins.then_inc(x_rows_turned, 1)
            norm_sum(0, BOTH)
            for m0, m1 in ((0, MOD_NEED), (MOD_NEED, MOD_FIRST)):
                mod_first_rows(m0)
                for m in range(m0 + 1, m1):
                    mod_first_rows(m)
                    mod_first_turn(m - 1)
                mod_first_turn(m1 - 1)
            ffn("l0f1", BOTH, 0, mods=True, squares=(1, BOTH))

            def held_sum(c):
                r = ph["k"][0] - MOD_SHIFT + c // U
                mod_sum(r, c % U, r, range(MOD_JOBS - MOD_HELD, MOD_JOBS))

            plain("k", BOTH, chunk_ready=normed(1), side=held_sum)
            for u in range(MOD_LAG):
                held_sum(MOD_HELD + u)
            def qk_sum(part, h):
                pe.wait_ge(S["qk_sq"], qk_sum_at(part, h))
                w = const("half_sums")[:, 2 * HEADS * h:2 * HEADS * (h + 1)]
                if part == "k":
                    o, x = bank(5, parts=slice(0, 2 * HEADS)), sq[:, (h % 2) * BOTH:(h % 2 + 1) * BOTH]
                else:
                    o, x = bank(6, SEQ, parts=slice(0, 2 * HEADS)), nt[:, (h % 2) * SEQ:(h % 2 + 1) * SEQ]
                pe.matmul(o, w, x, start=(h == 0), stop=(h == HEADS - 1)).then_inc(S["qk_summed"], 1)

            def qk_sums(c):
                if c:
                    qk_sum("k", c - 1)
                if c >= 2:
                    qk_sum("q", c - 2)

            plain("q", side=qk_sums)
            qk_sum("k", HEADS - 1)
            qk_sum("q", HEADS - 2)
            qk_sum("q", HEADS - 1)

            def qk_head(h):
                if h == 0:
                    pe.wait_ge(S["rotg_ready"], 2)
                    pe.wait_ge(S["in_halves"], 16)
                    pe.wait_ge(S["qk_rstd"], 1)
                else:
                    pe.wait_ge(S["qk_done"], h)
                rows = half_rows[:, h * P:(h + 1) * P]
                pe.matmul(bank(4, SEQ), rotg[:, 0:P], qk[:, h * QKW:h * QKW + SEQ], start=True, stop=True)
                pe.matmul(bank(4, SEQ, SEQ), rotg[:, P:2 * P], qk[:, h * QKW + 2 * SEQ:(h + 1) * QKW], start=True, stop=True)
                pe.matmul(bank(7, BOTH), rows, tq[0:2 * HEADS, 0:BOTH], start=True, stop=True)
                pe.matmul(bank(6, SEQ, SEQ), rows, tq[0:2 * HEADS, BOTH:QKW], start=True, stop=True).then_inc(S["qk_ss"], 1)

            def qk_heads(c, b):
                at = {2: 0, 4: 1, 6: 2, 8: 3, 10: 4, 12: 5, 14: 6, 15: 7}.get(BOTH // P * c + b)
                if at is not None:
                    qk_head(at)

            rows_pairs("v", BOTH, side=qk_heads)

            pe.wait_ge(S["qk_done"], HEADS)

            def scores(h):
                for ti in range(4):
                    q, c = ti // 2, ti % 2
                    if h:
                        pe.wait_ge(S["exp_done"], 4 * (h - 1) + ti + 1)
                    s = slice(64 * c, 64 * c + 64)
                    pe.matmul(bank(4 + ti), qk[s, h * QKW + q * P:h * QKW + (q + 1) * P], qk[s, h * QKW + SEQ:(h + 1) * QKW],
                              start=True, stop=True).then_inc(S["s_done"], 1)

            scores(0)
            for h in range(HEADS):
                if h + 1 < HEADS:
                    scores(h + 1)
                if h:
                    pe.wait_ge(S["at_copied"], 2 * h)
                for q in range(2):
                    pe.wait_ge(S["a_done"], 2 * h + q + 1)
                    for kc in range(4):
                        ins = pe.transpose(bank(kc // 2, P, (kc % 2) * SEQ + q * P), ee[:, 2 * q * BOTH + kc * P:2 * q * BOTH + (kc + 1) * P], const("ident"))
                ins.then_inc(S["at_done"], 1)
                pe.wait_ge(S["at_copied"], 2 * h + 2)
                if h >= 2:
                    pe.wait_ge(S["o_copied"], h - 1)
                for kc in range(4):
                    ins = pe.matmul(bank(2 + h % 2, SEQ), vv[:, kc * D + h * P:kc * D + (h + 1) * P], aT[:, kc * SEQ:(kc + 1) * SEQ],
                                    start=(kc == 0), stop=(kc == 3))
                ins.then_inc(S["o_done"], 1)
            for h in range(HEADS):
                pe.wait_ge(S["on_sq"], h + 1)
                ins = pe.matmul(bank(4, SEQ, parts=slice(0, HEADS)), const("head_sums")[:, HEADS * h:HEADS * (h + 1)],
                                qk[:, h * QKW:h * QKW + SEQ], start=(h == 0), stop=(h == HEADS - 1))
            ins.then_inc(S["on_ss"], 1)
            pe.wait_ge(S["in_heads"], 16)
            pe.wait_ge(S["on_rstd"], 1)

            def o_spread(h):
                if h >= 4:
                    pe.wait_ge(S["on_full"], h - 3)
                pe.matmul(bank(4 + h % 4, SEQ), head_rows[:, h * P:(h + 1) * P], tq[0:HEADS, 0:SEQ], start=True, stop=True).then_inc(S["on_spread"], 1)

            for h in range(4):
                o_spread(h)

            def o_chunk(k):
                if k + 4 < HEADS:
                    o_spread(k + 4)
                pe.wait_ge(S["on_lo"], k + 1)

            plain("wo", squares=(2, SEQ), chunk_ready=o_chunk)
            ffn("l0f2", SEQ, 2, squares=(3, SEQ))
            ffn("l1f1", SEQ, 3, squares=(4, SEQ))

            pe.wait_ge(nlo_ready, KD * 5)
            pe.wait_ge(S["in_dft"], 16)
            for tc in range(2):
                for g in range(4):
                    i = 4 * tc + g
                    if i >= 4:
                        pe.wait_ge(S["y_copied"], i - 3)
                    for k in range(2):
                        at = (2 * g + k) * SEQ + tc * P
                        ins = pe.matmul(bank(i % 4), xf[:, at:at + P], dft[:, 512 * k:512 * k + 512], start=(k == 0), stop=(k == 1))
                    ins.then_inc(S["y_done"], 1)
            pe.wait_ge(S["y_copied"], 8)
            for c in range(KD):
                if c >= 4:
                    pe.wait_ge(S["f_lo"], c - 3)
                for j in range(4):
                    tc, sine = j // 2, j % 2
                    at = (4 * tc + c // 2) * 512 + SEQ * sine + (c % 2) * P
                    ins = pe.matmul(bank(4 + c % 4, SEQ), yt[:, at:at + P], dft[:, 1024 + 512 * tc + SEQ * sine:1024 + 512 * tc + SEQ * (sine + 1)],
                                    start=(j == 0), stop=(j == 3))
                ins.then_inc(S["f_done"], 1)
            pe.wait_ge(S["f_lo"], KD)
            plain("fourier", squares=(5, SEQ))
            ffn("l1f2", SEQ, 5, squares=(6, SEQ))

            plain("sbq", chunk_ready=normed(6))
            plain("sbk")
            rows_pairs("sbv", SEQ)
            plain("rq")
            plain("rk")
            rows_pairs("rv", SEQ)
            plain("rg")
            plain("gates")
            pe.wait_ge(evacuated, U * ph["sbout"][0])

            def pair_scores(o, k_, q_, j, c):
                s = slice(64 * j, 64 * j + 64)
                pe.matmul(bank(o, SEQ), k_[s, c * SEQ:c * SEQ + P], q_[s, c * SEQ:(c + 1) * SEQ], start=True, stop=True)
                return pe.matmul(bank(o, P, SEQ), k_[s, c * SEQ + P:(c + 1) * SEQ], q_[s, c * SEQ + P:(c + 1) * SEQ], start=True, stop=True)

            for c in range(4):
                b = 2 * (c % 2)
                if c >= 2:
                    pe.wait_ge(S["w_done"], c - 1)
                for j in range(2):
                    ins = pair_scores(b + j, sbk, sbq, j, c)
                ins.then_inc(S["z_done"], 1)
                pe.wait_ge(S["lk_done"], 2 * c + 1)
                for j in range(2):
                    m = wk(4)[:, j * DEC_W:(j + 1) * DEC_W]
                    pe.matmul(bank(4 + b + j, SEQ), const("after"), m[:, 0:SEQ], start=True, stop=False)
                    pe.matmul(bank(4 + b + j, P, P), const("ones"), m[:, SEQ:DEC_W], start=False, stop=True)
                    ins = pe.matmul(bank(4 + b + j, P, SEQ), const("after"), m[:, SEQ:DEC_W], start=True, stop=True)
                ins.then_inc(S["suf_done"], 1)
                pe.wait_ge(S["lk_done"], 2 * c + 2)
                for j in range(2):
                    h = 2 * c + j
                    w = wk(3)[:, j * DEC_W:(j + 1) * DEC_W]
                    o = slice(64 * j, 64 * j + 64)
                    pe.matmul(bank(b, SEQ, parts=o), sbv[:, h * 64:h * 64 + 64], w[:, 0:SEQ], start=True, stop=False)
                    ins = pe.matmul(bank(b, P, P, parts=o), sbv[:, 512 + h * 64:512 + h * 64 + 64], w[:, SEQ:DEC_W], start=False, stop=True)
                ins.then_inc(S["sbo_done"], 1)
            pe.wait_ge(S["w_done"], 4)
            for i in range(8):
                if i >= 4:
                    pe.wait_ge(S["rot_done"], i - 3)
                x = (rq if i < 4 else rk)[:, (i % 4) * SEQ:(i % 4 + 1) * SEQ]
                pe.matmul(bank(4 + i % 4, SEQ), const("rot32"), x, start=True, stop=True).then_inc(S["rot_ps"], 1)
            pe.wait_ge(S["rot_done"], 8)

            def ret_scores(h):
                if h >= 2:
                    pe.wait_ge(S["rw_done"], h - 1)
                pair_scores(h % 2, rk, rq, h % 2, h // 2).then_inc(S["rs_done"], 1)

            ret_scores(0)
            for h in range(HEADS):
                if h + 1 < HEADS:
                    ret_scores(h + 1)
                pe.wait_ge(S["rw_done"], h + 1)
                if h >= 2:
                    pe.wait_ge(S["ro_full"], h - 1)
                w = wk(0)[:, (h % 2) * DEC_W:(h % 2 + 1) * DEC_W]
                pe.matmul(bank(2 + h % 2, SEQ), rvt[:, h * P:(h + 1) * P], w[:, 0:SEQ], start=True, stop=False)
                pe.matmul(bank(2 + h % 2, P, P), rvt[:, D + h * P:D + (h + 1) * P], w[:, SEQ:DEC_W], start=False, stop=True).then_inc(S["ro_done"], 1)
            pe.wait_ge(S["ro_sq"], 1)
            for b in range(4):
                ins = pe.matmul(bank(4 + b), const("ones"), rvt[:, 512 * b:512 * b + 512], start=True, stop=True)
            ins.then_inc(S["ro_ss"], 1)
            plain("sbout", part=slice(0, SEQ))
            pe.wait_ge(S["ro_lo"], HEADS)
            plain("retout")
            pe.wait_ge(S["mix_lo"], KD)
            plain("wout", squares=(7, SEQ))

            pe.wait_ge(nlo_ready, KD * 8)
            pe.wait_ge(S["in_router"], 32)
            for h in range(2):
                for k in range(KD):
                    ins = pe.matmul(bank(h, 20), xr[:, k * SEQ + h * P:k * SEQ + (h + 1) * P], wr[:, 20 * k:20 * k + 20], start=(k == 0), stop=(k == KD - 1))
                ins.then_inc(S["rt_ps"], 1)
            for h in range(2):
                pe.wait_ge(S["rt_comb"], h + 1)
                pe.transpose(bank(2, P, h * P, parts=slice(0, N_EXPERTS)), tn(h, "comb", 16), const("ident")).then_inc(S["rt_turned"], 1)
            pe.wait_ge(S["rt_copied"], 1)
            pe.wait_ge(S["in_sel"], 16)
            for e in range(N_EXPERTS):
                if e >= 8 and e % 2 == 0:
                    pe.wait_ge(S["cmb_done"], e // 2 - 3)
                pe.matmul(bank(4 + e // 2 % 4, SEQ, (e % 2) * SEQ), sel[:, e * P:(e + 1) * P], cmbT[:, :], start=True, stop=True).then_inc(S["cmb_ps"], 1)

            r0 = ph["moe"][0]

            def expert(e, last):
                for i in range(2):
                    for u in range(U):
                        slab(4 * e + (r0 + i), u, KD, SEQ, nhi, nlo, X_COLS)
                first_pair(4 * e + (r0 + 2), 4, SEQ, hhi, hlo, X_COLS, lambda k: pe.wait_ge(hlo_ready, 4 * e + (h_at[0] + k + 1)))
                for i in range(2):
                    for u in range(0 if i else 2, U):
                        slab(4 * e + (r0 + 2 + i), u, 4, SEQ, hhi, hlo, X_COLS)
            run(pe, N_EXPERTS, expert)
            norm_sum(8, SEQ)
            for k in range(KD):
                pe.wait_ge(nt_ready, KD * 8 + k + 1)
                if k >= 4:
                    pe.wait_ge(fin_copied, k - 3)
                f = nt[:, (k % 2) * BOTH:(k % 2) * BOTH + SEQ]
                for h in range(2):
                    ins = pe.transpose(bank(k % 4, P, h * P), f[:, h * P:(h + 1) * P], const("ident"))
                ins.then_inc(fin_turned, 1)


_INS = ["x", "c", "ctx", "c_ctx", "norm_g", "w_mod", "b_mod", "ffn1_w_gu", "ffn1_w_d", "ffn2_w_gu", "ffn2_w_d",
        "attn_w_qkv", "attn_w_o", "attn_q_g", "attn_k_g", "attn_lam_q1", "attn_lam_k1", "attn_lam_q2", "attn_lam_k2",
        "attn_sub_g", "fourier_w", "norm_mix_g_2", "w_in_2", "w_gate_2", "b_gate_2", "w_sb_out_2", "w_ret_out_2",
        "ret_norm_g_2", "w_out_2", "norm_ffn_g_2", "w_group_router_2", "b_group_router_2", "w_expert_router_2",
        "b_expert_router_2", "w_exp_gate_2", "w_exp_up_2", "w_exp_down_2", "norm_final_g_2"]


def kernel(**inputs):
    import numpy as _np
    import concourse.bacc as _bacc
    from concourse import mybir as _mybir
    from concourse.bass_utils import run_bass_kernel_spmd as _run

    nc = _bacc.Bacc("TRN2", target_bir_lowering=False, num_devices=1)
    arrays, tensors = {}, {}
    for name in _INS:
        a = _np.ascontiguousarray(inputs[name])
        arrays[f"in_{name}"] = a
        tensors[name] = nc.dram_tensor(f"in_{name}", a.shape, _mybir.dt.from_np(a.dtype), kind="ExternalInput").ap()
    for name, a in make_constants().items():
        arrays[f"const_{name}"] = a
        tensors[name] = nc.dram_tensor(f"const_{name}", a.shape, _mybir.dt.float32, kind="ExternalInput").ap()
    out = nc.dram_tensor("out_0", (1, SEQ, D), _mybir.dt.float32, kind="ExternalOutput").ap()
    build(nc, tensors, out)
    r = _run(nc, [arrays], core_ids=[0])
    return r.results[0]["out_0"]
```

```python
from contextlib import ExitStack

import numpy as np

import concourse.bass as bass
from concourse import mybir

F32 = mybir.dt.float32
F32R = mybir.dt.float32r
ALU = mybir.AluOpType
ACT = mybir.ActivationFunctionType
AX_X = mybir.AxisListType.X

P = 128
D = 1024
KD = D // P
SEQ = 256
CTX = 256
BOTH = SEQ + CTX
X_COLS = slice(CTX, BOTH)
D_FF = 2816
N_MOD = 9
EPS = 1e-6
U = 4
HEADS = 8
LAM_INIT = 0.2
THIRDS = (8, 8, 6)
MOD_W = 256
MOD_UNITS = N_MOD * D // MOD_W
MOD_NEED = 2 * D // MOD_W
MOD_FIRST = 3 * D // MOD_W
MOD_BOTH = 2 * D // MOD_W
MOD_JOBS = 2 * MOD_UNITS - MOD_FIRST + MOD_BOTH
MOD_HELD = 2 * U
MOD_SHIFT = MOD_HELD // U
MOD_SCALED = 6
MOD_AHEAD = 5
MOD_LAG = 3
N_EXPERTS = 16
EXP_FF = 512
BIG = 1e30

Z_AT = (0, 5, 13, 19)
SOFT_AT = (1, 6, 15, 20)
SUM_AT = (3, 9, 17, 22)
WEIGHT_AT = (4, 11, 18, 23)
SBO_AT = (5, 13, 19, 24)
SBO_LO_AT = (6, 15, 20, 25)
ROT_AT = 25
RET_AT = 29
GATE_AT = 33
ROOT_AT = 40
SILU_AT = 42
DECAY_AT = RET_AT - 2 + 2 * U

DEC_W = SEQ + P

CONST = {}
_at = 0
for _name, _n in (("ident", P), ("ones", P), ("blk64", P), ("rot16", P), ("rot32", P), ("after", P),
                  ("half_sums", 2 * HEADS * HEADS), ("head_sums", HEADS * HEADS), ("keep", DEC_W), ("first", 4), ("cosA", SEQ), ("sinA", SEQ), ("cosB", SEQ), ("sinB", SEQ)):
    CONST[_name] = (_at, _n)
    _at += _n
N_CONST = _at

VEC = {}
_at = 0
for _name, _n in (("c", 8), ("c_ctx", 8), ("norm_g", 48), ("norm_mix", 8), ("norm_ffn", 8), ("norm_final", 8),
                  ("ret_norm", 8), ("b_gate", 16), ("q_g", 1), ("k_g", 1), ("sub_g", 1)):
    VEC[_name] = _at
    _at += _n
N_VEC = _at
B_MOD = N_VEC
N_COLS = N_VEC + 2 * N_MOD * KD
N_VEC_DMAS = 8 + 4 + 1 + 2


def make_constants():
    c = np.zeros((P, N_CONST), np.float32)

    def put(name, a):
        at, n = CONST[name]
        c[:a.shape[0], at:at + n] = a

    i = np.arange(P)
    put("ident", np.eye(P))
    put("ones", np.ones((P, P)))
    put("blk64", (i[:, None] // 64 == i[None, :] // 64).astype(np.float32))
    for name, half in (("rot16", 16), ("rot32", 32)):
        m = np.zeros((P, P))
        for dst in range(P):
            low = dst % (2 * half) < half
            m[dst + half if low else dst - half, dst] = -1.0 if low else 1.0
        put(name, m)
    put("after", (i[:, None] > i[None, :]).astype(np.float32))
    before = (i[:, None] < i[None, :]).astype(np.float32)
    put("keep", np.concatenate([before, np.ones((P, P)), before], 1))
    put("first", np.tile(np.array([4.0, 3.0, 2.0, 1.0]), (P, 1)))
    halves = np.zeros((P, HEADS, 2 * HEADS))
    heads = np.zeros((P, HEADS, HEADS))
    for h in range(HEADS):
        halves[i, h, 2 * h + i // 64] = 1.0
        heads[:, h, h] = 1.0
    put("half_sums", halves.reshape(P, -1))
    put("head_sums", heads.reshape(P, -1))
    t = np.arange(SEQ)
    freq16 = (np.float32(10000.0) ** (-(np.arange(16, dtype=np.float32) / 16))).astype(np.float32)
    j = i % 64
    pos = np.where((j < 32)[:, None], (t // 64)[None, :], (t % 64)[None, :]).astype(np.float32)
    ang = (pos * freq16[j % 16][:, None]).astype(np.float32)
    put("cosA", np.cos(ang.astype(np.float64)))
    put("sinA", np.sin(ang.astype(np.float64)))
    freq32 = (np.float32(10000.0) ** (-(np.arange(32, dtype=np.float32)) / 32)).astype(np.float32)
    ang = (t[None, :].astype(np.float32) * freq32[i % 32][:, None]).astype(np.float32)
    put("cosB", np.cos(ang.astype(np.float64)))
    put("sinB", np.sin(ang.astype(np.float64)))
    gamma = 1.0 - 2.0 ** (-5.0 - np.arange(HEADS, dtype=np.float64))
    s, tt = np.arange(SEQ)[:, None], np.arange(SEQ)[None, :]
    dec = np.where(tt // 64 >= s // 64, 1.0, 0.0)[None] * gamma[:, None, None] ** np.abs(tt - s)[None]
    decay = np.concatenate([dec[:, :P, :], dec[:, P:, P:]], axis=2).transpose(1, 0, 2)
    a = 2 * np.pi * (np.outer(np.arange(256), np.arange(256)) % 256) / 256
    dft_d = (np.concatenate([np.cos(a), np.sin(a)], 1) / 16).reshape(2, P, 512).transpose(1, 0, 2)
    dft_n = (np.stack([np.cos(a), -np.sin(a)], 1) / 16).reshape(2, P, 512).transpose(1, 0, 2)
    sel = np.zeros((N_EXPERTS, N_EXPERTS, P))
    for e in range(N_EXPERTS):
        sel[e, e] = 1.0
    return {
        "consts": c,
        "decay": np.ascontiguousarray(decay.reshape(P, HEADS * DEC_W), np.float32),
        "dft": np.ascontiguousarray(np.concatenate([dft_d.reshape(P, 1024), dft_n.reshape(P, 1024)], 1), np.float32),
        "half_rows": np.ascontiguousarray(halves.transpose(2, 1, 0).reshape(2 * HEADS, HEADS * P), np.float32),
        "expert_rows": np.ascontiguousarray(sel.reshape(N_EXPERTS, N_EXPERTS * P), np.float32),
    }


def phases():
    table, r = {}, 0
    for name, rounds, nk in stream():
        table[name] = (r, rounds, nk)
        r += rounds
    return table


def stream():
    def ffn(name):
        for t, size in enumerate(THIRDS):
            yield f"{name}.up{t}", 2 * size // U, KD
            yield f"{name}.down{t}", KD // U, size
    yield from ffn("l0f1")
    yield "k", 2, KD
    yield "q", 2, KD
    yield "v", 2, KD
    yield "wo", 2, KD
    yield from ffn("l0f2")
    yield from ffn("l1f1")
    yield "fourier", 2, KD
    yield from ffn("l1f2")
    yield "sbq", 1, KD
    yield "sbk", 1, KD
    yield "sbv", 1, KD
    yield "rq", 1, KD
    yield "rk", 1, KD
    yield "rv", 2, KD
    yield "gates", 4, KD
    yield "rg", 2, KD
    yield "sbout", 2, 4
    yield "retout", 2, KD
    yield "wout", 2, KD
    yield "moe", 4 * N_EXPERTS, KD


def build(nc, t, out):
    ph = phases()
    names = [s[0] for s in stream()]

    def next_nk(name):
        i = names.index(name) + 1
        return ph[names[i]][2] if i < len(names) else 0

    with ExitStack() as ctx:
        place = [((nc.sbuf_base + 63) // 64) * 64]

        def sb(name, width, dt=F32, parts=P, at=None):
            where = place[0] if at is None else at
            if at is None:
                place[0] += 32 * -(-width // 8)
                assert place[0] <= 229344 - 32, (name, place[0])
            return nc.alloc_sbuf_tensor_at(name, [parts, width], dt, offset=where)

        def sem(name):
            return ctx.enter_context(nc.semaphore(name))

        SLOT = KD * P
        raw = sb("raw", U * SLOT)
        hi_at = place[0]
        hi = sb("hi", U * SLOT, F32R)
        lo = sb("lo", U * SLOT, F32R)
        xs = sb("xs", KD * BOTH)
        nhi_at = place[0]
        nhi = sb("nhi", KD * BOTH, F32R)
        nlo = sb("nlo", KD * BOTH, F32R)
        cst = sb("cst", N_CONST)
        cols = sb("cols", N_COLS)
        csil = sb("csil", 16)
        modc = sb("modc", 3 * 72)
        acol = sb("acol", 3 * 24)
        gcol = sb("gcol", 3 * 24)
        zcol = sb("zcol", KD)
        head_rows = sb("head_rows", HEADS * P, parts=HEADS)
        epsc = sb("epsc", 1)
        rootc = sb("rootc", 1)
        sq = sb("sq", 2 * BOTH)
        sqsum = sb("sqsum", BOTH)
        rs = sb("rs", BOTH)
        rv_ = sb("rv_", BOTH)
        rstd = sb("rstd", BOTH)
        nt = sb("nt", 2 * BOTH)
        sg = sb("sg", 2 * BOTH)
        hf = sb("hf", 2 * BOTH)
        region = place[0]
        hhi = sb("hhi", KD * BOTH, F32R)
        hlo = sb("hlo", KD * BOTH, F32R)
        modw_at = place[0]
        modw = sb("modw", U * KD * MOD_W)
        macc = sb("macc", U * MOD_W)
        mrow = sb("mrow", 2 * MOD_W, parts=2)
        end_ffn = place[0]
        xraw = sb("xraw", 4 * D, at=region + 4 * KD * BOTH)
        MOD_BYTES = 4 * KD * MOD_W
        early_at = [hi_at + MOD_BYTES * m for m in range(4)] + [nhi_at + MOD_BYTES * m for m in range(4)]
        early_at += [modw_at + MOD_BYTES, modw_at + 3 * MOD_BYTES, region + 4 * KD * BOTH, region + 4 * KD * BOTH + MOD_BYTES]
        mod_early = [sb(f"mod_early{m}", KD * MOD_W, at=early_at[m]) for m in range(MOD_FIRST)]
        vrow = sb("vrow", 3 * P, at=region)

        class At:
            def __init__(self, start):
                self.at = start

            def __call__(self, name, width, dt=F32, parts=P):
                x = sb(name, width, dt, parts, at=self.at)
                self.at += 32 * -(-width // 8)
                assert self.at <= 229344 - 32, (name, self.at)
                return x

        A = At(region)
        QKW = SEQ + BOTH
        qk = A("qk", HEADS * QKW)
        vv = A("vv", 4 * D)
        ee = A("ee", 2 * 2 * BOTH)
        half_rows = sb("half_rows", HEADS * P, parts=2 * HEADS, at=A.at)
        aT = A("aT", 4 * SEQ)
        lamv = A("lamv", 4 * 64)
        lamt = A("lamt", 2 * 64)
        lams = A("lams", 8)
        mx = A("mx", 4)
        rsum = A("rsum", 4)
        rinv = A("rinv", 4)
        rsum2 = A("rsum2", 4)
        gqk4 = A("gqk4", 4)
        rotg = A("rotg", 2 * P)
        tq = A("tq", QKW)
        tr = A("tr", QKW)
        gqk = A("gqk", 2)
        aTs = (aT, sg)
        oT = sb("oT", HEADS * SEQ, at=A.at)
        A.at += 4 * HEADS * SEQ
        assert A.at <= 229344 - 32
        A = At(region)
        xf = A("xf", KD * SEQ)
        yt = A("yt", 2 * 4 * 512)
        dft = sb("dft", 2048, at=modw_at)
        A = At(region)
        sbq = A("sbq", 4 * SEQ)
        sbk = A("sbk", 4 * SEQ)
        sbv = A("sbv", 2 * 512)
        rq = A("rq", 4 * SEQ)
        rk = A("rk", 4 * SEQ)
        rvt = A("rvt", 2 * D)
        rg = A("rg", KD * SEQ)
        gates = A("gates", 16 * SEQ)
        wz = A("wz", 5 * 2 * DEC_W)
        decay = A("decay", 2 * DEC_W)
        yr = sb("yr", HEADS * SEQ, at=region)
        A = At(modw_at)
        xr = A("xr", KD * SEQ)
        cmb = A("cmb", N_EXPERTS * SEQ)
        sel = A("sel", N_EXPERTS * P, parts=N_EXPERTS)
        wr = A("wr", KD * 20)
        rbias = A("rbias", 20)
        lg = A("lg", 2 * 20)
        tiny = A("tiny", 2 * 64)
        cmbT = A("cmbT", SEQ, parts=N_EXPERTS)
        yt_out = sb("yt_out", 2 * D, at=region)

        ps = ctx.enter_context(nc.psum_tensor("ps", [P, 8 * 512], F32))

        def bank(b, n=512, first=0, parts=slice(0, P)):
            return ps[parts, 512 * b + first:512 * b + first + n]

        modps = bank(7).rearrange("p (b c) -> p b c", c=2)

        landed = [sem(f"landed{u}") for u in range(U)]
        hi_ready = sem("hi_ready")
        lo_ready = sem("lo_ready")
        slab_done = sem("slab_done")
        evacuated = sem("evacuated")
        sg_ready = sem("sg_ready")
        hhi_ready = sem("hhi_ready")
        hlo_ready = sem("hlo_ready")
        mod_landed = [sem(f"mod_landed{s}") for s in range(U)]
        mod_early_landed = [sem(f"mod_early_landed{m}") for m in range(MOD_FIRST)]
        mod_first_done = sem("mod_first_done")
        mod_rows = sem("mod_rows")
        mod_rows_copied = sem("mod_rows_copied")
        mod_scaled = sem("mod_scaled")
        mod_link = sem("mod_link")
        mod_jobs = sem("mod_jobs")
        mod_summed = sem("mod_summed")
        mod_copied = sem("mod_copied")
        sq_ready = sem("sq_ready")
        sq_used = sem("sq_used")
        sq_summed = sem("sq_summed")
        var_ready = sem("var_ready")
        rstd_ready = sem("rstd_ready")
        nt_ready = sem("nt_ready")
        nhi_ready = sem("nhi_ready")
        nlo_ready = sem("nlo_ready")
        in_x = sem("in_x")
        in_vec = sem("in_vec")
        in_const = sem("in_const")
        vec_turned = sem("vec_turned")
        cols_ready = sem("cols_ready")
        csil_ready = sem("csil_ready")
        eps_ready = sem("eps_ready")
        dve_link = sem("dve_link")
        act_link = sem("act_link")
        out_done = sem("out_done")
        x_rows_turned = sem("x_rows_turned")
        x_turned = sem("x_turned")
        fin_turned = sem("fin_turned")
        fin_copied = sem("fin_copied")

        def x_half(x):
            return x[:, :].rearrange("p (k n) -> p k n", k=KD)[:, :, X_COLS]

        def two(b):
            return ps[:, 512 * b:512 * b + 1024].rearrange("p (a n) -> p a n", a=2)[:, :, 0:DEC_W]

        def wk(i):
            return wz[:, i * 2 * DEC_W:(i + 1) * 2 * DEC_W]

        def wk3(i):
            return wk(i).rearrange("p (a n) -> p a n", a=2)

        TINY = {}

        def tn(h, name, n):
            if name not in TINY:
                TINY[name] = (sum(w for _, w in TINY.values()), n)
            at, n = TINY[name]
            assert at + n <= 64
            return tiny[:, 64 * h + at:64 * h + at + n]

        def fin_copy(eng, k):
            eng.wait_ge(fin_turned, k + 1)
            dst = yt_out[:, :].rearrange("p (h n) -> p h n", h=2)[:, :, k * P:(k + 1) * P]
            nc.vector.tensor_copy(dst, bank(k % 4, SEQ).rearrange("p (h n) -> p h n", h=2)).then_inc(fin_copied, 1)

        def const(name, cols_=None):
            at, n = CONST[name]
            return cst[:, at:at + (n if cols_ is None else cols_)]

        def col(name, k=0):
            at = VEC[name] + k
            return cols[:, at:at + 1]

        def chunk(x, c, width=BOTH, part=slice(0, BOTH)):
            w = (part.stop if part.stop is not None else width) - (part.start or 0)
            return x[:, bass.ds(c * width + (part.start or 0), w)]

        def qk_sum_at(part, h):
            if part == "k":
                return max(2 * h, 1)
            return min(2 * h + 3, 2 * HEADS)

        def tok(T):
            return slice(BOTH - T, BOTH)

        def k128(w):
            return w.rearrange("(k p) n -> p k n", p=P)

        def run(eng, rounds, body, peel_first=False):
            first = 0
            if peel_first and rounds > 1:
                body(0, False)
                first = 1
            if rounds - 1 - first >= 2:
                with eng.Fori(first, rounds - 1) as i:
                    body(i, False)
            else:
                for i in range(first, rounds - 1):
                    body(i, False)
            body(rounds - 1, True)

        FOURIER_NORM = 4

        def splits_before(s):
            return KD * (s - (1 if s > FOURIER_NORM else 0))

        S = {}

        def stage_sem(name):
            if name not in S:
                S[name] = sem(name)
            return S[name]

        for name in ("in_lam", "in_halves", "in_heads", "qk_summed", "in_dft", "in_dec0", "in_dec1", "in_router", "in_rbias", "in_sel",
                     "qk_sq", "qk_ss", "qk_var", "qk_rstd", "qk_done", "rotg_ready", "s_done", "max_done", "exp_done",
                     "a_done", "at_done", "at_copied", "o_done", "o_copied", "lam_sum", "lam_exp", 
                     "on_sq", "on_ss", "on_spread", "on_var", "on_rstd", "on_full", "on_hi", "on_lo",
                     "xf_ready", "y_done", "y_copied", "f_done", "f_hi", "f_lo",
                     "rot_ps", "rot_done", "z_done", "sp_done", "lk_done", "suf_done",
                     "arg_done", "w_exp", "sbo_done", "sb_hi", "sb_lo",
                     "rs_done", "rw_done", "ro_done", "ro_spread", "ro_sq", "ro_ss", "ro_var", "ro_rstd", "ro_full", "ro_hi", "ro_lo",
                     "gate_raw", "gate_done", "rg_done", "mix_full", "mix_hi", "mix_lo",
                     "rt_ps", "rt_max", "rt_exp", "rt_e2in", "rt_e2", "rt_comb", "rt_turned", "rt_copied",
                     "cmb_ps", "cmb_done", "cu_ready"):
            stage_sem(name)

        def vector_rows():
            pairs = []
            for name, src in (("c", t["c"]), ("c_ctx", t["c_ctx"].rearrange("(a n) -> a n", a=1)),
                              ("norm_g", t["norm_g"].rearrange("l s n -> (l s) n")), ("norm_mix", t["norm_mix_g_2"]),
                              ("norm_ffn", t["norm_ffn_g_2"]), ("norm_final", t["norm_final_g_2"].rearrange("(a n) -> a n", a=1)),
                              ("ret_norm", t["ret_norm_g_2"]), ("b_gate", t["b_gate_2"])):
                n = src.shape[0] * src.shape[1] // P
                pairs.append((vrow[VEC[name]:VEC[name] + n, 0:P], src.rearrange("a (k p) -> (a k) p", p=P)))
            for half in range(2):
                for name, src in (("q_g", t["attn_q_g"]), ("k_g", t["attn_k_g"])):
                    pairs.append((vrow[VEC[name]:VEC[name] + 1, 64 * half:64 * half + 64], src))
            pairs.append((vrow[VEC["sub_g"]:VEC["sub_g"] + 1, 0:P], t["attn_sub_g"]))
            for l in range(2):
                pairs.append((vrow[0:72, (1 + l) * P:(2 + l) * P], t["b_mod"][l, :].rearrange("(k p) -> k p", p=P)))
            return pairs

        beside0 = ph["rq"][0]

        def beside_at(name):
            return U * (ph[name][0] - beside0)

        block = ctx.enter_context(nc.Block())

        @block.sync
        def _(sp):
            def mod_unit(l, m, dst, landed_):
                sp.dma_start(dst.rearrange("p (k n) -> p k n", k=KD), k128(t["w_mod"][l])[:, :, bass.ds(m * MOD_W, MOD_W)]).then_inc(landed_, 16)

            for i, src in enumerate((t["ctx"], t["x"])):
                for h in range(2):
                    sp.dma_start(xraw[:, (2 * i + h) * D:(2 * i + h + 1) * D], src[0, h * P:(h + 1) * P, :]).then_inc(in_x, 16)
            for dst, src in vector_rows()[:N_VEC_DMAS // 2]:
                sp.dma_start(dst, src).then_inc(in_vec, 16)
            for m in range(MOD_NEED):
                mod_unit(0, m, mod_early[m][:, :], mod_early_landed[m])

            def slab(r, u, nk, src, first=False):
                if not first:
                    sp.wait_ge(lo_ready, U * (r - 1) + u + 1)
                sp.dma_start(raw[:, u * SLOT:u * SLOT + nk * P].rearrange("p (k n) -> p k n", k=nk), src).then_inc(landed[u], 16)

            def cols_of(w, c):
                return k128(w)[:, :, bass.ds(c * P, P)]

            MOD_CUTS = ((0, 1, 2, 3, 4), (0, 3, 4), (0, 3))

            def mod_load(r, u, lowest, jobs=range(MOD_JOBS - MOD_HELD)):
                job = U * lowest + u - MOD_AHEAD

                def unit(l, m, slot):
                    mod_unit(l, m, modw[:, slot * KD * MOD_W:(slot + 1) * KD * MOD_W], mod_landed[slot])

                if job not in jobs:
                    return
                if job < 2 * MOD_BOTH:
                    q = job // 2
                    if job % 2 == 0:
                        if q >= 2:
                            sp.wait_ge(mod_jobs, 2 * (q - 1))
                        unit(0, MOD_FIRST + q, 2 * (q % 2))
                    return
                slot = (u - MOD_AHEAD) % U
                if job < 2 * MOD_BOTH + U:
                    if slot % 2:
                        sp.wait_ge(mod_first_done, MOD_NEED + 2)
                    else:
                        sp.wait_ge(mod_jobs, 2 * MOD_BOTH - 2 + slot)
                else:
                    sp.wait_ge(mod_jobs, U * r + (u - MOD_AHEAD - U + 1))
                first = MOD_FIRST - MOD_BOTH
                l = 1 if job + first >= MOD_UNITS else 0
                unit(l, U * r + (u - MOD_AHEAD + first - l * MOD_UNITS), slot)

            def ffn(name, w_gu, w_d, mods=False):
                at = 0
                for th, size in enumerate(THIRDS):
                    r0, rounds, _ = ph[f"{name}.up{th}"]
                    cuts = MOD_CUTS[th] if mods else (0, rounds)
                    for i0, i1 in zip(cuts, cuts[1:]):
                        def up(i):
                            for u in range(U):
                                slab(i + r0, u, KD, cols_of(w_gu, 2 * i + (at + u // 2 + (D_FF // P if u % 2 else 0))),
                                     first=r0 + i1 == 1)
                                if mods:
                                    mod_load(i + r0, u, r0 + i0)
                        if i1 - i0 > 1:
                            with sp.Fori(i0, i1) as i:
                                up(i)
                        else:
                            up(i0)
                        if mods and r0 + i0 == 0:
                            for m in range(MOD_NEED, MOD_FIRST):
                                if m == MOD_NEED + 2:
                                    sp.wait_ge(x_rows_turned, 8)
                                mod_unit(0, m, mod_early[m][:, :], mod_early_landed[m])
                    r0, rounds, _ = ph[f"{name}.down{th}"]
                    for i in range(rounds):
                        for u in range(U):
                            c = U * i + u
                            slab(r0 + i, u, size, k128(w_d[at * P:(at + size) * P, :])[:, :, c * P:(c + 1) * P])
                            if mods:
                                mod_load(r0 + i, u, r0 + i)
                    at += size

            ffn("l0f1", t["ffn1_w_gu"][0], t["ffn1_w_d"][0], mods=True)

            def plain(name, w, c0, nk=KD, mods=False, after=None):
                r0, rounds, _ = ph[name]
                for i in range(rounds):
                    for u in range(U):
                        c = c0 + U * i + u
                        slab(r0 + i, u, nk, k128(w)[:, :, c * P:(c + 1) * P])
                        if after:
                            after(U * i + u)
                        if mods:
                            r = r0 + i - MOD_SHIFT
                            mod_load(r, u, r, range(MOD_JOBS - MOD_HELD, MOD_JOBS))

            w = t["attn_w_qkv"][0]
            plain("k", w, KD, mods=True)
            plain("q", w, 0, mods=True)
            sp.wait_ge(evacuated, 4 * ph["k"][0])
            sp.wait_ge(mod_jobs, MOD_JOBS)
            for i, name in enumerate(("attn_lam_q1", "attn_lam_k1", "attn_lam_q2", "attn_lam_k2")):
                sp.dma_start(lamv[:, 64 * i:64 * i + 64], t[name][0:1, :].to_broadcast([P, 64])).then_inc(S["in_lam"], 16)
            sp.dma_start(half_rows[:, :], t["half_rows"]).then_inc(S["in_halves"], 16)
            plain("v", w, 2 * KD)
            plain("wo", t["attn_w_o"][0], 0)
            ffn("l0f2", t["ffn2_w_gu"][0], t["ffn2_w_d"][0])
            sp.wait_ge(evacuated, 4 * ph["l0f2.up0"][0])
            sp.dma_start(dft[:, :], t["dft"]).then_inc(S["in_dft"], 16)
            ffn("l1f1", t["ffn1_w_gu"][1], t["ffn1_w_d"][1])
            plain("fourier", t["fourier_w"][0], 0)
            ffn("l1f2", t["ffn2_w_gu"][1], t["ffn2_w_d"][1])
            w = t["w_in_2"][0]
            for name, c0 in (("sbq", 0), ("sbk", 4), ("sbv", 8), ("rq", 12), ("rk", 16), ("rv", 20)):
                plain(name, w, c0)

            def decay_load(h):
                if h >= 2:
                    sp.wait_ge(S["rw_done"], h - 1)
                sp.dma_start(decay[:, (h % 2) * DEC_W:(h % 2 + 1) * DEC_W], t["decay"][:, h * DEC_W:(h + 1) * DEC_W]).then_inc(S[f"in_dec{h % 2}"], 16)

            def decays(name):
                def after(c):
                    h = beside_at(name) + c - DECAY_AT
                    if 2 <= h < HEADS:
                        decay_load(h)
                return after

            sp.wait_ge(evacuated, 4 * ph["sbq"][0])
            for h in range(2):
                decay_load(h)
            plain("gates", t["w_gate_2"][0], 0, after=decays("gates"))
            plain("rg", w, 28, after=decays("rg"))
            plain("sbout", t["w_sb_out_2"][0], 0, 4, after=decays("sbout"))
            plain("retout", t["w_ret_out_2"][0], 0)
            plain("wout", t["w_out_2"][0], 0)
            sp.wait_ge(S["mix_lo"], KD)
            sp.dma_start(wr[:, :].rearrange("p (k n) -> p k n", k=KD)[:, :, 0:4], k128(t["w_group_router_2"][0])).then_inc(S["in_router"], 16)
            sp.dma_start(wr[:, :].rearrange("p (k n) -> p k n", k=KD)[:, :, 4:20], k128(t["w_expert_router_2"][0])).then_inc(S["in_router"], 16)
            sp.dma_start(rbias[:, 0:4], t["b_group_router_2"][0:1, :].to_broadcast([P, 4])).then_inc(S["in_rbias"], 16)
            sp.dma_start(rbias[:, 4:20], t["b_expert_router_2"][0:1, :].to_broadcast([P, 16])).then_inc(S["in_rbias"], 16)
            sp.dma_start(sel[:, :], t["expert_rows"]).then_inc(S["in_sel"], 16)

            r0 = ph["moe"][0]
            with sp.Fori(0, N_EXPERTS) as e:
                for i in range(2):
                    for u in range(U):
                        w = t["w_exp_up_2"] if u % 2 else t["w_exp_gate_2"]
                        src = w.rearrange("l e (k p) n -> p (l e) k n", p=P)[:, bass.ds(e, 1), :, (2 * i + u // 2) * P:(2 * i + u // 2 + 1) * P]
                        slab(4 * e + (r0 + i), u, KD, src.rearrange("p a k n -> p (a k) n"))
                for i in range(2):
                    for u in range(U):
                        c = U * i + u
                        src = t["w_exp_down_2"].rearrange("l e (k p) n -> p (l e) k n", p=P)[:, bass.ds(e, 1), :, c * P:(c + 1) * P]
                        slab(4 * e + (r0 + 2 + i), u, 4, src.rearrange("p a k n -> p (a k) n"))
            sp.wait_ge(fin_copied, KD)
            for h in range(2):
                sp.dma_start(out[0, h * P:(h + 1) * P, :], yt_out[:, h * D:(h + 1) * D]).then_inc(out_done, 16)
            sp.wait_ge(out_done, 32)

        @block.scalar
        def _(act):
            link_at = [0]

            def link(ins):
                link_at[0] += 1
                ins.then_inc(act_link, 1)
                act.wait_ge(act_link, link_at[0])

            def split_hi(r, u, nk, wait_done=True):
                act.wait_ge(landed[u], 16 * r + 16)
                if wait_done:
                    act.wait_ge(slab_done, U * (r - 1) + u + 1)
                nc.scalar.activation(hi[:, u * SLOT:u * SLOT + nk * P], raw[:, u * SLOT:u * SLOT + nk * P], ACT.Copy).then_inc(hi_ready, 1)

            def plain(name, side=None, squares=None, mods=None):
                r0, rounds, nk = ph[name]

                def body(i, last):
                    for u in range(U):
                        if mods is not None:
                            if i == u == 0:
                                mod_scale(r0 - mods, 0, r0 - mods)
                            if U * i + u + 1 < U * rounds:
                                mod_scale(r0 - mods + i + (u + 1) // U, (u + 1) % U, r0 - mods + i)
                        if squares and i == 0 and u == 0:
                            nc.scalar.activation(rootc[:, :], epsc[:, :], ACT.Sqrt)
                        n_k = next_nk(name) if last else nk
                        final = squares and last and u == U - 1
                        if n_k and not final:
                            split_hi(i + (r0 + 1), u, n_k)
                        if squares:
                            square(squares[0], squares[1], U * i + u, U * (r0 + i) + u + 1)
                        if n_k and final:
                            split_hi(i + (r0 + 1), u, n_k)
                        if side:
                            side(U * i + u)
                if side or squares or mods is not None:
                    for i in range(rounds):
                        body(i, i == rounds - 1)
                else:
                    run(act, rounds, body)

            def mod_scale(r, u, lowest):
                if U * lowest < 2 * MOD_BOTH:
                    return
                act.wait_ge(mod_landed[u], 16 * r + 16 * (1 - 2 * MOD_BOTH // U + (0 if u % 2 else MOD_BOTH // 2)))
                for k in range(MOD_SCALED):
                    at = (u * KD + k) * MOD_W
                    ins = nc.scalar.activation(modw[:, at:at + MOD_W], modw[:, at:at + MOD_W], ACT.Copy, scale=csil[:, k:k + 1])
                ins.then_inc(mod_scaled, 1)

            def hidden_pair(r, p, T, j, split0, split1):
                act.wait_ge(slab_done, U * r + 2 * p + 2)
                nc.scalar.activation(sg[:, p * BOTH:p * BOTH + T], bank(2 * p, T), ACT.Silu).then_inc(sg_ready, 1)
                split0()
                act.wait_ge(evacuated, U * r + 2 * p + 2)
                nc.scalar.activation(chunk(hhi, j, part=tok(T)), hf[:, p * BOTH:p * BOTH + T], ACT.Copy).then_inc(hhi_ready, 1)
                split1()

            def ffn(name, T, squares=None, mods=False):
                for th, size in enumerate(THIRDS):
                    key = f"{name}.up{th}"
                    r0, rounds, nk = ph[key]

                    def up(i, last):
                        n_k = next_nk(key) if last else nk
                        for p in range(2):
                            def split(u):
                                split_hi(i + (r0 + 1), u, n_k)
                                if mods:
                                    mod_scale(i + r0, u, r0)
                            hidden_pair(i + r0, p, T, 2 * i + p, lambda: split(2 * p), lambda: split(2 * p + 1))
                    run(act, rounds, up)
                    plain(f"{name}.down{th}", squares=squares if th == len(THIRDS) - 1 else None,
                          mods=0 if mods and th < len(THIRDS) - 1 else None)

            def square(s, T, k, after):
                if after:
                    act.wait_ge(evacuated, after)
                if k == 1 and s:
                    act.wait_ge(sq_summed, s)
                if k >= 2:
                    act.wait_ge(sq_used, (KD - 1) * s + k - 1)
                nc.scalar.activation(sq[:, (k % 2) * BOTH:(k % 2) * BOTH + T], chunk(xs, k, part=tok(T)), ACT.Square).then_inc(sq_ready, 1)

            def norm_root(s, T):
                act.wait_ge(var_ready, 2 * s + 2)
                nc.scalar.activation(rstd[:, 0:T], rv_[:, 0:T], ACT.Sqrt).then_inc(rstd_ready, 1)

            def norm_hi(s, T, shift, full=None, between=None):
                for k in range(KD):
                    if between:
                        between(k)
                    act.wait_ge(nt_ready, KD * s + k + 1)
                    src = nt[:, (k % 2) * BOTH:(k % 2) * BOTH + T]
                    if full is not None:
                        nc.scalar.activation(full[:, k * SEQ:(k + 1) * SEQ], src, ACT.Identity, bias=shift(k)[0]).then_inc(S["xf_ready"], 1)
                        if s == FOURIER_NORM:
                            continue
                    halves = list(zip(shift(k), (T - SEQ, 0)))
                    for b, at in halves:
                        ins = nc.scalar.activation(chunk(nhi, k, part=slice(BOTH - T + at, BOTH - T + at + SEQ)), src[:, at:at + SEQ], ACT.Identity, bias=b)
                    ins.then_inc(nhi_ready, 1)

            def norm(s, T, shift, full=None):
                norm_root(s, T)
                norm_hi(s, T, shift, full)

            def mod_shift(sets, s):
                return lambda k: [modc[:, 72 * c + 24 * s + k:72 * c + 24 * s + k + 1] for c in sets]

            act.dma_start(cst[:, :], t["consts"]).then_inc(in_const, 16)
            act.dma_start(head_rows[:, :], t["expert_rows"][0:HEADS, 0:HEADS * P]).then_inc(S["in_heads"], 16)
            for dst, src in vector_rows()[N_VEC_DMAS // 2:]:
                act.dma_start(dst, src).then_inc(in_vec, 16)

            act.wait_ge(cols_ready, 1)
            nc.scalar.activation(csil[:, :], cols[:, 0:16], ACT.Silu).then_inc(csil_ready, 1)
            act.wait_ge(eps_ready, 1)
            nc.scalar.activation(rootc[:, :], epsc[:, :], ACT.Sqrt)
            act.wait_ge(x_turned, 8)
            for k in range(KD):
                square(0, BOTH, k, 0)

            def mod_row_copy(m):
                act.wait_ge(mod_rows, m + 1)
                if m >= 2:
                    act.wait_ge(mod_first_done, m - 1)
                nc.scalar.activation(mrow[:, (m % 2) * MOD_W:(m % 2 + 1) * MOD_W], bank(5 + m % 2, MOD_W, parts=slice(0, 2)), ACT.Copy).then_inc(mod_rows_copied, 1)

            for m in range(MOD_NEED):
                mod_row_copy(m)
                if m == 1:
                    norm_root(0, BOTH)
                if m == 5:
                    act.wait_ge(mod_first_done, 4)
                if m >= 5:
                    split_hi(0, m - 5, KD, wait_done=False)
            split_hi(0, 3, KD, wait_done=False)

            norm_hi(0, BOTH, mod_shift((0, 1), 0), between=lambda k: mod_row_copy(MOD_NEED + k // 2) if k % 2 == 0 else None)
            ffn("l0f1", BOTH, squares=(1, BOTH), mods=True)
            norm(1, BOTH, mod_shift((0, 1), 1))
            plain("k", mods=MOD_SHIFT)
            def qk_square(part, h):
                n = BOTH if part == "k" else SEQ
                if part == "k":
                    src, dst = qk[:, h * QKW + SEQ:(h + 1) * QKW], sq[:, (h % 2) * BOTH:(h % 2 + 1) * BOTH]
                    act.wait_ge(evacuated, U * ph["q"][0])
                else:
                    src, dst = qk[:, h * QKW:h * QKW + SEQ], nt[:, (h % 2) * SEQ:(h % 2 + 1) * SEQ]
                    act.wait_ge(evacuated, U * ph["q"][0] + h + 1)
                if h >= 2:
                    act.wait_ge(S["qk_summed"], qk_sum_at(part, h - 2))
                nc.scalar.activation(dst, src, ACT.Square).then_inc(S["qk_sq"], 1)

            def qk_squares(c):
                qk_square("k", c)
                if c:
                    qk_square("q", c - 1)

            plain("q", side=qk_squares)
            qk_square("q", HEADS - 1)
            act.wait_ge(S["qk_var"], 2)
            nc.scalar.activation(tq[0:2 * HEADS, :], tr[0:2 * HEADS, :], ACT.Sqrt).then_inc(S["qk_rstd"], 1)
            plain("v")

            act.wait_ge(S["lam_sum"], 1)
            nc.scalar.activation(lams[:, 2:4], lams[:, 0:2], ACT.Exp).then_inc(S["lam_exp"], 1)

            def o_square(h):
                act.wait_ge(S["o_copied"], h + 1)
                nc.scalar.activation(qk[:, h * QKW:h * QKW + SEQ], oT[:, h * SEQ:(h + 1) * SEQ], ACT.Square).then_inc(S["on_sq"], 1)

            for h in range(HEADS):
                for ti in range(4):
                    act.wait_ge(S["max_done"], 4 * h + ti + 1)
                    if h:
                        act.wait_ge(S["at_done"], h)
                    nc.scalar.activation(ee[:, ti * BOTH:(ti + 1) * BOTH], bank(4 + ti), ACT.Exp, bias=mx[:, ti:ti + 1],
                                         scale=0.125, accum_out=rsum[:, ti:ti + 1]).then_inc(S["exp_done"], 1)
                act.wait_ge(S["at_done"], h + 1)
                if h >= 2:
                    act.wait_ge(S["o_done"], h - 1)
                for b in range(2):
                    nc.scalar.activation(aTs[h % 2][:, 512 * b:512 * b + 512], bank(b), ACT.Copy).then_inc(S["at_copied"], 1)
                if h >= 2:
                    o_square(h - 2)
            o_square(HEADS - 2)
            o_square(HEADS - 1)
            act.wait_ge(S["on_var"], 2)
            nc.scalar.activation(tq[0:HEADS, 0:SEQ], tr[0:HEADS, 0:SEQ], ACT.Sqrt).then_inc(S["on_rstd"], 1)
            for h in range(HEADS):
                act.wait_ge(S["on_full"], h + 1)
                nc.scalar.activation(chunk(nhi, h, part=X_COLS), oT[:, h * SEQ:(h + 1) * SEQ], ACT.Copy).then_inc(S["on_hi"], 1)
            plain("wo", squares=(2, SEQ))
            norm(2, SEQ, mod_shift((0,), 2))
            ffn("l0f2", SEQ, squares=(3, SEQ))
            norm(3, SEQ, mod_shift((2,), 0))
            ffn("l1f1", SEQ, squares=(4, SEQ))

            norm(4, SEQ, mod_shift((2,), 1), full=xf)
            for i in range(8):
                act.wait_ge(S["y_done"], i + 1)
                nc.scalar.activation(yt[:, 512 * i:512 * i + 512], bank(i % 4), ACT.Copy).then_inc(S["y_copied"], 1)
            for c in range(KD):
                act.wait_ge(S["f_done"], c + 1)
                nc.scalar.activation(chunk(nhi, c, part=X_COLS), bank(4 + c % 4, SEQ), ACT.Copy).then_inc(S["f_hi"], 1)
            plain("fourier", squares=(5, SEQ))
            norm(5, SEQ, mod_shift((2,), 2))
            ffn("l1f2", SEQ, squares=(6, SEQ))

            norm(6, SEQ, lambda k: [zcol[:, 0:1]])
            for name in ("sbq", "sbk", "sbv"):
                plain(name)

            def beside(T):
                for c in range(4):
                    if T == SBO_AT[c]:
                        act.wait_ge(S["sbo_done"], c + 1)
                        nc.scalar.activation(chunk(nhi, c, part=slice(0, SEQ)), bank(6, SEQ), ACT.Copy).then_inc(S["sb_hi"], 1)
                for c in range(4):
                    if T == Z_AT[c]:
                        if c:
                            act.wait_ge(S["lk_done"], 2 * c)
                        act.wait_ge(S["z_done"], c + 1)
                        link(nc.scalar.activation(wk3(0), two(4), ACT.Abs, scale=0.125))
                        link(nc.scalar.activation(wk(1), wk(0), ACT.Exp, scale=-1.0))
                        nc.scalar.activation(wk(0), wk(1), ACT.Ln, bias=const("ones", 1)).then_inc(S["sp_done"], 1)
                    if T == WEIGHT_AT[c]:
                        act.wait_ge(S["arg_done"], c + 1)
                        nc.scalar.activation(wk(0), wk(1), ACT.Exp).then_inc(S["w_exp"], 1)
                h = T - RET_AT - 2
                if 0 <= h < HEADS:
                    act.wait_ge(S["ro_full"], h + 1)
                    if h >= 2:
                        act.wait_ge(S["ro_ss"], h - 1)
                    nc.scalar.activation(sq[:, (h % 2) * BOTH:(h % 2) * BOTH + SEQ], yr[:, h * SEQ:(h + 1) * SEQ], ACT.Square).then_inc(S["ro_sq"], 1)
                b = T - GATE_AT
                if 0 <= b < KD:
                    act.wait_ge(evacuated, U * ph["rg"][0])
                    g = gates[:, 2 * b * SEQ:2 * (b + 1) * SEQ]
                    nc.scalar.activation(g, g, ACT.Sigmoid).then_inc(S["gate_done"], 1)
                if T == ROOT_AT + 1:
                    act.wait_ge(S["ro_var"], 2)
                    nc.scalar.activation(rstd[0:HEADS, 0:SEQ], rv_[0:HEADS, 0:SEQ], ACT.Sqrt).then_inc(S["ro_rstd"], 1)
                b = T - SILU_AT
                if 0 <= b < 2:
                    act.wait_ge(evacuated, U * ph["sbout"][0])
                    g = rg[:, 4 * b * SEQ:4 * (b + 1) * SEQ]
                    nc.scalar.activation(g, g, ACT.Silu).then_inc(S["rg_done"], 1)

            for name in ("rq", "rk", "rv", "gates", "rg", "sbout"):
                plain(name, side=lambda c: beside(beside_at(name) + c))
            for h in range(HEADS):
                act.wait_ge(S["mix_full"], h + 1)
                nc.scalar.activation(chunk(nhi, h, part=X_COLS), yr[:, h * SEQ:(h + 1) * SEQ], ACT.Copy).then_inc(S["ro_hi"], 1)

            def mix_hi(c):
                act.wait_ge(S["gate_raw"], c + 1)
                nc.scalar.activation(chunk(nhi, c, part=slice(0, SEQ)), gates[:, c * SEQ:(c + 1) * SEQ], ACT.Copy).then_inc(S["mix_hi"], 1)

            plain("retout", side=mix_hi)
            plain("wout", squares=(7, SEQ))

            norm(7, SEQ, lambda k: [zcol[:, 0:1]], full=xr)
            for h in range(2):
                act.wait_ge(S["rt_max"], h + 1)
                nc.scalar.activation(tn(h, "e", 4), lg[:, 20 * h:20 * h + 4], ACT.Exp, bias=tn(h, "negm", 1), accum_out=tn(h, "sum", 1)).then_inc(S["rt_exp"], 1)
                act.wait_ge(S["rt_e2in"], h + 1)
                nc.scalar.activation(tn(h, "e2", 1), tn(h, "d", 1), ACT.Exp).then_inc(S["rt_e2"], 1)
            for b in range(N_EXPERTS // 2):
                act.wait_ge(S["cmb_ps"], 2 * b + 2)
                nc.scalar.activation(cmb[:, 512 * b:512 * b + 512], bank(4 + b % 4), ACT.Copy).then_inc(S["cmb_done"], 1)

            r0 = ph["moe"][0]

            def expert(e, last):
                for i in range(2):
                    n_k = KD if i == 0 else 4
                    for p in range(2):
                        hidden_pair(4 * e + (r0 + i), p, SEQ, 2 * i + p, lambda: split_hi(4 * e + (r0 + i + 1), 2 * p, n_k),
                                    lambda: split_hi(4 * e + (r0 + i + 1), 2 * p + 1, n_k))
                for i in range(2):
                    for u in range(U):
                        if last:
                            square(8, SEQ, U * i + u, U * (4 * e + r0 + 2 + i) + u + 1)
                        if i == 0 or not last:
                            split_hi(4 * e + (r0 + 2 + i + 1), u, 4 if i == 0 else KD)
            run(act, N_EXPERTS, expert)

            norm_root(8, SEQ)

        @block.vector
        def _(dve):
            link_at = [0]

            def link(ins):
                link_at[0] += 1
                ins.then_inc(dve_link, 1)
                dve.wait_ge(dve_link, link_at[0])

            v = nc.vector

            def split_lo(r, u, nk):
                dve.wait_ge(hi_ready, U * r + u + 1)
                s = slice(u * SLOT, u * SLOT + nk * P)
                v.tensor_tensor(lo[:, s], raw[:, s], hi[:, s].bitcast(F32), ALU.subtract).then_inc(lo_ready, 1)

            def add_square(s, T, k):
                dve.wait_ge(sq_ready, KD * s + k + 1)
                acc, x = sqsum[:, 0:T], sq[:, (k % 2) * BOTH:(k % 2) * BOTH + T]
                if k == 1:
                    if s:
                        dve.wait_ge(sq_summed, s)
                    v.tensor_tensor(acc, sq[:, 0:T], x, ALU.add).then_inc(sq_used, 2)
                else:
                    dve.wait_ge(sq_used, (KD - 1) * s + k)
                    v.tensor_tensor(acc, acc, x, ALU.add).then_inc(sq_used, 1)

            def plain(name, evac, mods=None, side=None, squares=None):
                r0, rounds, nk = ph[name]

                def body(i, last):
                    for u in range(U):
                        if mods is not None:
                            mod_job(i + r0 - mods, u, r0 - mods)
                        dve.wait_ge(slab_done, U * i + (U * r0 + u + 1))
                        evac(u, U * i + u)
                        if squares and U * i + u >= 2:
                            add_square(squares[0], squares[1], U * i + u - 1)
                        n_k = next_nk(name) if last else nk
                        if n_k and not (squares and last and u == U - 1):
                            split_lo(i + (r0 + 1), u, n_k)
                        if side:
                            side(U * i + u)
                if mods is not None or side or squares:
                    for i in range(rounds):
                        body(i, i == rounds - 1)
                else:
                    run(dve, rounds, body)

            def late_split(name):
                r0, rounds, _ = ph[name]
                split_lo(r0 + rounds, U - 1, next_nk(name))

            def rows_pairs(name, evac, side=None, before=None):
                r0, rounds, nk = ph[name]
                for i in range(rounds):
                    for p in range(2):
                        if before:
                            before(2 * i + p)
                        dve.wait_ge(slab_done, U * (r0 + i) + 2 * p + 2)
                        evac(p, 2 * i + p)
                        for u in (2 * p, 2 * p + 1):
                            split_lo(i + (r0 + 1), u, nk if i < rounds - 1 else next_nk(name))
                        if side:
                            side(2 * i + p)

            def mod_job(r, u, lowest):
                def acc(u):
                    return macc[:, u * MOD_W:(u + 1) * MOD_W]

                if U * lowest < 2 * MOD_BOTH:
                    if u % 2 == 0:
                        return
                    p = u // 2
                    dve.wait_ge(mod_landed[2 * p], 16 * r + 16)
                    if lowest:
                        dve.wait_ge(mod_summed, U * r + (u - (U - 1)))
                    base = 4 * (KD - 1) * r + 2 * (KD - 1) * p
                    for k in range(KD):
                        wk_ = modw[:, (2 * p * KD + k) * MOD_W:(2 * p * KD + k + 1) * MOD_W]
                        for cond in range(2):
                            a, c = acc(u - 1 + cond), csil[:, KD * cond + k:KD * cond + k + 1]
                            if k == 0:
                                ins = v.tensor_scalar(a, wk_, c, None, ALU.mult)
                            else:
                                dve.wait_ge(mod_link, base + 2 * k + (cond - 1))
                                ins = v.scalar_tensor_tensor(out=a, in0=wk_, scalar=c, in1=a, op0=ALU.mult, op1=ALU.add)
                            if k < KD - 1:
                                ins.then_inc(mod_link, 1)
                    ins.then_inc(mod_jobs, 2)
                    return
                job = U * r + u
                rest = KD - MOD_SCALED
                w = modw[:, u * KD * MOD_W:(u + 1) * KD * MOD_W]
                dve.wait_ge(mod_scaled, job + (1 - 2 * MOD_BOTH))
                for k in range(rest):
                    wk_ = w[:, (MOD_SCALED + k) * MOD_W:(MOD_SCALED + k + 1) * MOD_W]
                    v.scalar_tensor_tensor(out=wk_, in0=wk_, scalar=csil[:, MOD_SCALED + k:MOD_SCALED + k + 1], in1=w[:, k * MOD_W:(k + 1) * MOD_W],
                                           op0=ALU.mult, op1=ALU.add).then_inc(mod_link, 1)
                dve.wait_ge(mod_link, rest * job + (rest + 2 * MOD_BOTH * (KD - 1 - rest)))
                dve.wait_ge(mod_summed, job - (U - 1))
                v.reduce_sum(acc(u), w[:, rest * MOD_W:].rearrange("p (k n) -> p n k", n=MOD_W), AX_X).then_inc(mod_jobs, 1)

            def hidden_pair(r, p, T, h, j, split0, split1, weigh=None):
                f = hf[:, p * BOTH:p * BOTH + T]
                up = bank(2 * p + 1, T)
                if not (isinstance(h, int) and h < 2):
                    dve.wait_ge(hlo_ready, h - 1)
                if weigh is not None:
                    dve.wait_ge(slab_done, U * r + 2 * p + 2)
                    v.tensor_tensor(f, up, weigh, ALU.mult).then_inc(S["cu_ready"], 1)
                    up = f
                    dve.wait_ge(S["cu_ready"], h + 1 - moe_h0)
                dve.wait_ge(sg_ready, h + 1)
                v.tensor_tensor(f, sg[:, p * BOTH:p * BOTH + T], up, ALU.mult).then_inc(evacuated, 2)
                split0()
                dve.wait_ge(hhi_ready, h + 1)
                v.tensor_tensor(chunk(hlo, j, part=tok(T)), f, chunk(hhi, j, part=tok(T)).bitcast(F32), ALU.subtract).then_inc(hlo_ready, 1)
                split1()

            h_at = [0]
            moe_h0 = 4 * sum(THIRDS)

            def ffn(name, T, gate, squares, mods=False):
                for th, size in enumerate(THIRDS):
                    key = f"{name}.up{th}"
                    r0, rounds, nk = ph[key]

                    def up(i, last):
                        n_k = next_nk(key) if last else nk
                        for p in range(2):
                            def split(u):
                                split_lo(i + (r0 + 1), u, n_k)
                                if mods:
                                    mod_job(i + r0, u, i if isinstance(i, int) and r0 == 0 else max(r0, 1))
                            hidden_pair(i + r0, p, T, 2 * i + (h_at[0] + p), 2 * i + p, lambda: split(2 * p), lambda: split(2 * p + 1))
                    run(dve, rounds, up, peel_first=mods and th == 0)
                    h_at[0] += size
                    plain(f"{name}.down{th}", add_to_x(T, gate), mods=0 if mods and th < len(THIRDS) - 1 else None,
                          squares=(squares, T) if th == len(THIRDS) - 1 else None)

            def add_to_x(T, gate):
                def evac(u, c):
                    g = gate(c)
                    for i, (col_, at) in enumerate(zip(g, (T - SEQ, 0))):
                        x = chunk(xs, c, part=slice(BOTH - T + at, BOTH - T + at + SEQ))
                        ins = v.scalar_tensor_tensor(out=x, in0=bank(u, SEQ, at), scalar=col_, in1=x, op0=ALU.mult, op1=ALU.add)
                    ins.then_inc(evacuated, 1)
                return evac

            def gates_of(sets, s):
                return lambda c: [gcol[:, bass.ds(24 * k + 8 * s + c, 1)] for k in sets]

            def norm_var(s, T):
                dve.wait_ge(sq_summed, s + 1)
                v.tensor_scalar(rs[:, 0:T], bank(4, T), 1.0 / D, EPS, ALU.mult, ALU.add).then_inc(var_ready, 1)
                dve.wait_ge(var_ready, 2 * s + 1)
                v.reciprocal(rv_[:, 0:T], rs[:, 0:T]).then_inc(var_ready, 1)

            def norm_apply(s, T, gain, shift, split=True):
                dve.wait_ge(rstd_ready, s + 1)

                def lo_of(k):
                    dve.wait_ge(nhi_ready, splits_before(s) + k + 1)
                    for b, at in zip(shift(k), (T - SEQ, 0)):
                        part = slice(BOTH - T + at, BOTH - T + at + SEQ)
                        f = nt[:, (k % 2) * BOTH + at:(k % 2) * BOTH + at + SEQ]
                        ins = v.scalar_tensor_tensor(out=chunk(nlo, k, part=part), in0=f, scalar=b,
                                                     in1=chunk(nhi, k, part=part).bitcast(F32), op0=ALU.add, op1=ALU.subtract)
                    ins.then_inc(nlo_ready, 1)

                for k in range(KD):
                    if k >= 2 and split:
                        dve.wait_ge(nlo_ready, splits_before(s) + k - 1)
                    elif k >= 2:
                        dve.wait_ge(S["xf_ready"], k - 1)
                    for a, at in zip(gain(k), (T - SEQ, 0)):
                        ins = v.scalar_tensor_tensor(out=nt[:, (k % 2) * BOTH + at:(k % 2) * BOTH + at + SEQ],
                                                     in0=chunk(xs, k, part=slice(BOTH - T + at, BOTH - T + at + SEQ)), scalar=a,
                                                     in1=rstd[:, at:at + SEQ], op0=ALU.mult, op1=ALU.mult)
                    ins.then_inc(nt_ready, 1)
                    if k and split:
                        lo_of(k - 1)
                if split:
                    lo_of(KD - 1)

            def mod_gain(sets, s):
                return lambda k: [acol[:, 24 * c + 8 * s + k:24 * c + 8 * s + k + 1] for c in sets]

            def mod_shift(sets, s):
                return lambda k: [modc[:, 72 * c + 24 * s + k:72 * c + 24 * s + k + 1] for c in sets]

            def vec_gain(name):
                return lambda k: [col(name, k)]

            def no_shift(k):
                return [zcol[:, 0:1]]

            def take_mod(sets, l, b0, b1, last=True):
                for i, (k, cond) in enumerate(sets):
                    ins = v.tensor_tensor(modc[:, 72 * k + b0:72 * k + b1], modps[:, 72 * l + b0:72 * l + b1, cond],
                                          cols[:, B_MOD + 72 * l + b0:B_MOD + 72 * l + b1], ALU.add)
                    if i == len(sets) - 1:
                        ins.then_inc(mod_copied, 1)
                    else:
                        link(ins)

            def gain_cols(sets, l, s):
                for k, _ in sets:
                    link(v.scalar_tensor_tensor(out=acol[:, 24 * k + 8 * s:24 * k + 8 * s + 8],
                                                in0=modc[:, 72 * k + 24 * s + 8:72 * k + 24 * s + 16], scalar=1.0,
                                                in1=cols[:, VEC["norm_g"] + 24 * l + 8 * s:VEC["norm_g"] + 24 * l + 8 * s + 8],
                                                op0=ALU.add, op1=ALU.mult))

            def gate_cols(sets, s):
                for k, _ in sets:
                    link(v.tensor_scalar(gcol[:, 24 * k + 8 * s:24 * k + 8 * s + 8], modc[:, 72 * k + 24 * s + 16:72 * k + 24 * s + 24],
                                         1.0 if s == 1 else 0.5, None, ALU.mult))

            XC = ((0, 0), (1, 1))

            link(v.memset(zcol[:, :], 0.0))
            v.memset(epsc[:, :], EPS).then_inc(eps_ready, 1)
            dve.wait_ge(vec_turned, 1)
            v.tensor_copy(cols[:, :], bank(6, N_COLS)).then_inc(cols_ready, 1)
            for i in range(8):
                dve.wait_ge(x_rows_turned, i + 1)
                half, tc = i % 2, i // 2
                dst = xs[:, :].rearrange("p (k n) -> p k n", k=KD)[:, 4 * half:4 * half + 4, tc * P:(tc + 1) * P]
                v.tensor_copy(dst, bank(i % 4).rearrange("p (k n) -> p k n", k=4)).then_inc(x_turned, 1)
            for k in range(1, KD - 1):
                add_square(0, BOTH, k)
            norm_var(0, BOTH)
            for u in range(U):
                split_lo(0, u, KD)
            dve.wait_ge(mod_first_done, MOD_NEED)
            dve.wait_ge(cols_ready, 1)
            take_mod(XC, 0, 0, 16)
            dve.wait_ge(mod_copied, 1)
            gain_cols(XC, 0, 0)
            norm_apply(0, BOTH, mod_gain((0, 1), 0), mod_shift((0, 1), 0))
            dve.wait_ge(mod_first_done, MOD_FIRST)
            take_mod(XC, 0, 16, 24)
            dve.wait_ge(mod_copied, 2)
            gate_cols(XC, 0)
            ffn("l0f1", BOTH, gates_of((0, 1), 0), 1, mods=True)
            norm_var(1, BOTH)
            dve.wait_ge(mod_summed, MOD_JOBS - MOD_HELD)
            take_mod(XC, 0, 24, 40)
            dve.wait_ge(mod_copied, 3)
            take_mod(((0, 0),), 0, 40, 72)
            dve.wait_ge(mod_copied, 4)
            gain_cols(XC, 0, 1)
            norm_apply(1, BOTH, mod_gain((0, 1), 1), mod_shift((0, 1), 1))
            late_split("l0f1.down2")
            gate_cols(((0, 0),), 1)
            gain_cols(((0, 0),), 0, 2)
            gate_cols(((0, 0),), 2)
            def norm(s, T, gain, shift, split=True):
                norm_var(s, T)
                norm_apply(s, T, gain, shift, split)

            def keep(dst_of, width):
                def evac(u, c):
                    v.tensor_copy(dst_of(c), bank(u, width)).then_inc(evacuated, 1)
                return evac

            plain("k", keep(lambda c: qk[:, bass.ds(c * QKW + SEQ, BOTH)], BOTH), mods=MOD_SHIFT)
            dve.wait_ge(mod_summed, MOD_JOBS)
            take_mod(((2, 0),), 1, 0, 72)
            dve.wait_ge(mod_copied, 5)
            for s in range(3):
                gain_cols(((2, 0),), 1, s)
                gate_cols(((2, 0),), s)

            plain("q", keep(lambda c: qk[:, bass.ds(c * QKW, SEQ)], SEQ))

            def keep_v(p, c):
                for h in range(2):
                    dst = vv[:, 2 * h * D:2 * (h + 1) * D].rearrange("p (t n) -> p t n", t=2)[:, :, c * 2 * P:(c + 1) * 2 * P]
                    v.tensor_copy(dst, bank(2 * p + h).rearrange("p (t n) -> p t n", t=2)).then_inc(evacuated, 1)

            for i, name in enumerate(("q_g", "k_g")):
                v.tensor_scalar(rotg[:, i * P:(i + 1) * P], const("rot16"), col(name), None, ALU.mult).then_inc(S["rotg_ready"], 1)
            dve.wait_ge(S["qk_summed"], 2 * HEADS)
            v.tensor_scalar(tq[0:2 * HEADS, :], ps[0:2 * HEADS, 5 * 512:5 * 512 + QKW], 1.0 / 64, EPS, ALU.mult, ALU.add).then_inc(S["qk_var"], 1)
            dve.wait_ge(S["qk_var"], 1)
            v.reciprocal(tr[0:2 * HEADS, :], tq[0:2 * HEADS, :]).then_inc(S["qk_var"], 1)

            def qk_head(h):
                q_ = qk[:, h * QKW:h * QKW + SEQ]
                kc = qk[:, h * QKW + SEQ:h * QKW + 2 * SEQ]
                kx = qk[:, h * QKW + 2 * SEQ:(h + 1) * QKW]
                dve.wait_ge(S["qk_ss"], h + 1)
                if h:
                    dve.wait_ge(S["qk_done"], h)
                sin2 = const("sinA").unsqueeze(1).to_broadcast([P, 2, SEQ])
                v.tensor_tensor(nt[:, 0:512].rearrange("p (a n) -> p a n", a=2), bank(4).rearrange("p (a n) -> p a n", a=2), sin2, ALU.mult)
                v.scalar_tensor_tensor(out=nt[:, 512:768], in0=q_, scalar=col("q_g"), in1=const("cosA"), op0=ALU.mult, op1=ALU.mult)
                link(v.scalar_tensor_tensor(out=nt[:, 768:1024], in0=kx, scalar=col("k_g"), in1=const("cosA"), op0=ALU.mult, op1=ALU.mult))
                link(v.tensor_tensor(nt[:, 0:512], nt[:, 0:512], nt[:, 512:1024], ALU.add))
                v.tensor_tensor(q_, nt[:, 0:256], bank(6, SEQ, SEQ), ALU.mult)
                v.tensor_tensor(kx, nt[:, 256:512], bank(7, SEQ, SEQ), ALU.mult)
                v.scalar_tensor_tensor(out=kc, in0=kc, scalar=col("k_g"), in1=bank(7, SEQ), op0=ALU.mult, op1=ALU.mult).then_inc(S["qk_done"], 1)

            def qk_heads(c):
                for h in ((0,), (1, 2), (3, 4), (5, 6, 7))[c]:
                    qk_head(h)

            rows_pairs("v", keep_v, before=qk_heads)

            dve.wait_ge(S["in_lam"], 64)
            lam2 = lamv[:, :].rearrange("p (a b n) -> p a b n", a=2, b=2)
            link(v.tensor_tensor(lamt[:, :].rearrange("p (a n) -> p a n", a=2), lam2[:, :, 0, :], lam2[:, :, 1, :], ALU.mult))
            v.reduce_sum(lams[:, 0:2], lamt[:, :].rearrange("p (a n) -> p a n", a=2), AX_X).then_inc(S["lam_sum"], 1)
            dve.wait_ge(S["lam_exp"], 1)
            link(v.tensor_tensor(lams[:, 4:5], lams[:, 3:4], lams[:, 2:3], ALU.subtract))
            link(v.tensor_scalar(lams[:, 5:6], lams[:, 4:5], -LAM_INIT, None, ALU.add))
            def rows_max(h):
                for ti in range(4):
                    dve.wait_ge(S["s_done"], 4 * h + ti + 1)
                    if h:
                        dve.wait_ge(S["exp_done"], 4 * h - 3 + ti)
                    link(v.reduce_max(gqk4[:, ti:ti + 1], bank(4 + ti), AX_X))
                    v.tensor_scalar(mx[:, ti:ti + 1], gqk4[:, ti:ti + 1], -0.125, None, ALU.mult).then_inc(S["max_done"], 1)

            def o_copy(h):
                dve.wait_ge(S["o_done"], h + 1)
                v.tensor_copy(oT[:, h * SEQ:(h + 1) * SEQ], bank(2 + h % 2, SEQ)).then_inc(S["o_copied"], 1)

            rows_max(0)
            for h in range(HEADS):
                dve.wait_ge(S["exp_done"], 4 * h + 4)
                link(v.reciprocal(rinv[:, :], rsum[:, :]))
                link(v.tensor_scalar(rsum2[:, :], rinv[:, :], lams[:, 5:6], None, ALU.mult))
                for q in range(2):
                    e0 = ee[:, 2 * q * BOTH:(2 * q + 1) * BOTH]
                    e1 = ee[:, (2 * q + 1) * BOTH:(2 * q + 2) * BOTH]
                    link(v.tensor_scalar(e0, e0, rinv[:, 2 * q:2 * q + 1], None, ALU.mult))
                    v.scalar_tensor_tensor(out=e0, in0=e1, scalar=rsum2[:, 2 * q + 1:2 * q + 2], in1=e0, op0=ALU.mult, op1=ALU.add).then_inc(S["a_done"], 1)
                if h + 1 < HEADS:
                    rows_max(h + 1)
                if h:
                    o_copy(h - 1)
            o_copy(HEADS - 1)
            link(v.tensor_scalar(gqk[:, 0:1], col("sub_g"), 1.0 - LAM_INIT, None, ALU.mult))
            dve.wait_ge(S["on_ss"], 1)
            v.tensor_scalar(tq[0:HEADS, 0:SEQ], bank(4, SEQ, parts=slice(0, HEADS)), 1.0 / P, EPS, ALU.mult, ALU.add).then_inc(S["on_var"], 1)
            dve.wait_ge(S["on_var"], 1)
            v.reciprocal(tr[0:HEADS, 0:SEQ], tq[0:HEADS, 0:SEQ]).then_inc(S["on_var"], 1)

            def o_lo(h):
                dve.wait_ge(S["on_hi"], h + 1)
                v.tensor_tensor(chunk(nlo, h, part=X_COLS), oT[:, h * SEQ:(h + 1) * SEQ], chunk(nhi, h, part=X_COLS).bitcast(F32), ALU.subtract).then_inc(S["on_lo"], 1)

            for h in range(HEADS):
                o = oT[:, h * SEQ:(h + 1) * SEQ]
                dve.wait_ge(S["on_spread"], h + 1)
                v.scalar_tensor_tensor(out=o, in0=o, scalar=gqk[:, 0:1], in1=bank(4 + h % 4, SEQ), op0=ALU.mult, op1=ALU.mult).then_inc(S["on_full"], 1)
                if h:
                    o_lo(h - 1)
            o_lo(HEADS - 1)

            plain("wo", add_to_x(SEQ, gates_of((0,), 1)), squares=(2, SEQ))
            norm(2, SEQ, mod_gain((0,), 2), mod_shift((0,), 2))
            late_split("wo")
            ffn("l0f2", SEQ, gates_of((0,), 2), 3)
            norm(3, SEQ, mod_gain((2,), 0), mod_shift((2,), 0))
            late_split("l0f2.down2")
            ffn("l1f1", SEQ, gates_of((2,), 0), 4)

            norm(4, SEQ, mod_gain((2,), 1), mod_shift((2,), 1), split=False)
            late_split("l1f1.down2")
            for c in range(KD):
                dve.wait_ge(S["f_hi"], c + 1)
                v.tensor_tensor(chunk(nlo, c, part=X_COLS), bank(4 + c % 4, SEQ), chunk(nhi, c, part=X_COLS).bitcast(F32), ALU.subtract).then_inc(S["f_lo"], 1)
            plain("fourier", add_to_x(SEQ, gates_of((2,), 1)), squares=(5, SEQ))
            norm(5, SEQ, mod_gain((2,), 2), mod_shift((2,), 2))
            late_split("fourier")
            ffn("l1f2", SEQ, gates_of((2,), 2), 6)

            norm(6, SEQ, vec_gain("norm_mix"), no_shift)
            late_split("l1f2.down2")

            def chunks_of(x):
                return keep(lambda c: x[:, bass.ds(c * SEQ, SEQ)], SEQ)

            def rows_of(x, width):
                def evac(p, c):
                    dst = x[:, :].rearrange("p (t n) -> p t n", t=2)[:, :, c * 2 * P:(c + 1) * 2 * P]
                    v.tensor_copy(dst, bank(2 * p).rearrange("p (t n) -> p t n", t=2)).then_inc(evacuated, 2)
                return evac

            def gate_in(u, c):
                v.tensor_scalar(gates[:, bass.ds(c * SEQ, SEQ)], bank(u, SEQ), cols[:, bass.ds(c + VEC["b_gate"], 1)], None, ALU.add).then_inc(evacuated, 1)

            plain("sbq", chunks_of(sbq))
            plain("sbk", chunks_of(sbk))
            rows_pairs("sbv", rows_of(sbv, 512))
            keep2 = const("keep").unsqueeze(1).to_broadcast([P, 2, DEC_W])

            def beside(T):
                for c in range(4):
                    if T == SBO_LO_AT[c]:
                        dve.wait_ge(S["sb_hi"], c + 1)
                        v.tensor_tensor(chunk(nlo, c, part=slice(0, SEQ)), bank(6, SEQ), chunk(nhi, c, part=slice(0, SEQ)).bitcast(F32), ALU.subtract).then_inc(S["sb_lo"], 1)
                for c in range(4):
                    if T == SOFT_AT[c]:
                        dve.wait_ge(S["sp_done"], c + 1)
                        link(v.tensor_scalar(wk3(2), two(4), 0.125, None, ALU.mult))
                        link(v.scalar_tensor_tensor(out=wk(3), in0=wk(2), scalar=0.0, in1=wk(0), op0=ALU.max, op1=ALU.add))
                        v.tensor_tensor(wk3(4), wk3(3), keep2, ALU.mult).then_inc(S["lk_done"], 1)
                        link(v.tensor_tensor(wk(2), wk(2), wk(3), ALU.subtract))
                    if T == SUM_AT[c]:
                        dve.wait_ge(S["suf_done"], c + 1)
                        v.tensor_tensor(wk3(1), wk3(2), two(6), ALU.subtract).then_inc(S["arg_done"], 1)
                    if T == WEIGHT_AT[c]:
                        dve.wait_ge(S["w_exp"], c + 1)
                        v.tensor_tensor(wk3(3), wk3(0), keep2, ALU.mult).then_inc(S["lk_done"], 1)
                j = T - ROT_AT
                if 0 <= j < 4:
                    for i, x in enumerate((rq, rk)):
                        n = 2 * j + i
                        x = x[:, j * SEQ:(j + 1) * SEQ]
                        dve.wait_ge(S["rot_ps"], n + 1)
                        if n:
                            dve.wait_ge(S["rot_done"], n)
                        link(v.tensor_tensor(nt[:, 0:SEQ], bank(4 + i, SEQ), const("sinB"), ALU.mult))
                        link(v.tensor_tensor(nt[:, SEQ:2 * SEQ], x, const("cosB"), ALU.mult))
                        v.tensor_tensor(x, nt[:, 0:SEQ], nt[:, SEQ:2 * SEQ], ALU.add).then_inc(S["rot_done"], 1)
                h = T - RET_AT - 1
                if 0 <= h < HEADS:
                    dve.wait_ge(S["ro_done"], h + 1)
                    v.tensor_copy(yr[:, h * SEQ:(h + 1) * SEQ], bank(6 + h % 2, SEQ)).then_inc(S["ro_full"], 1)
                h = T - RET_AT
                if 0 <= h < HEADS:
                    dve.wait_ge(S["rs_done"], h + 1)
                    dve.wait_ge(S[f"in_dec{h % 2}"], 16 * (h // 2 + 1))
                    if h >= 2:
                        dve.wait_ge(S["ro_done"], h - 1)
                    v.scalar_tensor_tensor(out=wk(0)[:, (h % 2) * DEC_W:(h % 2 + 1) * DEC_W], in0=bank(4, DEC_W), scalar=0.125,
                                           in1=decay[:, (h % 2) * DEC_W:(h % 2 + 1) * DEC_W], op0=ALU.mult, op1=ALU.mult).then_inc(S["rw_done"], 1)
                if T == ROOT_AT:
                    dve.wait_ge(S["ro_ss"], HEADS)
                    v.tensor_scalar(rs[0:HEADS, 0:SEQ], bank(5, SEQ, parts=slice(0, HEADS)), 1.0 / P, EPS, ALU.mult, ALU.add).then_inc(S["ro_var"], 1)
                    dve.wait_ge(S["ro_var"], 1)
                    v.reciprocal(rv_[0:HEADS, 0:SEQ], rs[0:HEADS, 0:SEQ]).then_inc(S["ro_var"], 1)

            def gated(first):
                def evac(u, c):
                    g = gates[:, (first + c) * SEQ:(first + c + 1) * SEQ]
                    dve.wait_ge(S["gate_done"], (first + c) // 2 + 1)
                    v.tensor_tensor(g, bank(u, SEQ), g, ALU.mult).then_inc(evacuated, 1)
                return evac

            def beside_phase(name):
                return lambda c: beside(beside_at(name) + c)

            plain("rq", chunks_of(rq), side=beside_phase("rq"))
            plain("rk", chunks_of(rk), side=beside_phase("rk"))
            rows_pairs("rv", rows_of(rvt, D), side=lambda c: beside(beside_at("rv") + 2 * c + 1))
            plain("gates", gate_in, side=beside_phase("gates"))
            plain("rg", chunks_of(rg), side=beside_phase("rg"))
            plain("sbout", gated(0), side=beside_phase("sbout"))

            def ret_lo(h):
                dve.wait_ge(S["ro_hi"], h + 1)
                v.tensor_tensor(chunk(nlo, h, part=X_COLS), yr[:, h * SEQ:(h + 1) * SEQ], chunk(nhi, h, part=X_COLS).bitcast(F32), ALU.subtract).then_inc(S["ro_lo"], 1)

            for h in range(HEADS):
                y = yr[:, h * SEQ:(h + 1) * SEQ]
                dve.wait_ge(S["ro_spread"], h + 1)
                link(v.scalar_tensor_tensor(out=y, in0=y, scalar=col("ret_norm", h), in1=bank(4 + h % 4, SEQ), op0=ALU.mult, op1=ALU.mult))
                dve.wait_ge(S["rg_done"], h // 4 + 1)
                v.tensor_tensor(y, y, rg[:, h * SEQ:(h + 1) * SEQ], ALU.mult).then_inc(S["mix_full"], 1)
                if h:
                    ret_lo(h - 1)
            ret_lo(HEADS - 1)

            def mix_lo(c):
                dve.wait_ge(S["mix_hi"], c + 1)
                v.tensor_tensor(chunk(nlo, c, part=slice(0, SEQ)), gates[:, c * SEQ:(c + 1) * SEQ], chunk(nhi, c, part=slice(0, SEQ)).bitcast(F32),
                                ALU.subtract).then_inc(S["mix_lo"], 1)

            def mix(c):
                dve.wait_ge(evacuated, U * ph["retout"][0] + c + 1)
                g = gates[:, c * SEQ:(c + 1) * SEQ]
                v.tensor_tensor(g, g, gates[:, (KD + c) * SEQ:(KD + c + 1) * SEQ], ALU.add).then_inc(S["gate_raw"], 1)
                if c:
                    mix_lo(c - 1)

            plain("retout", gated(KD), side=mix)
            mix_lo(KD - 1)
            plain("wout", add_to_x(SEQ, lambda c: [1.0]), squares=(7, SEQ))

            norm(7, SEQ, vec_gain("norm_ffn"), no_shift)
            late_split("wout")
            dve.wait_ge(S["in_rbias"], 32)
            for h in range(2):
                def best(x, out_, n):
                    link(v.reduce_max(n, x, AX_X))
                    link(v.tensor_scalar(tn(h, "eq", 4), x, n, None, ALU.is_ge))
                    link(v.tensor_tensor(tn(h, "eq", 4), tn(h, "eq", 4), const("first"), ALU.mult))
                    link(v.reduce_max(tn(h, "m", 1), tn(h, "eq", 4), AX_X))
                    link(v.tensor_scalar(out_, tn(h, "eq", 4), tn(h, "m", 1), None, ALU.is_ge))

                l = lg[:, 20 * h:20 * h + 20]
                dve.wait_ge(S["rt_ps"], h + 1)
                link(v.tensor_tensor(l, bank(4 + h, 20), rbias[:, :], ALU.add))
                best(l[:, 0:4], tn(h, "group", 4), tn(h, "v", 1))
                v.tensor_scalar(tn(h, "negm", 1), tn(h, "v", 1), -1.0, None, ALU.mult).then_inc(S["rt_max"], 1)
                dve.wait_ge(S["rt_exp"], h + 1)
                link(v.reduce_max(tn(h, "pg", 1), tn(h, "e", 4), AX_X))
                link(v.reciprocal(tn(h, "r", 1), tn(h, "sum", 1)))
                link(v.tensor_tensor(tn(h, "pg", 1), tn(h, "pg", 1), tn(h, "r", 1), ALU.mult))
                link(v.tensor_scalar(tn(h, "in", 4), l[:, 4:8], tn(h, "group", 4)[:, 0:1], None, ALU.mult))
                for g in range(1, 4):
                    link(v.scalar_tensor_tensor(out=tn(h, "in", 4), in0=l[:, 4 + 4 * g:8 + 4 * g], scalar=tn(h, "group", 4)[:, g:g + 1],
                                                in1=tn(h, "in", 4), op0=ALU.mult, op1=ALU.add))
                best(tn(h, "in", 4), tn(h, "one", 4), tn(h, "v", 1))
                link(v.scalar_tensor_tensor(out=tn(h, "in", 4), in0=tn(h, "one", 4), scalar=-BIG, in1=tn(h, "in", 4), op0=ALU.mult, op1=ALU.add))
                best(tn(h, "in", 4), tn(h, "two", 4), tn(h, "v2", 1))
                v.tensor_tensor(tn(h, "d", 1), tn(h, "v2", 1), tn(h, "v", 1), ALU.subtract).then_inc(S["rt_e2in"], 1)
                dve.wait_ge(S["rt_e2"], h + 1)
                link(v.tensor_scalar(tn(h, "r", 1), tn(h, "e2", 1), 1.0, None, ALU.add))
                link(v.reciprocal(tn(h, "sum", 1), tn(h, "r", 1)))
                link(v.tensor_tensor(tn(h, "g1", 1), tn(h, "sum", 1), tn(h, "pg", 1), ALU.mult))
                link(v.tensor_tensor(tn(h, "g2", 1), tn(h, "g1", 1), tn(h, "e2", 1), ALU.mult))
                link(v.tensor_scalar(tn(h, "one", 4), tn(h, "one", 4), tn(h, "g1", 1), None, ALU.mult))
                link(v.scalar_tensor_tensor(out=tn(h, "one", 4), in0=tn(h, "two", 4), scalar=tn(h, "g2", 1), in1=tn(h, "one", 4), op0=ALU.mult, op1=ALU.add))
                for g in range(4):
                    ins = v.tensor_scalar(tn(h, "comb", 16)[:, 4 * g:4 * g + 4], tn(h, "one", 4), tn(h, "group", 4)[:, g:g + 1], None, ALU.mult)
                ins.then_inc(S["rt_comb"], 1)
            dve.wait_ge(S["rt_turned"], 2)
            v.tensor_copy(cmbT[:, :], bank(6, SEQ, parts=slice(0, N_EXPERTS))).then_inc(S["rt_copied"], 1)
            dve.wait_ge(S["cmb_done"], N_EXPERTS // 2)

            r0 = ph["moe"][0]
            evac = add_to_x(SEQ, lambda c: [1.0])

            def expert(e, last):
                for i in range(2):
                    n_k = KD if i == 0 else 4
                    for p in range(2):
                        hidden_pair(4 * e + (r0 + i), p, SEQ, 4 * e + (moe_h0 + 2 * i + p), 2 * i + p,
                                    lambda: split_lo(4 * e + (r0 + i + 1), 2 * p, n_k),
                                    lambda: split_lo(4 * e + (r0 + i + 1), 2 * p + 1, n_k), weigh=cmb[:, bass.ds(e * SEQ, SEQ)])
                for i in range(2):
                    for u in range(U):
                        dve.wait_ge(slab_done, 16 * e + (U * (r0 + 2 + i) + u + 1))
                        evac(u, U * i + u)
                        if last and U * i + u >= 2:
                            add_square(8, SEQ, U * i + u - 1)
                        if i == 0 or not last:
                            split_lo(4 * e + (r0 + 2 + i + 1), u, 4 if i == 0 else KD)
            run(dve, N_EXPERTS, expert)

            norm_var(8, SEQ)
            dve.wait_ge(rstd_ready, 9)
            for k in range(KD):
                f = nt[:, (k % 2) * BOTH:(k % 2) * BOTH + SEQ]
                if k >= 2:
                    dve.wait_ge(fin_turned, k - 1)
                v.scalar_tensor_tensor(out=f, in0=chunk(xs, k, part=X_COLS), scalar=col("norm_final", k), in1=rstd[:, 0:SEQ],
                                       op0=ALU.mult, op1=ALU.mult).then_inc(nt_ready, 1)
                if k:
                    fin_copy(dve, k - 1)
            fin_copy(dve, KD - 1)

        @block.tensor
        def _(pe):
            def w_hi(u, k):
                return hi[:, u * SLOT + k * P:u * SLOT + (k + 1) * P]

            def w_lo(u, k):
                return lo[:, u * SLOT + k * P:u * SLOT + (k + 1) * P]

            def ready(r, u, first=False):
                pe.wait_ge(lo_ready, U * r + u + 1)
                if not first:
                    pe.wait_ge(evacuated, U * (r - 1) + u + 1)

            def slab(r, u, nk, T, xh, xl, part, first=False):
                ready(r, u, first)
                for k in range(nk):
                    h_, l_ = chunk(xh, k, part=part), chunk(xl, k, part=part)
                    pe.matmul(bank(u, T), w_hi(u, k), h_, start=(k == 0), stop=False)
                    pe.matmul(bank(u, T), w_hi(u, k), l_, start=False, stop=False)
                    ins = pe.matmul(bank(u, T), w_lo(u, k), h_, start=False, stop=(k == nk - 1))
                ins.then_inc(slab_done, 1)

            def first_pair(r, nk, T, xh, xl, part, chunk_ready, first=False):
                for u in range(2):
                    ready(r, u, first)
                for k in range(nk):
                    chunk_ready(k)
                    h_, l_ = chunk(xh, k, part=part), chunk(xl, k, part=part)
                    for u in range(2):
                        pe.matmul(bank(u, T), w_hi(u, k), h_, start=(k == 0), stop=False)
                        pe.matmul(bank(u, T), w_hi(u, k), l_, start=False, stop=False)
                        ins = pe.matmul(bank(u, T), w_lo(u, k), h_, start=False, stop=(k == nk - 1))
                        if k == nk - 1:
                            ins.then_inc(slab_done, 1)

            def rows_pairs(name, T, side=None):
                r0, rounds, _ = ph[name]

                def two_slabs(x, p, k):
                    return x[:, 2 * p * SLOT:2 * (p + 1) * SLOT].rearrange("p (u n) -> p u n", u=2)[:, :, k * P:(k + 1) * P]

                for i in range(rounds):
                    for p in range(2):
                        ready(r0 + i, 2 * p + 1)
                        for b in range(T // P):
                            part = slice(BOTH - T + b * P, BOTH - T + (b + 1) * P)
                            o = bank(2 * p + b // 2, 2 * P, 2 * P * (b % 2)).rearrange("p (u n) -> p u n", u=2)
                            for k in range(KD):
                                h_, l_ = chunk(nhi, k, part=part), chunk(nlo, k, part=part)
                                pe.matmul(o, h_, two_slabs(hi, p, k), start=(k == 0), stop=False)
                                pe.matmul(o, h_, two_slabs(lo, p, k), start=False, stop=False)
                                ins = pe.matmul(o, l_, two_slabs(hi, p, k), start=False, stop=(k == KD - 1))
                            if b == T // P - 1:
                                ins.then_inc(slab_done, 2)
                            if side:
                                side(2 * i + p, b)

            def rounds_of(i0, i1, body):
                if i1 - i0 > 1:
                    with pe.Fori(i0, i1) as i:
                        body(i)
                elif i1 > i0:
                    body(i0)

            def plain(name, T=SEQ, xh=nhi, xl=nlo, part=None, squares=None, chunk_ready=None, side=None):
                r0, rounds, nk = ph[name]

                def body(i, first=False):
                    for u in range(U):
                        if chunk_ready and first and u < 2:
                            if u == 0:
                                first_pair(r0, nk, T, xh, xl, part or tok(T), chunk_ready)
                        else:
                            slab(i + r0, u, nk, T, xh, xl, part or tok(T))
                        if side:
                            side(U * i + u)
                if side:
                    for i in range(rounds):
                        body(i, i == 0)
                elif chunk_ready:
                    body(0, True)
                    rounds_of(1, rounds, body)
                else:
                    rounds_of(0, rounds, body)
                if squares:
                    norm_sum(*squares)

            def mod_first_rows(m):
                pe.wait_ge(mod_early_landed[m], 16)
                for k in range(KD):
                    ins = pe.matmul(bank(5 + m % 2, MOD_W, parts=slice(0, 2)), csil[:, :].rearrange("p (c k) -> p k c", c=2)[:, k, :],
                                    mod_early[m][:, k * MOD_W:(k + 1) * MOD_W], start=(k == 0), stop=(k == KD - 1))
                ins.then_inc(mod_rows, 1)

            def mod_first_turn(m):
                pe.wait_ge(mod_rows_copied, m + 1)
                if m == MOD_NEED:
                    pe.wait_ge(mod_copied, 1)
                for b in range(2):
                    at = (m % 2) * MOD_W + b * P
                    ins = pe.matmul(bank(7, 2, 4 * m + 2 * b), mrow[:, at:at + P], const("ident", 2)[0:2, :], start=True, stop=True)
                ins.then_inc(mod_first_done, 1)

            def mod_sum(r, u, lowest, jobs=range(MOD_JOBS - MOD_HELD)):
                n = U * lowest + u - MOD_LAG
                if n not in jobs:
                    return
                a = (u - MOD_LAG) % U
                if n == 0:
                    pe.wait_ge(mod_copied, 2)
                both = n < 2 * MOD_BOTH
                pe.wait_ge(mod_jobs, U * r + (u - MOD_LAG + 1 + (1 if both and n % 2 == 0 else 0)))
                if both:
                    s = (u - MOD_LAG) % 2
                    at = 2 * U * r + (2 * (u - MOD_LAG - s) + 4 * MOD_FIRST + s)
                else:
                    at = 4 * U * r + 4 * (u - MOD_LAG + MOD_FIRST - MOD_BOTH)
                for b in range(2):
                    w = macc[:, a * MOD_W + b * P:a * MOD_W + (b + 1) * P]
                    ins = pe.matmul(ps[:, bass.ds(at + (7 * 512 + 2 * b), 1)], w, const("ones", 1), start=True, stop=True)
                ins.then_inc(mod_summed, 1)

            h_at = [0]

            def ffn(name, T, norm, mods=False, squares=None):
                for th, size in enumerate(THIRDS):
                    r0, rounds, nk = ph[f"{name}.up{th}"]

                    def up(i, lowest=0, first=False):
                        for u in range(U):
                            start = isinstance(i, int) and r0 + i == 0
                            if first and u < 2:
                                if u == 0:
                                    first_pair(r0, nk, T, nhi, nlo, tok(T), normed(norm), start)
                            else:
                                slab(i + r0, u, nk, T, nhi, nlo, tok(T), start)
                            if mods:
                                mod_sum(i + r0, u, r0 + lowest)
                    if th == 0:
                        up(0, 0, True)
                        rounds_of(1, rounds, lambda i: up(i, 1))
                    elif mods and th == 1:
                        for i in range(rounds):
                            up(i, i)
                    else:
                        rounds_of(0, rounds, up)
                    r0, rounds, nk = ph[f"{name}.down{th}"]
                    for i in range(rounds):
                        for u in range(U):
                            c = U * i + u
                            if c < 2:
                                if c == 0:
                                    first_pair(r0, nk, T, hhi, hlo, tok(T), lambda k: pe.wait_ge(hlo_ready, h_at[0] + k + 1))
                            else:
                                slab(r0 + i, u, nk, T, hhi, hlo, tok(T))
                            if mods:
                                mod_sum(r0 + i, u, r0 + i)
                    h_at[0] += size
                if squares:
                    norm_sum(*squares)

            def norm_sum(s, T):
                pe.wait_ge(sq_used, (KD - 1) * (s + 1))
                pe.matmul(bank(4, T), const("ones"), sqsum[:, 0:T], start=True, stop=False)
                pe.wait_ge(sq_ready, KD * (s + 1))
                last = (KD - 1) % 2 * BOTH
                pe.matmul(bank(4, T), const("ones"), sq[:, last:last + T], start=False, stop=True).then_inc(sq_summed, 1)

            def normed(s):
                return lambda k: pe.wait_ge(nlo_ready, splits_before(s) + k + 1)

            pe.wait_ge(in_vec, 16 * N_VEC_DMAS)
            pe.wait_ge(in_const, 16)
            pe.transpose(bank(6, N_VEC), vrow[0:N_VEC, 0:P], const("ident")[0:N_VEC, 0:N_VEC])
            for l in range(2):
                ins = pe.transpose(bank(6, 72, N_VEC + 72 * l), vrow[0:72, (1 + l) * P:(2 + l) * P], const("ident")[0:72, 0:72])
            ins.then_inc(vec_turned, 1)

            pe.wait_ge(csil_ready, 1)
            pe.wait_ge(in_x, 64)
            for i in range(8):
                half, tc = i % 2, i // 2
                if i >= 4:
                    pe.wait_ge(x_turned, i - 3)
                for k in range(4):
                    at = tc * D + (4 * half + k) * P
                    ins = pe.transpose(bank(i % 4, P, k * P), xraw[:, at:at + P], const("ident"))
                ins.then_inc(x_rows_turned, 1)
            for m0, m1 in ((0, MOD_NEED), (MOD_NEED, MOD_FIRST)):
                mod_first_rows(m0)
                for m in range(m0 + 1, m1):
                    mod_first_rows(m)
                    if m == 1:
                        norm_sum(0, BOTH)
                    mod_first_turn(m - 1)
                mod_first_turn(m1 - 1)
            ffn("l0f1", BOTH, 0, mods=True, squares=(1, BOTH))

            def held_sum(c):
                r = ph["k"][0] - MOD_SHIFT + c // U
                mod_sum(r, c % U, r, range(MOD_JOBS - MOD_HELD, MOD_JOBS))

            plain("k", BOTH, chunk_ready=normed(1), side=held_sum)
            for u in range(MOD_LAG):
                held_sum(MOD_HELD + u)
            def qk_sum(part, h):
                pe.wait_ge(S["qk_sq"], qk_sum_at(part, h))
                w = const("half_sums")[:, 2 * HEADS * h:2 * HEADS * (h + 1)]
                if part == "k":
                    o, x = bank(5, parts=slice(0, 2 * HEADS)), sq[:, (h % 2) * BOTH:(h % 2 + 1) * BOTH]
                else:
                    o, x = bank(6, SEQ, parts=slice(0, 2 * HEADS)), nt[:, (h % 2) * SEQ:(h % 2 + 1) * SEQ]
                pe.matmul(o, w, x, start=(h == 0), stop=(h == HEADS - 1)).then_inc(S["qk_summed"], 1)

            def qk_sums(c):
                if c:
                    qk_sum("k", c - 1)
                if c >= 2:
                    qk_sum("q", c - 2)

            plain("q", side=qk_sums)
            qk_sum("k", HEADS - 1)
            qk_sum("q", HEADS - 2)
            qk_sum("q", HEADS - 1)

            def qk_head(h):
                if h == 0:
                    pe.wait_ge(S["rotg_ready"], 2)
                    pe.wait_ge(S["in_halves"], 16)
                    pe.wait_ge(S["qk_rstd"], 1)
                else:
                    pe.wait_ge(S["qk_done"], h)
                rows = half_rows[:, h * P:(h + 1) * P]
                pe.matmul(bank(4, SEQ), rotg[:, 0:P], qk[:, h * QKW:h * QKW + SEQ], start=True, stop=True)
                pe.matmul(bank(4, SEQ, SEQ), rotg[:, P:2 * P], qk[:, h * QKW + 2 * SEQ:(h + 1) * QKW], start=True, stop=True)
                pe.matmul(bank(7, BOTH), rows, tq[0:2 * HEADS, 0:BOTH], start=True, stop=True)
                pe.matmul(bank(6, SEQ, SEQ), rows, tq[0:2 * HEADS, BOTH:QKW], start=True, stop=True).then_inc(S["qk_ss"], 1)

            def qk_heads(c, b):
                at = {2: 0, 4: 1, 6: 2, 7: 3, 9: 4, 11: 5, 13: 6, 14: 7}.get(BOTH // P * c + b)
                if at is not None:
                    qk_head(at)

            rows_pairs("v", BOTH, side=qk_heads)

            pe.wait_ge(S["qk_done"], HEADS)

            def scores(h):
                for ti in range(4):
                    q, c = ti // 2, ti % 2
                    if h:
                        pe.wait_ge(S["exp_done"], 4 * (h - 1) + ti + 1)
                    s = slice(64 * c, 64 * c + 64)
                    pe.matmul(bank(4 + ti), qk[s, h * QKW + q * P:h * QKW + (q + 1) * P], qk[s, h * QKW + SEQ:(h + 1) * QKW],
                              start=True, stop=True).then_inc(S["s_done"], 1)

            def values(h):
                pe.wait_ge(S["at_copied"], 2 * h + 2)
                if h >= 2:
                    pe.wait_ge(S["o_copied"], h - 1)
                for kc in range(4):
                    ins = pe.matmul(bank(2 + h % 2, SEQ), vv[:, kc * D + h * P:kc * D + (h + 1) * P], aTs[h % 2][:, kc * SEQ:(kc + 1) * SEQ],
                                    start=(kc == 0), stop=(kc == 3))
                ins.then_inc(S["o_done"], 1)

            scores(0)
            for h in range(HEADS):
                if h + 1 < HEADS:
                    scores(h + 1)
                if h:
                    pe.wait_ge(S["at_copied"], 2 * h)
                for q in range(2):
                    pe.wait_ge(S["a_done"], 2 * h + q + 1)
                    for kc in range(4):
                        ins = pe.transpose(bank(kc // 2, P, (kc % 2) * SEQ + q * P), ee[:, 2 * q * BOTH + kc * P:2 * q * BOTH + (kc + 1) * P], const("ident"))
                ins.then_inc(S["at_done"], 1)
                if h:
                    values(h - 1)
            values(HEADS - 1)
            for h in range(HEADS):
                pe.wait_ge(S["on_sq"], h + 1)
                ins = pe.matmul(bank(4, SEQ, parts=slice(0, HEADS)), const("head_sums")[:, HEADS * h:HEADS * (h + 1)],
                                qk[:, h * QKW:h * QKW + SEQ], start=(h == 0), stop=(h == HEADS - 1))
            ins.then_inc(S["on_ss"], 1)
            pe.wait_ge(S["in_heads"], 16)
            pe.wait_ge(S["on_rstd"], 1)

            def o_spread(h):
                if h >= 4:
                    pe.wait_ge(S["on_full"], h - 3)
                pe.matmul(bank(4 + h % 4, SEQ), head_rows[:, h * P:(h + 1) * P], tq[0:HEADS, 0:SEQ], start=True, stop=True).then_inc(S["on_spread"], 1)

            for h in range(4):
                o_spread(h)

            def o_chunk(k):
                if k + 4 < HEADS:
                    o_spread(k + 4)
                pe.wait_ge(S["on_lo"], k + 1)

            plain("wo", squares=(2, SEQ), chunk_ready=o_chunk)
            ffn("l0f2", SEQ, 2, squares=(3, SEQ))
            ffn("l1f1", SEQ, 3, squares=(4, SEQ))

            pe.wait_ge(S["in_dft"], 16)
            pe.wait_ge(evacuated, U * ph["fourier"][0])
            for g in range(4):
                pe.wait_ge(S["xf_ready"], 2 * g + 2)
                for tc in range(2):
                    i = 2 * g + tc
                    if i >= 4:
                        pe.wait_ge(S["y_copied"], i - 3)
                    for k in range(2):
                        at = (2 * g + k) * SEQ + tc * P
                        ins = pe.matmul(bank(i % 4), xf[:, at:at + P], dft[:, 512 * k:512 * k + 512], start=(k == 0), stop=(k == 1))
                    ins.then_inc(S["y_done"], 1)

            def over_tokens(c):
                if c >= 4:
                    pe.wait_ge(S["f_lo"], c - 3)
                pe.wait_ge(S["y_copied"], 2 * (c // 2) + 2)
                for j in range(4):
                    tc, sine = j // 2, j % 2
                    at = (2 * (c // 2) + tc) * 512 + SEQ * sine + (c % 2) * P
                    ins = pe.matmul(bank(4 + c % 4, SEQ), yt[:, at:at + P], dft[:, 1024 + 512 * tc + SEQ * sine:1024 + 512 * tc + SEQ * (sine + 1)],
                                    start=(j == 0), stop=(j == 3))
                ins.then_inc(S["f_done"], 1)

            for c in range(4):
                over_tokens(c)

            def f_chunk(k):
                if k == 0:
                    pe.wait_ge(S["y_copied"], KD)
                if k + 4 < KD:
                    over_tokens(k + 4)
                pe.wait_ge(S["f_lo"], k + 1)

            plain("fourier", squares=(5, SEQ), chunk_ready=f_chunk)
            ffn("l1f2", SEQ, 5, squares=(6, SEQ))

            plain("sbq", chunk_ready=normed(6))
            plain("sbk")
            rows_pairs("sbv", SEQ)

            def pair_scores(o, k_, q_, j, c):
                s = slice(64 * j, 64 * j + 64)
                pe.matmul(bank(o, SEQ), k_[s, c * SEQ:c * SEQ + P], q_[s, c * SEQ:(c + 1) * SEQ], start=True, stop=True)
                return pe.matmul(bank(o, P, SEQ), k_[s, c * SEQ + P:(c + 1) * SEQ], q_[s, c * SEQ + P:(c + 1) * SEQ], start=True, stop=True)

            def beside(T):
                for c in range(4):
                    if T == SBO_AT[c]:
                        pe.wait_ge(S["lk_done"], 2 * c + 2)
                        for j in range(2):
                            h = 2 * c + j
                            w = wk(3)[:, j * DEC_W:(j + 1) * DEC_W]
                            o = slice(64 * j, 64 * j + 64)
                            pe.matmul(bank(6, SEQ, parts=o), sbv[:, h * 64:h * 64 + 64], w[:, 0:SEQ], start=True, stop=False)
                            ins = pe.matmul(bank(6, P, P, parts=o), sbv[:, 512 + h * 64:512 + h * 64 + 64], w[:, SEQ:DEC_W], start=False, stop=True)
                        ins.then_inc(S["sbo_done"], 1)
                for c in range(4):
                    if T == Z_AT[c]:
                        if c == 0:
                            pe.wait_ge(evacuated, U * ph["rq"][0])
                        for j in range(2):
                            ins = pair_scores(4 + j, sbk, sbq, j, c)
                        ins.then_inc(S["z_done"], 1)
                    if T == SUM_AT[c]:
                        pe.wait_ge(S["lk_done"], 2 * c + 1)
                        if c:
                            pe.wait_ge(S["sb_lo"], c)
                        for j in range(2):
                            m = wk(4)[:, j * DEC_W:(j + 1) * DEC_W]
                            pe.matmul(bank(6 + j, SEQ), const("after"), m[:, 0:SEQ], start=True, stop=False)
                            pe.matmul(bank(6 + j, P, P), const("ones"), m[:, SEQ:DEC_W], start=False, stop=True)
                            ins = pe.matmul(bank(6 + j, P, SEQ), const("after"), m[:, SEQ:DEC_W], start=True, stop=True)
                        ins.then_inc(S["suf_done"], 1)
                j = T - ROT_AT
                if 0 <= j < 4:
                    if j == 0:
                        pe.wait_ge(evacuated, U * ph["rv"][0])
                    else:
                        pe.wait_ge(S["rot_done"], 2 * j)
                    for i, x in enumerate((rq, rk)):
                        pe.matmul(bank(4 + i, SEQ), const("rot32"), x[:, j * SEQ:(j + 1) * SEQ], start=True, stop=True).then_inc(S["rot_ps"], 1)
                h = T - RET_AT - 3
                if 0 <= h < HEADS:
                    pe.wait_ge(S["ro_sq"], h + 1)
                    pe.matmul(bank(5, SEQ, parts=slice(0, HEADS)), const("head_sums")[:, HEADS * h:HEADS * (h + 1)],
                              sq[:, (h % 2) * BOTH:(h % 2) * BOTH + SEQ], start=(h == 0), stop=(h == HEADS - 1)).then_inc(S["ro_ss"], 1)
                h = T - RET_AT - 1
                if 0 <= h < HEADS:
                    if h == 0:
                        pe.wait_ge(evacuated, U * ph["gates"][0])
                        pe.wait_ge(S["sb_lo"], 4)
                    pe.wait_ge(S["rw_done"], h + 1)
                    if h >= 2:
                        pe.wait_ge(S["ro_full"], h - 1)
                    w = wk(0)[:, (h % 2) * DEC_W:(h % 2 + 1) * DEC_W]
                    pe.matmul(bank(6 + h % 2, SEQ), rvt[:, h * P:(h + 1) * P], w[:, 0:SEQ], start=True, stop=False)
                    pe.matmul(bank(6 + h % 2, P, P), rvt[:, D + h * P:D + (h + 1) * P], w[:, SEQ:DEC_W], start=False, stop=True).then_inc(S["ro_done"], 1)
                h = T - RET_AT
                if 0 <= h < HEADS:
                    if h == 0:
                        pe.wait_ge(S["rot_done"], 8)
                    else:
                        pe.wait_ge(S["rw_done"], h)
                    pair_scores(4, rk, rq, h % 2, h // 2).then_inc(S["rs_done"], 1)

            def beside_phase(name):
                return lambda c: beside(beside_at(name) + c)

            plain("rq", side=beside_phase("rq"))
            plain("rk", side=beside_phase("rk"))
            rows_pairs("rv", SEQ, side=lambda c, b: beside(beside_at("rv") + 2 * c + 1) if b else None)
            plain("gates", side=beside_phase("gates"))
            plain("rg", side=beside_phase("rg"))
            pe.wait_ge(S["sb_lo"], 4)
            plain("sbout", part=slice(0, SEQ), side=beside_phase("sbout"))

            pe.wait_ge(S["ro_rstd"], 1)

            def ret_spread(h):
                if h >= 4:
                    pe.wait_ge(S["mix_full"], h - 3)
                pe.matmul(bank(4 + h % 4, SEQ), head_rows[:, h * P:(h + 1) * P], rstd[0:HEADS, 0:SEQ], start=True, stop=True).then_inc(S["ro_spread"], 1)

            for h in range(4):
                ret_spread(h)

            def ret_chunk(k):
                if k + 4 < HEADS:
                    ret_spread(k + 4)
                pe.wait_ge(S["ro_lo"], k + 1)

            plain("retout", chunk_ready=ret_chunk)
            plain("wout", part=slice(0, SEQ), squares=(7, SEQ), chunk_ready=lambda k: pe.wait_ge(S["mix_lo"], k + 1))

            pe.wait_ge(S["in_router"], 32)
            for k in range(KD):
                pe.wait_ge(S["xf_ready"], KD + k + 1)
                for h in range(2):
                    ins = pe.matmul(bank(4 + h, 20), xr[:, k * SEQ + h * P:k * SEQ + (h + 1) * P], wr[:, 20 * k:20 * k + 20], start=(k == 0), stop=(k == KD - 1))
                    if k == KD - 1:
                        ins.then_inc(S["rt_ps"], 1)

            def combine_weights():
                for h in range(2):
                    pe.wait_ge(S["rt_comb"], h + 1)
                    pe.transpose(bank(6, P, h * P, parts=slice(0, N_EXPERTS)), tn(h, "comb", 16), const("ident")).then_inc(S["rt_turned"], 1)
                pe.wait_ge(S["rt_copied"], 1)
                pe.wait_ge(S["in_sel"], 16)
                for e in range(N_EXPERTS):
                    if e >= 8 and e % 2 == 0:
                        pe.wait_ge(S["cmb_done"], e // 2 - 3)
                    pe.matmul(bank(4 + e // 2 % 4, SEQ, (e % 2) * SEQ), sel[:, e * P:(e + 1) * P], cmbT[:, :], start=True, stop=True).then_inc(S["cmb_ps"], 1)

            r0 = ph["moe"][0]

            def expert(e, last):
                first = isinstance(e, int) and e == 0
                for i in range(2):
                    for u in range(U):
                        if first and i == 0 and u < 2:
                            if u == 0:
                                first_pair(r0, KD, SEQ, nhi, nlo, X_COLS, normed(7))
                        else:
                            slab(4 * e + (r0 + i), u, KD, SEQ, nhi, nlo, X_COLS)
                    if first and i == 0:
                        combine_weights()
                first_pair(4 * e + (r0 + 2), 4, SEQ, hhi, hlo, X_COLS, lambda k: pe.wait_ge(hlo_ready, 4 * e + (h_at[0] + k + 1)))
                for i in range(2):
                    for u in range(0 if i else 2, U):
                        slab(4 * e + (r0 + 2 + i), u, 4, SEQ, hhi, hlo, X_COLS)
            run(pe, N_EXPERTS, expert, peel_first=True)
            norm_sum(8, SEQ)
            for k in range(KD):
                pe.wait_ge(nt_ready, KD * 8 + k + 1)
                if k >= 4:
                    pe.wait_ge(fin_copied, k - 3)
                f = nt[:, (k % 2) * BOTH:(k % 2) * BOTH + SEQ]
                for h in range(2):
                    ins = pe.transpose(bank(k % 4, P, h * P), f[:, h * P:(h + 1) * P], const("ident"))
                ins.then_inc(fin_turned, 1)


_INS = ["x", "c", "ctx", "c_ctx", "norm_g", "w_mod", "b_mod", "ffn1_w_gu", "ffn1_w_d", "ffn2_w_gu", "ffn2_w_d",
        "attn_w_qkv", "attn_w_o", "attn_q_g", "attn_k_g", "attn_lam_q1", "attn_lam_k1", "attn_lam_q2", "attn_lam_k2",
        "attn_sub_g", "fourier_w", "norm_mix_g_2", "w_in_2", "w_gate_2", "b_gate_2", "w_sb_out_2", "w_ret_out_2",
        "ret_norm_g_2", "w_out_2", "norm_ffn_g_2", "w_group_router_2", "b_group_router_2", "w_expert_router_2",
        "b_expert_router_2", "w_exp_gate_2", "w_exp_up_2", "w_exp_down_2", "norm_final_g_2"]


def kernel(**inputs):
    import numpy as _np
    import concourse.bacc as _bacc
    from concourse import mybir as _mybir
    from concourse.bass_utils import run_bass_kernel_spmd as _run

    nc = _bacc.Bacc("TRN2", target_bir_lowering=False, num_devices=1)
    arrays, tensors = {}, {}
    for name in _INS:
        a = _np.ascontiguousarray(inputs[name])
        arrays[f"in_{name}"] = a
        tensors[name] = nc.dram_tensor(f"in_{name}", a.shape, _mybir.dt.from_np(a.dtype), kind="ExternalInput").ap()
    for name, a in make_constants().items():
        arrays[f"const_{name}"] = a
        tensors[name] = nc.dram_tensor(f"const_{name}", a.shape, _mybir.dt.float32, kind="ExternalInput").ap()
    out = nc.dram_tensor("out_0", (1, SEQ, D), _mybir.dt.float32, kind="ExternalOutput").ap()
    build(nc, tensors, out)
    r = _run(nc, [arrays], core_ids=[0])
    return r.results[0]["out_0"]
```
